# Optimizing a Trainium2 kernel written in Bass

```python
import math
import jax
import jax.numpy as jnp
from jax import lax
import numpy as np

D_MODEL = 1024
BATCH = 1
SEQ = 1024
DEPTH = 1

CHUNK = 64
PLE_DIM = 256
EPS = 1e-6

SSM_WIDTH = D_MODEL // 2
SSM_GROUP = 16
SSM_GROUPS = SSM_WIDTH // SSM_GROUP
SSM_STATE = 64
DT_MIN = 1e-3
DT_MAX = 1e-1

N_HEADS = 8
HEAD_DIM = 64
ATTN_WIDTH = N_HEADS * HEAD_DIM
IDX_HEADS = 8
IDX_DIM = 32
TOPK_MAX = 256
Q_BLOCK = 128
ROPE_THETA = 10000.0

IN_SIZES = (SSM_WIDTH, ATTN_WIDTH, ATTN_WIDTH, ATTN_WIDTH, IDX_HEADS * IDX_DIM, IDX_DIM, IDX_HEADS, D_MODEL, D_MODEL)
IN_COLS = sum(IN_SIZES)

N_EXPERTS = 32
TOP_K = 4
D_FF = D_MODEL
SWIGLU_LIMIT = 7.0
SWIGLU_ALPHA = 1.702

kernel_name = 'hybrid_s5_dsa_moe_ple_block'

def rmsnorm(x, g):
    xf = x.astype(jnp.float32)
    y = xf * lax.rsqrt(jnp.mean(xf * xf, axis=-1, keepdims=True) + EPS)
    return (y * g.astype(jnp.float32)).astype(x.dtype)

def rope(x, pos):
    d = x.shape[-1]
    half = d // 2
    inv = ROPE_THETA ** (-jnp.arange(half, dtype=jnp.float32) * 2.0 / d)
    ang = pos.astype(jnp.float32)[:, None] * inv[None, :]
    cos = jnp.cos(ang)[:, None, :]
    sin = jnp.sin(ang)[:, None, :]
    x1 = x[..., :half].astype(jnp.float32)
    x2 = x[..., half:].astype(jnp.float32)
    out = jnp.concatenate([x1 * cos - x2 * sin, x2 * cos + x1 * sin], axis=-1)
    return out.astype(x.dtype)

def split_in(z):
    pts = np.cumsum(IN_SIZES)[:-1].tolist()
    return jnp.split(z, pts, axis=-1)

def s5_scan(u, lam_re, lam_im, log_dt, b_re, b_im, c_re, c_im, d_skip):
    f32 = jnp.float32
    lam = lax.complex(lam_re.astype(f32), lam_im.astype(f32))
    dt = jnp.exp(log_dt.astype(f32))[:, None]
    lam_bar = jnp.exp(lam * dt)
    b = lax.complex(b_re.astype(f32), b_im.astype(f32))
    b_bar = ((lam_bar - 1.0) / lam)[..., None] * b
    c = lax.complex(c_re.astype(f32), c_im.astype(f32))

    def combine(e1, e2):
        a1, s1 = e1
        a2, s2 = e2
        return a1 * a2, a2 * s1 + s2

    def per_seq(u_seq):
        bu = jnp.einsum('gph,lgh->lgp', b_bar, u_seq.astype(f32))
        a = jnp.broadcast_to(lam_bar, bu.shape)
        _, states = lax.associative_scan(combine, (a, bu), axis=0)
        return jnp.einsum('ghp,lgp->lgh', c, states).real

    y = lax.map(per_seq, u)
    y = y + d_skip.astype(f32) * u.astype(f32)
    return y.astype(u.dtype)

def dsa_attention(q, k, v, q_idx, k_idx, w_idx):
    f32 = jnp.float32
    bsz, seq = q.shape[0], q.shape[1]
    topk = min(TOPK_MAX, seq // 4)
    key_chunk = jnp.arange(seq) // CHUNK
    scale = HEAD_DIM ** -0.5
    idx_scale = (IDX_HEADS * IDX_DIM) ** -0.5
    kf = k_idx.astype(f32)
    gather = jax.vmap(lambda t, i: t[i])

    def block(start):
        q_chunk = (start + jnp.arange(Q_BLOCK)) // CHUNK
        qb = lax.dynamic_slice_in_dim(q, start, Q_BLOCK, axis=1)
        qib = lax.dynamic_slice_in_dim(q_idx, start, Q_BLOCK, axis=1).astype(f32)
        wb = lax.dynamic_slice_in_dim(w_idx, start, Q_BLOCK, axis=1).astype(f32) * idx_scale
        dots = jnp.einsum('bthd,bsd->bths', qib, kf)
        score = jnp.einsum('bth,bths->bts', wb, jax.nn.relu(dots))
        allowed = key_chunk[None, :] <= q_chunk[:, None]
        score = jnp.where(allowed[None], score, -jnp.inf)
        _, sel = lax.top_k(score, topk)
        valid = key_chunk[sel] <= q_chunk[None, :, None]
        kg = gather(k, sel)
        vg = gather(v, sel)
        logits = jnp.einsum('bthd,btjhd->bthj', qb, kg).astype(f32) * scale
        logits = jnp.where(valid[:, :, None, :], logits, -jnp.inf)
        probs = jax.nn.softmax(logits, axis=-1).astype(v.dtype)
        return jnp.einsum('bthj,btjhd->bthd', probs, vg)

    starts = jnp.arange(seq // Q_BLOCK) * Q_BLOCK
    out = lax.map(block, starts)
    return jnp.moveaxis(out, 0, 1).reshape(bsz, seq, N_HEADS * HEAD_DIM)

def moe(h, w_router, b_router, w_gate, b_gate, w_up, b_up, w_down, b_down):
    bsz, seq, d = h.shape
    t = h.reshape(-1, d)
    logits = (t @ w_router + b_router).astype(jnp.float32)
    top_val, top_idx = lax.top_k(logits, TOP_K)
    weights = jax.nn.softmax(top_val, axis=-1)
    flat_e = top_idx.reshape(-1)
    order = jnp.argsort(flat_e)
    e_sorted = flat_e[order]
    xs = t[order // TOP_K]
    sizes = jnp.bincount(flat_e, length=N_EXPERTS).astype(jnp.int32)
    g = lax.ragged_dot(xs, w_gate, sizes) + b_gate[e_sorted]
    u = lax.ragged_dot(xs, w_up, sizes) + b_up[e_sorted]
    g = jnp.minimum(g, SWIGLU_LIMIT)
    u = jnp.clip(u, -SWIGLU_LIMIT, SWIGLU_LIMIT)
    a = (u + 1.0) * (g * jax.nn.sigmoid(SWIGLU_ALPHA * g))
    ys = lax.ragged_dot(a, w_down, sizes) + b_down[e_sorted]
    inv = jnp.argsort(order)
    y = ys[inv].reshape(-1, TOP_K, d)
    out = jnp.einsum('tk,tkd->td', weights.astype(y.dtype), y)
    return out.reshape(bsz, seq, d)

def setup_inputs(seed: int = 0) -> dict:
    key = jax.random.key(seed)
    ks = iter(jax.random.split(key, 40))
    f32 = jnp.float32

    def nrm(shape, scale):
        return jax.random.normal(next(ks), shape, f32) * scale

    def gain(shape):
        return 1.0 + nrm(shape, 0.05)

    nl, G, P, H, D, E = DEPTH, SSM_GROUPS, SSM_STATE, SSM_GROUP, D_MODEL, N_EXPERTS
    x = nrm((BATCH, SEQ, D), 1.0)
    p = nrm((DEPTH, BATCH, SEQ, PLE_DIM), 1.0)
    w_in = nrm((nl, D, IN_COLS), D ** -0.5)
    b_gates = nrm((nl, 2 * D), 0.01)
    n_idx = jnp.arange(P, dtype=f32)
    lam_re = -0.5 + nrm((nl, G, P), 0.01)
    lam_im = jnp.pi * n_idx + nrm((nl, G, P), 0.01)
    log_dt = jax.random.uniform(next(ks), (nl, G), f32, math.log(DT_MIN), math.log(DT_MAX))
    b_re = nrm((nl, G, P, H), (2 * H) ** -0.5)
    b_im = nrm((nl, G, P, H), (2 * H) ** -0.5)
    c_re = nrm((nl, G, H, P), (2 * P) ** -0.5)
    c_im = nrm((nl, G, H, P), (2 * P) ** -0.5)
    d_skip = nrm((nl, G, H), 1.0)
    w_glu = nrm((nl, SSM_WIDTH, SSM_WIDTH), SSM_WIDTH ** -0.5)
    b_glu = nrm((nl, SSM_WIDTH), 0.01)
    w_ssm_br = nrm((nl, SSM_WIDTH, D), SSM_WIDTH ** -0.5)
    w_attn_br = nrm((nl, ATTN_WIDTH, D), ATTN_WIDTH ** -0.5)
    w_o = nrm((nl, D, D), D ** -0.5)
    norm_mix = gain((nl, D))
    norm_ffn = gain((nl, D))
    w_router = nrm((nl, D, E), D ** -0.5)
    b_router = nrm((nl, E), 0.01)
    w_gate = nrm((nl, E, D, D_FF), D ** -0.5)
    b_gate = nrm((nl, E, D_FF), 0.01)
    w_up = nrm((nl, E, D, D_FF), D ** -0.5)
    b_up = nrm((nl, E, D_FF), 0.01)
    w_down = nrm((nl, E, D_FF, D), D_FF ** -0.5)
    b_down = nrm((nl, E, D), 0.01)
    w_ple_gate = nrm((nl, D, D), D ** -0.5)
    w_ple_proj = nrm((nl, PLE_DIM, D), PLE_DIM ** -0.5)
    norm_final = gain((D,))
    return {'x': x, 'p': p, 'w_in': w_in, 'b_gates': b_gates, 'lam_re': lam_re, 'lam_im': lam_im,
            'log_dt': log_dt, 'b_re': b_re, 'b_im': b_im, 'c_re': c_re, 'c_im': c_im, 'd_skip': d_skip,
            'w_glu': w_glu, 'b_glu': b_glu, 'w_ssm_br': w_ssm_br, 'w_attn_br': w_attn_br, 'w_o': w_o,
            'norm_mix': norm_mix, 'norm_ffn': norm_ffn, 'w_router': w_router, 'b_router': b_router,
            'w_gate': w_gate, 'b_gate': b_gate, 'w_up': w_up, 'b_up': b_up, 'w_down': w_down,
            'b_down': b_down, 'w_ple_gate': w_ple_gate, 'w_ple_proj': w_ple_proj, 'norm_final': norm_final}

def reference(x, p, w_in, b_gates, lam_re, lam_im, log_dt, b_re, b_im, c_re, c_im, d_skip,
              w_glu, b_glu, w_ssm_br, w_attn_br, w_o, norm_mix, norm_ffn, w_router, b_router,
              w_gate, b_gate, w_up, b_up, w_down, b_down, w_ple_gate, w_ple_proj, norm_final):
    bsz, seq, _ = x.shape
    pos = jnp.arange(seq)
    r = x
    for i in range(DEPTH):
        h = rmsnorm(r, norm_mix[i])
        z = h @ w_in[i]
        u_ssm, q, k, v, q_idx, k_idx, w_idx, z_gs, z_ga = split_in(z)

        u_ssm = u_ssm.reshape(bsz, seq, SSM_GROUPS, SSM_GROUP)
        y_ssm = s5_scan(u_ssm, lam_re[i], lam_im[i], log_dt[i], b_re[i], b_im[i],
                        c_re[i], c_im[i], d_skip[i]).reshape(bsz, seq, SSM_WIDTH)
        y_ssm = jax.nn.gelu(y_ssm)
        y_ssm = y_ssm * jax.nn.sigmoid(y_ssm @ w_glu[i] + b_glu[i])
        br_ssm = y_ssm @ w_ssm_br[i]

        q = rope(q.reshape(bsz, seq, N_HEADS, HEAD_DIM), pos)
        k = rope(k.reshape(bsz, seq, N_HEADS, HEAD_DIM), pos)
        v = v.reshape(bsz, seq, N_HEADS, HEAD_DIM)
        q_idx = rope(q_idx.reshape(bsz, seq, IDX_HEADS, IDX_DIM), pos)
        k_idx = rope(k_idx[:, :, None, :], pos)[:, :, 0, :]
        y_attn = dsa_attention(q, k, v, q_idx, k_idx, w_idx)
        br_attn = y_attn @ w_attn_br[i]

        g_ssm = jax.nn.sigmoid(z_gs + b_gates[i, :D_MODEL])
        g_attn = jax.nn.sigmoid(z_ga + b_gates[i, D_MODEL:])
        r = r + (g_ssm * br_ssm + g_attn * br_attn) @ w_o[i]

        h2 = rmsnorm(r, norm_ffn[i])
        r = r + moe(h2, w_router[i], b_router[i], w_gate[i], b_gate[i], w_up[i], b_up[i],
                    w_down[i], b_down[i])

        r = r + jax.nn.sigmoid(r @ w_ple_gate[i]) * (p[i] @ w_ple_proj[i])
    return rmsnorm(r, norm_final)


_drawn_inputs = setup_inputs


def setup_inputs(seed=0):
    import zlib

    import numpy as np

    out = dict(_drawn_inputs(seed))
    spreads = {}
    factors = {'b_gates': 6.444,
     'lam_re': 200.0,
     'b_glu': 16.857,
     'b_gate': 8.0,
     'b_up': 8.0,
     'b_down': 8.0,
     'lam_im': 22.232,
     'log_dt': 26.392,
     'b_re': 21.949,
     'b_im': 26.712,
     'c_re': 24.987,
     'c_im': 27.548}
    for name, (base, spread) in spreads.items():
        noise = np.random.default_rng([zlib.crc32(name.encode()), seed]).standard_normal(out[name].shape)
        drawn = base * np.exp(spread * noise) if base else spread * noise
        out[name] = jnp.asarray(drawn.astype(out[name].dtype))
    for name, factor in factors.items():
        out[name] = (out[name] * factor).astype(out[name].dtype)
    return out
```

```python
import math
from contextlib import ExitStack

import numpy as np

import concourse.bass as bass
from concourse import mybir

F32 = mybir.dt.float32
BF16 = mybir.dt.bfloat16
U32 = mybir.dt.uint32
I32 = mybir.dt.int32
ALU = mybir.AluOpType
ACT = mybir.ActivationFunctionType
AX = mybir.AxisListType

P = 128
D = 1024
SEQ = 1024
EPS = 1e-6
KC = D // P
TT = SEQ // P
HALF = 512
GROUPS, GCH, STATE = 32, 16, 64
SSM = GROUPS * GCH
PAIRS = GROUPS // 2
STEP = P // GCH
CHUNKS = SEQ // STEP
HEADS, HD = 8, 64
AW = HEADS * HD
IH, ID = 8, 32
TOPK = 256
PLE = 256
EXPERTS, TOP = 32, 4
FF = 1024
SWIGLU_LIMIT = 7.0
C_U, C_Q, C_K, C_V = 0, SSM, SSM + AW, SSM + 2 * AW
C_QI = SSM + 3 * AW
C_KI = C_QI + IH * ID
C_WI = C_KI + ID
C_GS = C_WI + IH
C_GA = C_GS + D
NI = IH * ID + ID + IH
NEG = -1e30
MAGIC = 12582912.0


def own_sem(nc, sems, name):
    sems.append(nc.alloc_semaphore(name))
    return sems[-1]


def clear_sems(nc, sems):
    nc.clear_and_free_semaphores(sems)
    nc.all_engine_barrier()


class Order:

    def __init__(self, eng, sem):
        self.eng, self.sem, self.n, self.said = eng, sem, 0, {}

    def go(self, ins):
        self.n += 1
        return ins.then_inc(self.sem, 1)

    def wait(self):
        self.eng.wait_ge(self.sem, self.n)

    def then(self, ins):
        self.go(ins)
        self.wait()

    def tell(self, ins, sem):
        self.said[sem.name] = self.said.get(sem.name, 0) + 1
        ins.then_inc(sem, 1)
        self.eng.wait_ge(sem, self.said[sem.name])


def norm_and_ssm(nc, I, S, hT, y2T, psb, const):
    ctx, sems = ExitStack(), []
    with ctx:
        sb = lambda n, s, d=F32: ctx.enter_context(nc.sbuf_tensor("a_" + n, s, d))
        sem = lambda n: own_sem(nc, sems, "a_" + n)
        x_all = sb("x_all", [P, TT, D])
        flat = x_all[:, :, :].rearrange("p a b -> p (a b)")
        n_st = PAIRS * CHUNKS
        view = lambda at: flat[:, at * n_st:(at + 1) * n_st].rearrange("p (j c) -> p j c", j=PAIRS)
        st_re, st_im, turned_re, turned_im = (view(i) for i in range(4))
        w_u = sb("w_u", [P, KC, SSM])
        u_grp = sb("u_grp", [P, GROUPS, CHUNKS])
        toep = sb("toep", [P, GROUPS, P])
        m_both = y2T[:, :, :].rearrange("p b t -> p (b t)").rearrange("p (i j n) -> p i j n", i=2, j=PAIRS)
        m_in = [m_both[:, 0], m_both[:, 1]]
        m_out = [sb("m_out_re", [P, PAIRS, STEP + 1, GCH]), sb("m_out_im", [P, PAIRS, STEP + 1, GCH])]
        scratch = sb("scratch", [P, PAIRS * CHUNKS * 4])
        w1 = [scratch[:, i * n_st:(i + 1) * n_st].rearrange("p (j s h) -> p j s h", j=PAIRS, s=STEP) for i in range(2)]
        ph_re, ph_im = (scratch[:, (2 + i) * n_st:(3 + i) * n_st].rearrange("p (j c) -> p j c", j=PAIRS) for i in range(2))
        u_ch = scratch[:, 2 * n_st:4 * n_st].rearrange("p (b s c) -> p b s c", b=4, s=STEP)
        tmp = sb("tmp", [P, PAIRS * (STEP + 1) * GCH])
        small = sb("small", [P, 40, PAIRS])
        powers = sb("powers", [P, 4, PAIRS, STEP + 1])
        lam = sb("lam", [P, 3, PAIRS])
        b_sb = sb("b_sb", [P, 4, PAIRS, GCH])
        c_nat = sb("c_nat", [P, 2, 4, 2, STATE])
        c_sb = sb("c_sb", [P, 2, PAIRS, GCH])
        d_sb = sb("d_sb", [GCH, GROUPS])
        k_sb = scratch[0:GCH, 0:GROUPS * P].rearrange("p (g n) -> p g n", g=GROUPS)
        gain = sb("gain", [P, KC])
        b_glu = sb("b_glu", [P, 4])
        ssq = sb("ssq", [P, 6, TT])
        ssq_done, rstd_done, h_done = sem("ssq"), sem("rstd"), sem("h")
        x_in, w_in_, par_in = [sem(f"x_in{i}") for i in range(TT)], sem("w_in"), sem("par_in")
        dve_step, act_step = sem("dve_step"), sem("act_step")
        tr_ready, tr_used = sem("tr_ready"), sem("tr_used")
        c_tr, c_used = sem("c_tr"), sem("c_used")
        u_ready, u_used, u_out, u_back = sem("u_ready"), sem("u_used"), sem("u_out"), sem("u_back")
        w1_ready, m_tr, m_used = sem("w1_ready"), sem("m_tr"), sem("m_used")
        mo_ready, k_ready, k_used, k_diag, k_out, t_back = (sem(n) for n in ("mo_ready", "k_ready", "k_used", "k_diag", "k_out", "t_back"))
        toep_zero = sem("toep_zero")
        s_ready, s_used, s_turned = sem("s_ready"), sem("s_used"), sem("s_turned")
        y_ready, y_used, y_out, y_back = sem("y_ready"), sem("y_used"), sem("y_out"), sem("y_back")
        sq_done, inner_done, sig_done, gel_done = sem("sq_done"), sem("inner_done"), sem("sig_done"), sem("gel_done")
        glu_w, z_ready, z_sig, y2_done = sem("glu_w"), sem("z_ready"), sem("z_sig"), sem("y2_done")
        y_grp = toep
        block = ctx.enter_context(nc.Block())
        ident = const["ident"]

        lamv = lambda a: a[0].rearrange("(j g) p -> (g p) j", g=2)
        N_PAR = 14

        def bank_groups(t, q):
            return t[:, :, :].rearrange("p (j g) n -> p g j n", g=2)[:, q % 2, 4 * (q // 2):4 * (q // 2) + 4, :]

        @block.sync
        def _(sp):
            for i in range(TT):
                sp.dma_start(x_all[:, i, :], I["x"][0, i * P:(i + 1) * P, :]).then_inc(x_in[i], 16)
            sp.dma_start(w_u[:, :, :], I["w_in"][0][:, C_U:C_U + SSM].rearrange("(k p) n -> p k n", p=P)).then_inc(w_in_, 16)
            sp.wait_ge(u_used, 8)
            for b in range(4):
                sp.dma_start(S["u"][b * P:(b + 1) * P, :, :], u_ch[:, b]).then_inc(u_out, 16)
            sp.wait_ge(u_out, 64)
            for s in range(STEP):
                sp.dma_start(u_grp[s * GCH:(s + 1) * GCH, :, :],
                             S["u"][:, s, :].rearrange("(g h) c -> h g c", h=GCH)).then_inc(u_back, 16)
            sp.wait_ge(k_diag, 1)
            sp.dma_start(S["k"].rearrange("g h n -> h g n"), k_sb[:, :, :]).then_inc(k_out, 16)
            sp.wait_ge(k_out, 16)
            sp.wait_ge(toep_zero, 1)
            for s in range(STEP):
                sp.dma_start(toep[s * GCH:(s + 1) * GCH, :, s * GCH:],
                             S["k"].rearrange("g h n -> h g n")[:, :, 0:P - s * GCH]).then_inc(t_back, 16)
            sp.wait_ge(u_ready, 8)
            sp.dma_start(w_u[:, 0:4, :], I["w_glu"][0].rearrange("(k p) n -> p k n", p=P)).then_inc(glu_w, 16)
            sp.wait_ge(y_used, 8)
            for s in range(STEP):
                sp.dma_start(S["y"][:, s, :].rearrange("(g h) c -> h g c", h=GCH),
                             y_grp[s * GCH:(s + 1) * GCH, :, :]).then_inc(y_out, 16)
            sp.wait_ge(y_out, 16 * STEP)
            for b in range(4):
                sp.dma_start(u_ch[:, b], S["y"][b * P:(b + 1) * P, :, :]).then_inc(y_back, 16)

        @block.gpsimd
        def _(pool):
            nc.gpsimd.memset(toep[:, :, :], 0.0).then_inc(toep_zero, 1)

        @block.scalar
        def _(act):
            o = Order(act, act_step)
            with nc.allow_non_contiguous_dma(reason="parameters laid out by state, a few KB"):
                act.dma_start(lam[:, 0, :], lamv(I["lam_re"])).then_inc(par_in, 16)
                act.dma_start(lam[:, 1, :], lamv(I["lam_im"])).then_inc(par_in, 16)
                for g in range(2):
                    act.dma_start(lam[g * STATE:(g + 1) * STATE, 2, :],
                                  I["log_dt"][0].rearrange("(j g) -> g j", g=2)[g].unsqueeze(0).broadcast_to([STATE, PAIRS])).then_inc(par_in, 16)
                act.dma_start(b_sb[:, 0], I["b_re"][0].rearrange("(j g) p h -> (g p) j h", g=2)).then_inc(par_in, 16)
                act.dma_start(b_sb[:, 1], I["b_im"][0].rearrange("(j g) p h -> (g p) j h", g=2)).then_inc(par_in, 16)
                for n, name in enumerate(("c_re", "c_im")):
                    for twice in range(2):
                        act.dma_start(c_nat[:, n, :, twice, :], I[name][0].rearrange("(b g) h p -> (g h) b p", b=4)).then_inc(par_in, 16)
                act.dma_start(d_sb[:, :], I["d_skip"][0].rearrange("g h -> h g")).then_inc(par_in, 16)
                act.dma_start(gain[:, :], I["norm_mix"][0].rearrange("(k p) -> p k", p=P)).then_inc(par_in, 16)
                act.dma_start(b_glu[:, :], I["b_glu"][0].rearrange("(k p) -> p k", p=P)).then_inc(par_in, 16)
                act.dma_start(ident, I["t_ident"]).then_inc(par_in, 16)
            for i in range(TT):
                act.wait_ge(x_in[i], 16)
                nc.scalar.activation(tmp[:, 0:D], x_all[:, i, :], ACT.Square, accum_out=ssq[:, 0, i:i + 1]).then_inc(ssq_done, 1)
                act.wait_ge(ssq_done, i + 1)
            act.wait_ge(rstd_done, 1)
            o.then(nc.scalar.activation(ssq[:, 2, :], ssq[:, 1, :], ACT.Sqrt))
            nc.scalar.activation(ssq[:, 5, :], ssq[:, 2, :], ACT.Copy).then_inc(ssq_done, 1)
            act.wait_ge(rstd_done, 2)
            for i in range(TT):
                nc.scalar.activation(x_all[:, i, :], x_all[:, i, :], ACT.Copy, scale=ssq[:, 3, i:i + 1]).then_inc(h_done, 1)
            for b in range(4):
                for t in range(2):
                    n = 2 * b + t
                    act.wait_ge(u_ready, n + 1)
                    nc.scalar.copy(u_ch[:, b].rearrange("p s c -> p c s")[:, t * 64:(t + 1) * 64, :],
                                   psb[n % 8][:, :].rearrange("p (c s) -> p c s", s=STEP)).then_inc(u_used, 1)
            for q in range(8):
                act.wait_ge(k_ready, q + 1)
                nc.scalar.copy(bank_groups(k_sb, q), psb[q][0:GCH, :].rearrange("p (g n) -> p g n", g=4)).then_inc(k_used, 1)
            for q in range(8):
                act.wait_ge(y_ready, q + 1)
                nc.scalar.copy(bank_groups(y_grp, q), psb[q][:, :].rearrange("p (g n) -> p g n", g=4)).then_inc(y_used, 1)
            for b in range(4):
                act.wait_ge(y_back, 64)
                nc.scalar.activation(flat[:, b * SEQ:(b + 1) * SEQ], u_ch[:, b].rearrange("p s c -> p (s c)"), ACT.Square).then_inc(sq_done, 1)
            for b in range(4):
                act.wait_ge(inner_done, b + 1)
                nc.scalar.activation(flat[:, b * SEQ:(b + 1) * SEQ], flat[:, b * SEQ:(b + 1) * SEQ], ACT.Sigmoid,
                                     scale=2.0 * math.sqrt(2.0 / math.pi)).then_inc(sig_done, 1)
            for n in range(8):
                act.wait_ge(z_ready, n + 1)
                b, t = n // 2, n % 2
                nc.scalar.activation(flat[:, 4 * SEQ + n * HALF:4 * SEQ + (n + 1) * HALF], psb[n][:, :], ACT.Sigmoid,
                                     bias=b_glu[:, b:b + 1]).then_inc(z_sig, 1)

        @block.vector
        def _(dve):
            v = nc.vector
            o = Order(dve, dve_step)
            sm = lambda i: small[:, i, :]
            mul = lambda out, a, b: o.then(v.tensor_tensor(out, a, b, ALU.mult))
            add = lambda out, a, b: o.then(v.tensor_tensor(out, a, b, ALU.add))
            sub = lambda out, a, b: o.then(v.tensor_tensor(out, a, b, ALU.subtract))

            def wide(a, like):
                for _ in range(len(like.shape) - len(a.shape)):
                    a = a.unsqueeze(len(a.shape))
                return a.broadcast_to(list(like.shape))

            def cmul(out, a, b, t1, t2):
                o.go(v.tensor_tensor(t1, a[0], b[0], ALU.mult))
                o.go(v.tensor_tensor(t2, a[1], b[1], ALU.mult))
                o.then(v.tensor_tensor(out[1], a[0], b[1], ALU.mult))
                o.then(v.tensor_tensor(out[0], t1, t2, ALU.subtract))
                o.then(v.tensor_tensor(t1, a[1], b[0], ALU.mult))
                o.then(v.tensor_tensor(out[1], out[1], t1, ALU.add))

            def round_to_int(out, a):
                o.then(v.tensor_scalar(out, a, MAGIC, None, ALU.add))
                o.then(v.tensor_scalar(out, out, -MAGIC, None, ALU.add))

            def horner(out, z, cs):
                o.then(v.tensor_scalar(out, z, cs[0], None, ALU.mult))
                for c in cs[1:]:
                    o.then(v.scalar_tensor_tensor(out, out, c, z, ALU.add, ALU.mult))

            def exp(out, a, t1, t2, t3):
                o.then(v.tensor_scalar(t1, a, -87.0, 88.0, ALU.max, ALU.min))
                o.then(v.tensor_scalar(t2, t1, 1.0 / math.log(2.0), None, ALU.mult))
                round_to_int(t2, t2)
                o.then(v.scalar_tensor_tensor(t1, t2, -0.693359375, t1, ALU.mult, ALU.add))
                o.then(v.scalar_tensor_tensor(t1, t2, 2.12194440e-4, t1, ALU.mult, ALU.add))
                horner(out, t1, [1.0 / math.factorial(n) for n in range(8, 0, -1)])
                o.then(v.tensor_scalar(out, out, 1.0, None, ALU.add))
                o.then(v.tensor_scalar(t3.bitcast(I32), t2, 127.0, 8388608.0, ALU.add, ALU.mult))
                mul(out, out, t3)

            dve.wait_ge(ssq_done, TT)
            o.then(v.tensor_scalar(ssq[:, 0, :], ssq[:, 0, :], 1.0 / D, EPS, ALU.mult, ALU.add))
            o.tell(v.reciprocal(ssq[:, 1, :], ssq[:, 0, :]), rstd_done)
            dve.wait_ge(ssq_done, TT + 1)
            mul(ssq[:, 4, :], ssq[:, 5, :], ssq[:, 5, :])
            mul(ssq[:, 4, :], ssq[:, 4, :], ssq[:, 0, :])
            o.then(v.tensor_scalar(ssq[:, 4, :], ssq[:, 4, :], -0.5, 1.5, ALU.mult, ALU.add))
            o.tell(v.tensor_tensor(ssq[:, 3, :], ssq[:, 5, :], ssq[:, 4, :], ALU.mult), rstd_done)

            dve.wait_ge(par_in, 16 * N_PAR)
            for n in range(2 * KC):
                k, t = n // 2, n % 2
                dve.wait_ge(tr_ready, n + 1)
                v.tensor_scalar(hT[:, k, t * HALF:(t + 1) * HALF], psb[n % 8][:, :], gain[:, k:k + 1], None, ALU.mult).then_inc(tr_used, 1)

            DT, ER, EI, E, T1, T2, T3, SN, CS, AR, AI, FR, FI, DEN, E8, PR, PI = range(17)
            exp(sm(DT), lam[:, 2, :], sm(T1), sm(T2), sm(T3))
            mul(sm(ER), lam[:, 0, :], sm(DT))
            mul(sm(EI), lam[:, 1, :], sm(DT))
            exp(sm(E), sm(ER), sm(T1), sm(T2), sm(T3))
            o.then(v.tensor_scalar(sm(T2), sm(EI), 1.0 / (2.0 * math.pi), None, ALU.mult))
            round_to_int(sm(T2), sm(T2))
            for part in (-6.28125, -1.9350051879882812e-3, -3.0199159819e-7):
                o.then(v.scalar_tensor_tensor(sm(EI), sm(T2), part, sm(EI), ALU.mult, ALU.add))
            o.then(v.tensor_scalar(sm(EI), sm(EI), 0.5, None, ALU.mult))
            mul(sm(T1), sm(EI), sm(EI))
            horner(sm(T2), sm(T1), [(-1.0) ** n / math.factorial(2 * n + 1) for n in range(7, 0, -1)])
            o.then(v.scalar_tensor_tensor(sm(T2), sm(T2), 1.0, sm(EI), ALU.add, ALU.mult))
            horner(sm(T3), sm(T1), [(-1.0) ** n / math.factorial(2 * n) for n in range(8, 0, -1)])
            o.then(v.tensor_scalar(sm(T3), sm(T3), 1.0, None, ALU.add))
            mul(sm(SN), sm(T2), sm(T3))
            o.then(v.tensor_scalar(sm(SN), sm(SN), 2.0, None, ALU.mult))
            mul(sm(CS), sm(T2), sm(T2))
            o.then(v.tensor_scalar(sm(CS), sm(CS), -2.0, 1.0, ALU.mult, ALU.add))
            mul(sm(AR), sm(E), sm(CS))
            mul(sm(AI), sm(E), sm(SN))
            mul(sm(DEN), lam[:, 0, :], lam[:, 0, :])
            mul(sm(T1), lam[:, 1, :], lam[:, 1, :])
            add(sm(DEN), sm(DEN), sm(T1))
            o.then(v.reciprocal(sm(DEN), sm(DEN)))
            o.then(v.tensor_scalar(sm(T1), sm(AR), -1.0, None, ALU.add))
            mul(sm(FR), sm(T1), lam[:, 0, :])
            mul(sm(T2), sm(AI), lam[:, 1, :])
            add(sm(FR), sm(FR), sm(T2))
            mul(sm(FR), sm(FR), sm(DEN))
            mul(sm(FI), sm(AI), lam[:, 0, :])
            mul(sm(T2), sm(T1), lam[:, 1, :])
            sub(sm(FI), sm(FI), sm(T2))
            mul(sm(FI), sm(FI), sm(DEN))
            b_bar = (b_sb[:, 2], b_sb[:, 3])
            half = PAIRS * CHUNKS // 8
            tv = lambda n, at=0: tmp[:, at * half:at * half + n]
            tb = [tv(PAIRS * GCH, i).rearrange("p (j h) -> p j h", j=PAIRS) for i in range(2)]
            cmul(b_bar, (wide(sm(FR), b_bar[0]), wide(sm(FI), b_bar[0])), (b_sb[:, 0], b_sb[:, 1]), *tb)
            pw = [powers[:, 0], powers[:, 1]]
            rev = [powers[:, 2], powers[:, 3]]
            o.go(v.memset(pw[0][:, :, 0], 1.0))
            o.then(v.memset(pw[1][:, :, 0], 0.0))
            for n in range(STEP):
                cmul((pw[0][:, :, n + 1], pw[1][:, :, n + 1]), (pw[0][:, :, n], pw[1][:, :, n]), (sm(AR), sm(AI)), sm(T1), sm(T2))
            for n in range(STEP):
                for i in range(2):
                    o.go(v.tensor_copy(rev[i][:, :, n], pw[i][:, :, STEP - 1 - n]))
            o.wait()
            shape = [P, PAIRS, STEP, GCH]
            rw = [r[:, :, 0:STEP].unsqueeze(3).broadcast_to(shape) for r in rev]
            bw = [b.unsqueeze(2).broadcast_to(shape) for b in b_bar]
            t4 = tmp[:, 0:n_st].rearrange("p (j s h) -> p j s h", j=PAIRS, s=STEP)
            mul(w1[0], rw[0], bw[0])
            mul(t4, rw[1], bw[1])
            sub(w1[0], w1[0], t4)
            mul(w1[1], rw[0], bw[1])
            mul(t4, rw[1], bw[0])
            o.tell(v.tensor_tensor(w1[1], w1[1], t4, ALU.add), w1_ready)
            for n in range(8):
                dve.wait_ge(c_tr, 1)
                i, b = n // 4, n % 4
                src = psb[i][:, b * P:(b + 1) * P].rearrange("p (j g h) -> p g j h", g=2, h=GCH)
                for g in range(2):
                    o.go(v.tensor_copy(c_sb[g * STATE:(g + 1) * STATE, i, 4 * b:4 * b + 4, :], src[g * STATE:(g + 1) * STATE, g]))
            o.wait()
            shape = [P, PAIRS, STEP + 1, GCH]
            pb = [x.unsqueeze(3).broadcast_to(shape) for x in pw]
            cb = [c_sb[:, i].unsqueeze(2).broadcast_to(shape) for i in range(2)]
            t4 = tmp[:, :].rearrange("p (j s h) -> p j s h", j=PAIRS, s=STEP + 1)
            mul(m_out[0][:, :, :, :], pb[0], cb[0])
            mul(t4, pb[1], cb[1])
            sub(m_out[0][:, :, :, :], m_out[0][:, :, :, :], t4)
            mul(m_out[1][:, :, :, :], pb[0], cb[1])
            mul(t4, pb[1], cb[0])
            o.then(v.tensor_tensor(m_out[1][:, :, :, :], m_out[1][:, :, :, :], t4, ALU.add))
            o.tell(v.tensor_scalar(m_out[1][:, :, :, :].rearrange("p a b c -> p (a b c)"),
                                   m_out[1][:, :, :, :].rearrange("p a b c -> p (a b c)"), -1.0, None, ALU.mult), mo_ready)
            for n in range(8):
                dve.wait_ge(m_tr, n + 1)
                v.tensor_copy(m_in[n // 4][:, 4 * (n % 4):4 * (n % 4) + 4, :], psb[n][:, :].rearrange("p (j n) -> p j n", j=4)).then_inc(m_used, 1)
            dve.wait_ge(k_used, 8)
            shape = [GCH, GROUPS, GCH]
            t3 = tmp[0:GCH, 0:GROUPS * GCH].rearrange("p (g h) -> p g h", g=GROUPS)
            mul(t3, d_sb[:, :].unsqueeze(2).broadcast_to(shape), ident[0:GCH, 0:GCH].unsqueeze(1).broadcast_to(shape))
            o.tell(v.tensor_tensor(k_sb[:, :, 0:GCH], k_sb[:, :, 0:GCH], t3, ALU.add), k_diag)
            cur = [(sm(CS), sm(SN)), (sm(17), sm(18)), (sm(19), sm(20)), (sm(PR), sm(PI))]
            for n in range(3):
                cmul(cur[n + 1], cur[n], cur[n], sm(T1), sm(T2))
            mul(sm(E8), sm(E), sm(E))
            mul(sm(T1), sm(E8), sm(E8))
            mul(sm(E8), sm(T1), sm(T1))
            dve.wait_ge(u_back, 16 * STEP)
            o.go(v.memset(ph_re[:, :, 0], 1.0))
            o.then(v.memset(ph_im[:, :, 0], 0.0))
            a, b = (sm(PR), sm(PI)), (sm(21), sm(22))
            n = 1
            while n < CHUNKS:
                new = (ph_re[:, :, n:2 * n], ph_im[:, :, n:2 * n])
                old = (ph_re[:, :, 0:n], ph_im[:, :, 0:n])
                sc = [tmp[:, i * 1024:i * 1024 + PAIRS * n].rearrange("p (j c) -> p j c", j=PAIRS) for i in range(2)]
                cmul(new, (wide(a[0], new[0]), wide(a[1], new[0])), old, *sc)
                cmul(b, a, a, sm(T1), sm(T2))
                a, b = b, a
                n *= 2
            for q in range(4):
                dve.wait_ge(s_ready, 2 * q + 2)
                js = slice(4 * q, 4 * q + 4)
                s_in = [psb[2 * q + i][:, :].rearrange("p (j c) -> p j c", j=4) for i in range(2)]
                tq = tmp[:, 0:HALF].rearrange("p (j c) -> p j c", j=4)
                mul(turned_re[:, js], s_in[0], ph_re[:, js])
                mul(tq, s_in[1], ph_im[:, js])
                add(turned_re[:, js], turned_re[:, js], tq)
                mul(turned_im[:, js], s_in[1], ph_re[:, js])
                mul(tq, s_in[0], ph_im[:, js])
                sub(turned_im[:, js], turned_im[:, js], tq)
            for j in range(PAIRS):
                for t in (turned_re, turned_im):
                    o.go(v.tensor_tensor_scan(t[:, j, :], small[:, E8, j:j + 1].broadcast_to([P, CHUNKS]), t[:, j, :], 0.0, ALU.mult, ALU.add))
            o.wait()
            last = CHUNKS - 1
            t3 = tmp[:, 0:PAIRS * last].rearrange("p (j c) -> p j c", j=PAIRS)
            cut = lambda t: t[:, :, 0:last]
            o.go(v.memset(st_re[:, :, 0], 0.0))
            o.go(v.memset(st_im[:, :, 0], 0.0))
            mul(st_re[:, :, 1:], cut(turned_re), cut(ph_re))
            mul(t3, cut(turned_im), cut(ph_im))
            sub(st_re[:, :, 1:], st_re[:, :, 1:], t3)
            mul(st_im[:, :, 1:], cut(turned_re), cut(ph_im))
            mul(t3, cut(turned_im), cut(ph_re))
            o.tell(v.tensor_tensor(st_im[:, :, 1:], st_im[:, :, 1:], t3, ALU.add), s_turned)
            for b in range(4):
                dve.wait_ge(sq_done, b + 1)
                f = flat[:, b * SEQ:(b + 1) * SEQ]
                o.then(v.tensor_scalar(f, f, 0.044715, 1.0, ALU.mult, ALU.add))
                o.tell(v.tensor_tensor(f, f, u_ch[:, b].rearrange("p s c -> p (s c)"), ALU.mult), inner_done)
            for b in range(4):
                dve.wait_ge(sig_done, b + 1)
                f = flat[:, b * SEQ:(b + 1) * SEQ]
                o.tell(v.tensor_tensor(f, f, u_ch[:, b].rearrange("p s c -> p (s c)"), ALU.mult), gel_done)
            for n in range(8):
                dve.wait_ge(z_sig, n + 1)
                b, t = n // 2, n % 2
                to = y2T[:, b, :].rearrange("p (c s) -> p s c", s=STEP)[:, 4 * t:4 * t + 4, :]
                cs = lambda x: x.rearrange("p (s c) -> p s c", s=4)
                o.tell(v.tensor_tensor(to, cs(flat[:, b * SEQ + t * HALF:b * SEQ + (t + 1) * HALF]),
                                       cs(flat[:, 4 * SEQ + n * HALF:4 * SEQ + (n + 1) * HALF]), ALU.mult), y2_done)

        @block.tensor
        def _(pe):
            mm = nc.tensor.matmul
            pe.wait_ge(par_in, 16 * N_PAR)
            pe.wait_ge(h_done, TT)
            for n in range(2 * KC):
                k, t = n // 2, n % 2
                if n >= 8:
                    pe.wait_ge(tr_used, n - 7)
                for i in range(4):
                    last = nc.tensor.transpose(psb[n % 8][:, i * P:(i + 1) * P], x_all[:, 4 * t + i, k * P:(k + 1) * P], ident)
                last.then_inc(tr_ready, 1)
            pe.wait_ge(w_in_, 16)
            pe.wait_ge(tr_used, 2 * KC)
            for b in range(4):
                for t in range(2):
                    for k in range(KC):
                        last = mm(psb[2 * b + t][:, :], w_u[:, k, b * P:(b + 1) * P], hT[:, k, t * HALF:(t + 1) * HALF], start=k == 0, stop=k == KC - 1)
                    last.then_inc(u_ready, 1)
            pe.wait_ge(u_used, 8)
            for n in range(8):
                i, b = n // 4, n % 4
                last = nc.tensor.transpose(psb[i][:, b * P:(b + 1) * P], c_nat[:, i, b].rearrange("p a b -> p (a b)"), ident)
            last.then_inc(c_tr, 1)
            pe.wait_ge(mo_ready, 1)
            for n in range(8):
                for q in range(4):
                    last = nc.tensor.transpose(psb[n][:, q * P:(q + 1) * P], w1[n // 4][:, 4 * (n % 4) + q].rearrange("p s h -> p (s h)"), ident)
                last.then_inc(m_tr, 1)
            for q in range(8):
                pe.wait_ge(m_used, q + 1)
                for gg in range(4):
                    j, at = 4 * (q // 2) + gg, (q % 2) * STATE
                    g = 2 * j + q % 2
                    for i in range(2):
                        last = mm(psb[q][0:GCH, gg * P:(gg + 1) * P], b_sb[at:at + STATE, 2 + i, j, :],
                                  m_out[i][at:at + STATE, j, 0:STEP, :].rearrange("p s h -> p (s h)"), start=i == 0, stop=i == 1)
                last.then_inc(k_ready, 1)
            pe.wait_ge(u_back, 16 * STEP)
            for q in range(4):
                for i in range(2):
                    pe.wait_ge(k_used, 2 * q + i + 1)
                    for jj in range(4):
                        j = 4 * q + jj
                        for g in range(2):
                            last = mm(psb[2 * q + i][g * STATE:(g + 1) * STATE, jj * P:(jj + 1) * P],
                                      m_in[i][:, j, g * STATE:(g + 1) * STATE], u_grp[:, 2 * j + g, :], start=True, stop=True)
                    last.then_inc(s_ready, 1)
            pe.wait_ge(t_back, 16 * STEP)
            pe.wait_ge(s_turned, 1)
            for q in range(8):
                for gg in range(4):
                    j, at = 4 * (q // 2) + gg, (q % 2) * STATE
                    g = 2 * j + q % 2
                    out = psb[q][:, gg * P:(gg + 1) * P]
                    mm(out, toep[:, g, :], u_grp[:, g, :], start=True, stop=False)
                    for i, st in enumerate((st_re, st_im)):
                        last = mm(out, m_out[i][at:at + STATE, j, 1:STEP + 1, :].rearrange("p s h -> p (s h)"),
                                  st[at:at + STATE, j, :], start=False, stop=i == 1)
                last.then_inc(y_ready, 1)
            pe.wait_ge(glu_w, 16)
            pe.wait_ge(gel_done, 4)
            for n in range(8):
                b, t = n // 2, n % 2
                pe.wait_ge(y_used, n + 1)
                for k in range(4):
                    last = mm(psb[n][:, :], w_u[:, k, b * P:(b + 1) * P], flat[:, k * SEQ + t * HALF:k * SEQ + (t + 1) * HALF], start=k == 0, stop=k == 3)
                last.then_inc(z_ready, 1)
    clear_sems(nc, sems)


def attention(nc, I, S, hT, y2T, oT, psb, const):
    ctx, sems = ExitStack(), []
    with ctx:
        sb = lambda n, s, d=F32: ctx.enter_context(nc.sbuf_tensor("b_" + n, s, d))
        sem = lambda n: own_sem(nc, sems, "b_" + n)
        wring = sb("wring", [P, 3, KC * HALF])
        wv = lambda s: wring[:, s, :].rearrange("p (k n) -> p k n", k=KC)
        w_br = wring[:, 2, :].rearrange("p (k n) -> p k n", k=4)
        att = wring[:, :, :].rearrange("p a b -> p (a b)")
        pr = lambda s: att[:, s * SEQ:(s + 1) * SEQ]
        sm_ = lambda s: att[:, (2 + s) * SEQ:(3 + s) * SEQ]
        pT = lambda s: att[:, (4 + s) * SEQ:(5 + s) * SEQ]
        o_nat = lambda s: att[:, 6 * SEQ + s * AW:6 * SEQ + (s + 1) * AW]
        qT, kT = sb("qT", [P, 4, SEQ]), sb("kT", [P, 4, SEQ])
        v_sb = sb("v", [P, TT, AW])
        qiT, kiT = sb("qiT", [P, 2, SEQ]), sb("kiT", [P, SEQ])
        wi = sb("wi", [P, TT, IH])
        off = [P * i * (i + 1) // 2 for i in range(TT + 1)]
        score = sb("score", [P, off[TT]])
        mask = sb("mask", [P, off[TT]], BF16)
        buf = sb("buf", [P, 4, HALF])
        nat = sb("nat", [P, 2, HALF])
        rt = lambda s: buf[:, s, :]
        top8 = sb("top8", [P, 8])
        stats = sb("stats", [P, 4, 4])
        b_gates = sb("b_gates", [P, 16])
        cos, sin = (sb(n, [P, TT, (HD + ID) // 2]) for n in ("cos", "sin"))
        ident = const["ident"]

        w_in_ = [sem(f"w_in{s}") for s in range(3)]
        bias_in, rope_in = sem("bias_in"), sem("rope_in")
        dve_step, pool_done = sem("dve_step"), sem("pool_done")
        proj_ready, rope_done, tr_ready, tr_used, v_used = (sem(n) for n in ("proj_ready", "rope_done", "tr_ready", "tr_used", "v_used"))
        dots_ready, relu_done, relu_used = sem("dots_ready"), sem("relu_done"), sem("relu_used")
        gate_ready, gate_used, br_used = sem("gate_ready"), sem("gate_used"), sem("br_used")
        gate_out = [sem(f"gate_out{s}") for s in range(2)]
        masks_done = sem("masks_done")
        s_ready, m_done, e_done, pt_ready, pt_act, pt_dve, pv_ready, o_done, ot_ready, ot_used = (
            sem(n) for n in ("s_ready", "m_done", "e_done", "pt_ready", "pt_act", "pt_dve", "pv_ready", "o_done", "ot_ready", "ot_used"))
        block = ctx.enter_context(nc.Block())

        N_UNITS = 3 * TT
        blocks = [(C_QI, NI), (C_Q, AW), (C_K, AW), (C_V, AW), (C_GS, HALF), (C_GS + HALF, HALF), (C_GA, HALF), (C_GA + HALF, HALF)]
        order = list(range(TT - 1, -1, -1))
        dots = [(i, kb, h) for i in order if (i + 1) * P > TOPK for kb in range((i + 4) // 4) for h in range(IH)]
        heads = [(i, h) for i in order for h in range(HEADS)]
        wide_before = [sum(1 for i, h in heads[:n] if i >= 4) for n in range(len(heads) + 1)]

        @block.sync
        def _(sp):
            w3 = I["w_in"][0].rearrange("(k p) n -> p k n", p=P)
            for n, (c, width) in enumerate(blocks):
                if 2 <= n <= 4:
                    sp.wait_ge(proj_ready, TT * (n - 1))
                if n == 5:
                    sp.wait_ge(proj_ready, 4 * TT)
                if n >= 6:
                    sp.wait_ge(gate_ready, 8 * (n - 5))
                sp.dma_start(wv(n % 2)[:, :, 0:width], w3[:, :, c:c + width]).then_inc(w_in_[n % 2], 16)
                if n == 1:
                    sp.dma_start(w_br, I["w_ssm_br"][0].rearrange("(k p) n -> p k n", p=P)).then_inc(w_in_[2], 16)
                    with nc.allow_non_contiguous_dma(reason="8 KB of biases"):
                        sp.dma_start(b_gates[:, :], I["b_gates"][0].rearrange("(b p) -> p b", p=P)).then_inc(bias_in, 16)
                if n >= 5:
                    for m in range(8 * (n - 5), 8 * (n - 4)) if n < 7 else range(8 * (n - 5), 32):
                        to = S["mix_s"] if m < 16 else S["gate_a"]
                        b, t = (m % 16) // 2, m % 2
                        if m < 16:
                            sp.wait_ge(pool_done, m + 1)
                        else:
                            sp.wait_ge(gate_used, m + 1)
                        sp.dma_start(to[b, :, t * HALF:(t + 1) * HALF], buf[:, m % 2, :]).then_inc(gate_out[m % 2], 16)
            for s in range(2):
                sp.wait_ge(gate_out[s], 16 * 16)

        @block.gpsimd
        def _(pool):
            for m in range(16):
                pool.wait_ge(br_used, m + 1)
                nc.gpsimd.tensor_tensor(buf[:, m % 2, :], buf[:, m % 2, :], buf[:, 2 + m % 2, :], ALU.mult).then_inc(pool_done, 1)

        @block.scalar
        def _(act):
            for t, name in ((cos, "t_cos"), (sin, "t_sin")):
                act.dma_start(t[:, :, :], I[name].rearrange("(t p) n -> p t n", p=P)).then_inc(rope_in, 16)
            for n in range(N_UNITS):
                act.wait_ge(tr_ready, n + 1)
                kind, t = n // TT, n % TT
                cols = slice(t * P, (t + 1) * P)
                src = psb[4 + n % 4][:, :].rearrange("p (b n) -> p b n", b=4)
                if kind == 0:
                    nc.scalar.copy(qiT[:, :, cols], src[:, 0:2])
                    nc.scalar.copy(kiT[:, cols], src[:, 2]).then_inc(tr_used, 1)
                else:
                    nc.scalar.copy((qT if kind == 1 else kT)[:, :, cols], src).then_inc(tr_used, 1)
            for t in range(TT):
                act.wait_ge(proj_ready, N_UNITS + t + 1)
                nc.scalar.copy(v_sb[:, t, :], psb[(N_UNITS + t) % 4][:, :]).then_inc(v_used, 1)
            act.wait_ge(rope_done, N_UNITS)
            for m, (i, kb, h) in enumerate(dots):
                w = min(HALF, (i + 1) * P - kb * HALF)
                act.wait_ge(dots_ready, m + 1)
                if m >= 4:
                    act.wait_ge(relu_used, m - 3)
                nc.scalar.activation(buf[:, m % 4, 0:w], psb[m % 2][:, 0:w], ACT.Relu).then_inc(relu_done, 1)
            act.wait_ge(relu_used, len(dots))
            act.wait_ge(bias_in, 16)
            for m in range(32):
                b, t = (m % 16) // 2, m % 2
                act.wait_ge(gate_ready, m + 1)
                if m >= 2:
                    act.wait_ge(gate_out[m % 2], 16 * (m // 2))
                nc.scalar.activation(buf[:, m % 2, :], psb[2 + m % 2][:, :], ACT.Sigmoid,
                                     bias=b_gates[:, m // 2:m // 2 + 1]).then_inc(gate_used, 1)
                if m < 16:
                    act.wait_ge(gate_used, m + 1)
                    nc.scalar.copy(buf[:, 2 + m % 2, :], psb[4 + m % 2][:, :]).then_inc(br_used, 1)
            for n in range(len(heads) + 1):
                if n < len(heads):
                    i, h = heads[n]
                    nk = (i + 1) * P
                    act.wait_ge(m_done, n + 1)
                    if n >= 2:
                        act.wait_ge(pt_ready, n - 1)
                    nc.scalar.activation(pr(n % 2)[:, 0:nk], sm_(n % 2)[:, 0:nk], ACT.Exp, bias=stats[:, n % 4, 1:2],
                                         scale=HD ** -0.5, accum_out=stats[:, n % 4, 2:3]).then_inc(e_done, 1)
                if n >= 1:
                    i = heads[n - 1][0]
                    w = min(HALF, (i + 1) * P)
                    act.wait_ge(pt_ready, n)
                    if n >= 3:
                        act.wait_ge(pv_ready, n - 2)
                    nc.scalar.copy(pT((n - 1) % 2)[:, 0:w], psb[2][:, 0:w]).then_inc(pt_act, 1)
                if n > HEADS and n % HEADS == 2 or n == len(heads):
                    a = min(n // HEADS, TT)
                    i = order[a - 1]
                    act.wait_ge(ot_ready, a)
                    nc.scalar.copy(oT[:, :, i * P:(i + 1) * P], psb[3][:, :].rearrange("p (b n) -> p b n", b=4)).then_inc(ot_used, 1)

        @block.vector
        def _(dve):
            v = nc.vector
            o = Order(dve, dve_step)
            dve.wait_ge(rope_in, 32)
            for n in range(N_UNITS):
                kind, t = n // TT, n % TT
                dve.wait_ge(proj_ready, n + 1)
                if n >= 2:
                    dve.wait_ge(tr_ready, n - 1)
                nh, hw = (IH + 1, ID) if kind == 0 else (HEADS, HD)
                half = hw // 2
                z = psb[n % 4][:, 0:nh * hw].rearrange("p (h two c) -> p h two c", h=nh, two=2)
                out = nat[:, n % 2, 0:nh * hw].rearrange("p (h two c) -> p h two c", h=nh, two=2)
                at = 0 if kind else HD // 2
                cs, sn = (c[:, t, at:at + half].unsqueeze(1).broadcast_to([P, nh, half]) for c in (cos, sin))
                tm = [rt(s)[:, 0:nh * half].rearrange("p (h c) -> p h c", h=nh) for s in range(4)]
                for s, (a, b) in enumerate(((0, cs), (1, sn), (1, cs), (0, sn))):
                    o.go(v.tensor_tensor(tm[s], z[:, :, a], b, ALU.mult))
                if kind == 0:
                    o.go(v.tensor_scalar(wi[:, t, :], psb[n % 4][:, NI - IH:NI], float(IH * ID) ** -0.5, None, ALU.mult))
                o.wait()
                if kind == 0:
                    o.go(v.tensor_tensor(out[:, :, 0], tm[0], tm[1], ALU.subtract))
                    o.then(v.tensor_tensor(out[:, :, 1], tm[2], tm[3], ALU.add))
                    o.tell(v.tensor_copy(nat[:, n % 2, (IH + 1) * ID:(IH + 4) * ID].rearrange("p (a c) -> p a c", a=3),
                                         nat[:, n % 2, IH * ID:(IH + 1) * ID].unsqueeze(1).broadcast_to([P, 3, ID])), rope_done)
                else:
                    o.then(v.tensor_tensor(out[:, :, 0], tm[0], tm[1], ALU.subtract))
                    o.tell(v.tensor_tensor(out[:, :, 1], tm[2], tm[3], ALU.add), rope_done)
            for m, (i, kb, h) in enumerate(dots):
                w = min(HALF, (i + 1) * P - kb * HALF)
                sc = score[:, off[i] + kb * HALF:off[i] + kb * HALF + w]
                dve.wait_ge(relu_done, m + 1)
                if h == 0:
                    o.tell(v.tensor_scalar(sc, buf[:, m % 4, 0:w], wi[:, i, h:h + 1], None, ALU.mult), relu_used)
                else:
                    o.tell(v.scalar_tensor_tensor(sc, buf[:, m % 4, 0:w], wi[:, i, h:h + 1], sc, ALU.mult, ALU.add), relu_used)
            for i in order:
                row, m_row = score[:, off[i]:off[i + 1]], mask[:, off[i]:off[i + 1]]
                corner = (slice(0, P // 2), slice((i + 1) * P - P // 2, (i + 1) * P))
                if (i + 1) * P > TOPK:
                    o.then(v.memset(row[corner[0], corner[1]], NEG))
                    for _ in range(TOPK // 8):
                        o.then(v.max(top8[:, :], row))
                        o.then(v.match_replace(row, top8[:, :], row, 10.0 * NEG))
                    o.then(v.tensor_scalar(m_row, row, 10.0 * NEG, NEG, ALU.not_equal, ALU.mult))
                else:
                    o.then(v.memset(m_row, 0.0))
                    o.then(v.memset(m_row[corner[0], corner[1]], NEG))
            dve.wait_ge(gate_ready, 32)
            for n in range(len(heads) + 2):
                if n < len(heads):
                    i, h = heads[n]
                    nk = (i + 1) * P
                    dve.wait_ge(s_ready, n + 1)
                    if n >= 2:
                        dve.wait_ge(e_done, n - 1)
                    st = stats[:, n % 4]
                    s2 = att_psum(psb, n)
                    for kb in range((i + 4) // 4):
                        w = min(HALF, nk - kb * HALF)
                        o.go(v.tensor_tensor_reduce(out=sm_(n % 2)[:, kb * HALF:kb * HALF + w], in0=s2[kb][:, 0:w],
                                                    in1=mask[:, off[i] + kb * HALF:off[i] + kb * HALF + w], scale=1.0,
                                                    scalar=10.0 * NEG, op0=ALU.add, op1=ALU.max, accum_out=st[:, 2 * kb:2 * kb + 1]))
                    o.wait()
                    if nk > HALF:
                        o.then(v.tensor_tensor(st[:, 0:1], st[:, 0:1], st[:, 2:3], ALU.max))
                    o.tell(v.tensor_scalar(st[:, 1:2], st[:, 0:1], -(HD ** -0.5), None, ALU.mult), m_done)
                if 1 <= n <= len(heads) and heads[n - 1][0] >= 4:
                    i = heads[n - 1][0]
                    w = (i + 1) * P - HALF
                    dve.wait_ge(pt_ready, n)
                    if n >= 3:
                        dve.wait_ge(pv_ready, n - 2)
                    o.tell(v.tensor_copy(pT((n - 1) % 2)[:, HALF:HALF + w], psb[3][:, 0:w]), pt_dve)
                if n >= 2:
                    i, h = heads[n - 2]
                    st = stats[:, (n - 2) % 4]
                    a = (n - 2) // HEADS
                    dve.wait_ge(pv_ready, n - 1)
                    if h == 0 and a >= 2:
                        dve.wait_ge(ot_ready, a - 1)
                    o.then(v.reciprocal(st[:, 3:4], st[:, 2:3]))
                    o.tell(v.tensor_scalar(o_nat(a % 2)[:, h * HD:(h + 1) * HD], psb[h % 2][:, h * HD:(h + 1) * HD], st[:, 3:4], None, ALU.mult), o_done)

        @block.tensor
        def _(pe):
            mm = nc.tensor.matmul
            for n in range(4 * TT + 2):
                kind, t = n // TT, n % TT
                if n < 4 * TT:
                    if t == 0:
                        pe.wait_ge(w_in_[kind % 2], 16 * (kind // 2 + 1))
                    if 4 <= n < N_UNITS + 4:
                        pe.wait_ge(rope_done, n - 3)
                    elif n >= N_UNITS + 4:
                        pe.wait_ge(v_used, n - 3 - N_UNITS)
                    width = blocks[kind][1]
                    for k in range(KC):
                        last = mm(psb[n % 4][:, 0:width], hT[:, k, t * P:(t + 1) * P], wv(kind % 2)[:, k, 0:width], start=k == 0, stop=k == KC - 1)
                    last.then_inc(proj_ready, 1)
                if 2 <= n < N_UNITS + 2:
                    u = n - 2
                    pe.wait_ge(rope_done, u + 1)
                    if u >= 4:
                        pe.wait_ge(tr_used, u - 3)
                    for b in range(3 if u < TT else 4):
                        last = nc.tensor.transpose(psb[4 + u % 4][:, b * P:(b + 1) * P], nat[:, u % 2, b * P:(b + 1) * P], ident)
                    last.then_inc(tr_ready, 1)
            pe.wait_ge(v_used, TT)
            pe.wait_ge(tr_used, N_UNITS)
            for m, (i, kb, h) in enumerate(dots):
                w = min(HALF, (i + 1) * P - kb * HALF)
                r = ID * (h % 4)
                if m >= 2:
                    pe.wait_ge(relu_done, m - 1)
                mm(psb[m % 2][:, 0:w], qiT[r:r + ID, h // 4, i * P:(i + 1) * P], kiT[r:r + ID, kb * HALF:kb * HALF + w],
                   start=True, stop=True).then_inc(dots_ready, 1)
            pe.wait_ge(w_in_[2], 16)
            for m in range(32):
                b, t = (m % 16) // 2, m % 2
                wb = m // 8
                if m % 8 == 0:
                    pe.wait_ge(w_in_[wb % 2], 16 * (wb // 2 + 3))
                if m >= 2:
                    pe.wait_ge(gate_used, m - 1)
                if 2 <= m < 16:
                    pe.wait_ge(br_used, m - 1)
                last = None
                if m < 16:
                    for k in range(4):
                        mm(psb[4 + m % 2][:, :], w_br[:, k, b * P:(b + 1) * P], y2T[:, k, t * HALF:(t + 1) * HALF], start=k == 0, stop=k == 3)
                for k in range(KC):
                    last = mm(psb[2 + m % 2][:, :], wv(wb % 2)[:, k, (b % 4) * P:(b % 4 + 1) * P], hT[:, k, t * HALF:(t + 1) * HALF],
                              start=k == 0, stop=k == KC - 1)
                last.then_inc(gate_ready, 1)
            pe.wait_ge(gate_used, 32)
            pe.wait_ge(br_used, 16)
            for n in range(-1, len(heads) + 1):
                if n + 1 < len(heads):
                    i, h = heads[n + 1]
                    r = HD * (h % 2)
                    s2 = att_psum(psb, n + 1)
                    if n + 1 >= 2:
                        pe.wait_ge(m_done, n)
                    for kb in range((i + 4) // 4):
                        w = min(HALF, (i + 1) * P - kb * HALF)
                        last = mm(s2[kb][:, 0:w], qT[r:r + HD, h // 2, i * P:(i + 1) * P], kT[r:r + HD, h // 2, kb * HALF:kb * HALF + w], start=True, stop=True)
                    last.then_inc(s_ready, 1)
                if 0 <= n < len(heads):
                    i, h = heads[n]
                    pe.wait_ge(e_done, n + 1)
                    if n >= 1:
                        pe.wait_ge(pt_act, n)
                        if wide_before[n]:
                            pe.wait_ge(pt_dve, wide_before[n])
                    a = n // HEADS
                    if h == 2 and a >= 1:
                        pe.wait_ge(o_done, a * HEADS)
                        for b in range(4):
                            last = nc.tensor.transpose(psb[3][:, b * P:(b + 1) * P], o_nat((a - 1) % 2)[:, b * P:(b + 1) * P], ident)
                        last.then_inc(ot_ready, 1)
                    if h >= 2 and a >= 1:
                        pe.wait_ge(ot_used, a)
                    for b in range(i + 1):
                        last = nc.tensor.transpose(psb[2 + b // 4][:, (b % 4) * P:(b % 4 + 1) * P], pr(n % 2)[:, b * P:(b + 1) * P], ident)
                    last.then_inc(pt_ready, 1)
                if n >= 1:
                    i, h = heads[n - 1]
                    pe.wait_ge(pt_act, n)
                    if i >= 4:
                        pe.wait_ge(pt_dve, wide_before[n])
                    if n >= 3:
                        pe.wait_ge(o_done, n - 2)
                    for b in range(i + 1):
                        last = mm(psb[h % 2][:, h * HD:(h + 1) * HD], pT((n - 1) % 2)[:, b * P:(b + 1) * P],
                                  v_sb[:, b, h * HD:(h + 1) * HD], start=b == 0, stop=b == i)
                    last.then_inc(pv_ready, 1)
            pe.wait_ge(o_done, TT * HEADS)
            for b in range(4):
                last = nc.tensor.transpose(psb[3][:, b * P:(b + 1) * P], o_nat((TT - 1) % 2)[:, b * P:(b + 1) * P], ident)
            last.then_inc(ot_ready, 1)

    clear_sems(nc, sems)


def att_psum(psb, n):
    return psb[4 + 2 * (n % 2)], psb[5 + 2 * (n % 2)]


NT = 160
NT2 = NT - P
ITEMS = (SEQ * TOP + EXPERTS * (NT - 1)) // NT
LIST = -(-((ITEMS + 1) * NT) // P) * P
REC = 4
NO_ROW = SEQ * TOP


def rsqrt(v, o, out, a, t):
    o.then(v.tensor_scalar(t.bitcast(I32), a.bitcast(I32), 1, None, ALU.logical_shift_right))
    o.then(v.tensor_scalar(out.bitcast(I32), t.bitcast(I32), -1.0, float(0x5F3759DF), ALU.mult, ALU.add))
    for _ in range(4):
        o.then(v.scalar_tensor_tensor(t, out, 1.0, out, ALU.mult, ALU.mult))
        o.then(v.tensor_tensor(t, t, a, ALU.mult))
        o.then(v.tensor_scalar(t, t, -0.5, 1.5, ALU.mult, ALU.add))
        o.then(v.tensor_tensor(out, out, t, ALU.mult))


def mix_and_route(nc, I, S, oT, mixT, items_sb, bias_all, psb, const):
    ctx, sems = ExitStack(), []
    with ctx:
        sb = lambda n, s, d=F32: ctx.enter_context(nc.sbuf_tensor("c_" + n, s, d))
        sem = lambda n: own_sem(nc, sems, "c_" + n)
        w_ab = sb("w_ab", [P, 4, D])
        w_o = sb("w_o", [P, KC, D])
        gate = sb("gate", [P, 2, HALF])
        mix_s = sb("mix_s", [P, 2, HALF])
        x_t = sb("x_t", [P, 2, D])
        r1 = sb("r1", [P, 2, D])
        h2 = sb("h2", [P, 2, D])
        h2T = sb("h2T", [P, 2, KC, P])
        gain = sb("gain", [P, D])
        w_r = sb("w_r", [P, KC, EXPERTS])
        b_r = sb("b_r", [P, EXPERTS])
        sq = sb("sq", [P, D])
        ssq = sb("ssq", [P, 4, TT])
        logits = sb("logits", [P, TT, EXPERTS])
        v8 = sb("v8", [P, TT, 8])
        i8 = sb("i8", [P, TT, 8], U32)
        i4f = sb("i4f", [P, TT, TOP])
        wts = sb("wts", [P, TT, TOP])
        wsum = sb("wsum", [P, 2, TT])
        iota_e = sb("iota_e", [P, EXPERTS])
        iota_w = sb("iota_w", [P, 1])
        hot = sb("hot", [P, TOP, TT, EXPERTS])
        hsum = sb("hsum", [P, TT, EXPERTS])
        hsum16 = sb("hsum16", [P, TT, EXPERTS], BF16)
        tri = sb("tri", [P, P])
        tri16, ones16 = sb("tri16", [P, P], BF16), sb("ones16", [P, P], BF16)
        place = sb("place", [P, TT, EXPERTS])
        picked = sb("picked", [P, TT, EXPERTS])
        cnt = sb("cnt", [P, 8, EXPERTS])
        slot_f = sb("slot_f", [P, TOP, TT])
        slot_u = sb("slot_u", [P, TOP, TT], U32)
        rec = sb("rec", [P, TT, TOP, REC])
        empty = sb("empty", [P, LIST // P, REC])
        item_e = sb("item_e", [P, 1])
        item_i = sb("item_i", [P, 1], I32)
        b_nat = sb("b_nat", [P, 6, P])
        ident = const["ident"]

        dve_step, act_step = sem("dve_step"), sem("act_step")
        w_in_, wo_in, par_in = sem("w_in"), sem("wo_in"), sem("par_in")
        gm_in = [sem(f"gm_in{s}") for s in range(2)]
        x_in = [sem(f"x_in{s}") for s in range(2)]
        br_ready, mix_done = sem("br_ready"), sem("mix_done")
        o_ready, r1_done, sq_done, h2_done = sem("o_ready"), sem("r1_done"), sem("sq_done"), sem("h2_done")
        r1_out = [sem(f"r1_out{s}") for s in range(2)]
        ht_ready, ht_used, lg_ready, lg_done = sem("ht_ready"), sem("ht_used"), sem("lg_ready"), sem("lg_done")
        sh_done, e_done = sem("sh_done"), sem("e_done")
        hs_done, pos_ready, slots_done, items_done = sem("hs_done"), sem("pos_ready"), sem("slots_done"), sem("items_done")
        list_clear, pool_step, pool_const, list_out, item_out, item_back, w_out = (
            sem(n) for n in ("list_clear", "pool_step", "pool_const", "list_out", "item_out", "item_back", "w_out"))
        b_in, bt_ready = sem("b_in"), sem("bt_ready")
        block = ctx.enter_context(nc.Block())

        @block.sync
        def _(sp):
            sp.dma_start(w_ab[:, :, :], I["w_attn_br"][0].rearrange("(k p) n -> p k n", p=P)).then_inc(w_in_, 16)
            for m in range(2 * KC):
                b, t = m // 2, m % 2
                if m >= 2:
                    sp.wait_ge(mix_done, m - 1)
                cols = slice(t * HALF, (t + 1) * HALF)
                sp.dma_start(gate[:, m % 2, :], S["gate_a"][b, :, cols]).then_inc(gm_in[m % 2], 16)
                sp.dma_start(mix_s[:, m % 2, :], S["mix_s"][b, :, cols]).then_inc(gm_in[m % 2], 16)
                if m == 1:
                    sp.dma_start(w_o[:, :, :], I["w_o"][0].rearrange("(k p) n -> p k n", p=P)).then_inc(wo_in, 16)
            for i in range(TT + 1):
                if i < TT:
                    if i >= 2:
                        sp.wait_ge(r1_done, i - 1)
                    sp.dma_start(x_t[:, i % 2, :], I["x"][0, i * P:(i + 1) * P, :]).then_inc(x_in[i % 2], 16)
                if i >= 1:
                    rows = slice((i - 1) * P, i * P)
                    sp.wait_ge(h2_done, i)
                    sp.dma_start(S["r1"][rows, :], r1[:, (i - 1) % 2, :]).then_inc(r1_out[(i - 1) % 2], 16)
                    sp.dma_start(S["h2"][rows, :], h2[:, (i - 1) % 2, :]).then_inc(r1_out[(i - 1) % 2], 16)
            sp.wait_ge(items_done, 1)
            with nc.allow_non_contiguous_dma(reason="512 bytes"):
                sp.dma_start(S["items"].unsqueeze(1), item_i[:, :]).then_inc(item_out, 16)
            for s in range(2):
                sp.wait_ge(r1_out[s], 16 * TT)
            sp.wait_ge(item_out, 16)

        @block.gpsimd
        def _(pool):
            g = nc.gpsimd
            g.iota(iota_e[:, :], pattern=[[1, EXPERTS]], base=0, channel_multiplier=0, allow_small_or_imprecise_dtypes=True).then_inc(pool_const, 1)
            g.iota(iota_w[:, :], pattern=[[1, 1]], base=0, channel_multiplier=1, allow_small_or_imprecise_dtypes=True).then_inc(pool_const, 1)
            g.memset(empty[:, :, :], 0.0).then_inc(pool_step, 1)
            pool.wait_ge(pool_step, 1)
            g.iota(empty[:, :, 1:2].bitcast(U32), pattern=[[0, LIST // P]], base=NO_ROW, channel_multiplier=0).then_inc(pool_step, 1)
            g.memset(rec[:, :, :, :], 0.0).then_inc(pool_step, 1)
            pool.wait_ge(pool_step, 3)
            pool.dma_start(S["list"].rearrange("(p n) r -> p n r", p=P), empty[:, :, :]).then_inc(list_clear, 16)
            g.iota(rec[:, :, :, 0].bitcast(U32), pattern=[[P, TT], [0, TOP]], base=0, channel_multiplier=1).then_inc(pool_step, 1)
            g.iota(rec[:, :, :, 1].bitcast(U32), pattern=[[P * TOP, TT], [1, TOP]], base=0, channel_multiplier=TOP).then_inc(pool_step, 1)
            pool.wait_ge(pool_step, 5)
            pool.wait_ge(list_clear, 16)
            pool.wait_ge(slots_done, 1)
            for k in range(TOP):
                for i in range(TT):
                    g.indirect_dma_start(out=S["list"], out_offset=bass.IndirectOffsetOnAxis(ap=slot_u[:, k, i:i + 1], axis=0),
                                         in_=rec[:, i, k, :], in_offset=None).then_inc(list_out, 16)
            pool.wait_ge(list_out, 16 * TOP * TT)

        @block.scalar
        def _(act):
            o = Order(act, act_step)
            with nc.allow_non_contiguous_dma(reason="small rows, repeated over partitions"):
                act.dma_start(gain[:, :], I["norm_ffn"][0].unsqueeze(0).broadcast_to([P, D])).then_inc(par_in, 16)
                act.dma_start(b_r[:, :], I["b_router"][0].unsqueeze(0).broadcast_to([P, EXPERTS])).then_inc(par_in, 16)
                act.dma_start(w_r[:, :, :], I["w_router"][0].rearrange("(k p) e -> p k e", p=P)).then_inc(par_in, 16)
                act.dma_start(tri[:, :], I["t_tri"]).then_inc(par_in, 16)
            for j, name in enumerate(("b_gate", "b_up", "b_down")):
                act.dma_start(b_nat[:, 2 * j:2 * j + 2, :], I[name][0].rearrange("(a e) (b p) -> (e b) a p", a=2, p=P)).then_inc(b_in, 16)
            act.wait_ge(bt_ready, 1)
            for j in range(3):
                o.go(nc.scalar.copy(bias_all[:, :, j, :].rearrange("p (a e) b -> p a e b", a=2),
                                    psb[4 + j][:, 0:2 * P].rearrange("p (a e b) -> p a e b", a=2, b=KC)))
            for i in range(TT):
                act.wait_ge(r1_done, i + 1)
                if i:
                    act.wait_ge(sq_done, i)
                nc.scalar.activation(sq[:, :], r1[:, i % 2, :], ACT.Square, accum_out=ssq[:, 0, i:i + 1]).then_inc(sq_done, 1)
                for b in range(2):
                    act.wait_ge(ht_ready, 2 * i + b + 1)
                    nc.scalar.copy(h2T[:, i % 2, 4 * b:4 * b + 4, :], psb[4 + b][:, :].rearrange("p (b n) -> p b n", b=4)).then_inc(ht_used, 1)
            act.wait_ge(sh_done, 1)
            nc.scalar.activation(wts[:, :, :], wts[:, :, :], ACT.Exp).then_inc(e_done, 1)
            o.wait()

        @block.vector
        def _(dve):
            v = nc.vector
            o = Order(dve, dve_step)
            dve.wait_ge(par_in, 64)
            o.go(v.tensor_copy(tri16[:, :], tri[:, :]))
            o.go(v.memset(ones16[:, :], 1.0))
            for m in range(2 * KC):
                b, t = m // 2, m % 2
                to = mixT[:, b, t * HALF:(t + 1) * HALF]
                dve.wait_ge(br_ready, m + 1)
                dve.wait_ge(gm_in[m % 2], 32 * (m // 2 + 1))
                o.then(v.tensor_tensor(to, psb[m % 4][:, :], gate[:, m % 2, :], ALU.mult))
                o.tell(v.tensor_tensor(to, to, mix_s[:, m % 2, :], ALU.add), mix_done)
            for i in range(TT + 1):
                if i < TT:
                    dve.wait_ge(x_in[i % 2], 16 * (i // 2 + 1))
                    dve.wait_ge(o_ready, i + 1)
                    if i >= 2:
                        dve.wait_ge(r1_out[i % 2], 32 * (i // 2))
                    half = lambda b: (r1[:, i % 2, b * HALF:(b + 1) * HALF], psb[2 * (i % 2) + b][:, :], x_t[:, i % 2, b * HALF:(b + 1) * HALF])
                    o.then(v.tensor_tensor(*half(0), ALU.add))
                    o.tell(v.tensor_tensor(*half(1), ALU.add), r1_done)
                    dve.wait_ge(sq_done, i + 1)
                    one = lambda r: ssq[:, r, i:i + 1]
                    o.then(v.tensor_scalar(one(0), one(0), 1.0 / D, EPS, ALU.mult, ALU.add))
                    rsqrt(v, o, one(1), one(0), one(2))
                    o.tell(v.scalar_tensor_tensor(h2[:, i % 2, :], r1[:, i % 2, :], one(1), gain[:, :], ALU.mult, ALU.mult), h2_done)
                if i >= 1:
                    dve.wait_ge(lg_ready, i)
                    o.tell(v.tensor_tensor(logits[:, i - 1, :], psb[6 + (i - 1) % 2][:, 0:EXPERTS], b_r[:, :], ALU.add), lg_done)
            for i in range(TT):
                o.go(v.max(v8[:, i, :], logits[:, i, :]))
            o.wait()
            for i in range(TT):
                o.go(v.max_index(i8[:, i, :], v8[:, i, :], logits[:, i, :]))
            o.tell(v.tensor_tensor(wts[:, :, :], v8[:, :, 0:TOP], v8[:, :, 0:1].broadcast_to([P, TT, TOP]), ALU.subtract), sh_done)
            o.wait()
            o.then(v.tensor_copy(i4f[:, :, :], i8[:, :, 0:TOP]))
            dve.wait_ge(pool_const, 2)
            shape = [P, TT, EXPERTS]
            for k in range(TOP):
                o.go(v.tensor_tensor(hot[:, k], iota_e[:, :].unsqueeze(1).broadcast_to(shape), i4f[:, :, k:k + 1].broadcast_to(shape), ALU.is_equal))
            o.wait()
            o.go(v.tensor_tensor(hsum[:, :, :], hot[:, 0], hot[:, 1], ALU.add))
            o.then(v.tensor_tensor(picked[:, :, :], hot[:, 2], hot[:, 3], ALU.add))
            o.tell(v.tensor_tensor(hsum16[:, :, :], hsum[:, :, :], picked[:, :, :], ALU.add), hs_done)
            dve.wait_ge(e_done, 1)
            o.then(v.tensor_reduce(wsum[:, 0, :], wts[:, :, :], AX.X, ALU.add))
            o.then(v.reciprocal(wsum[:, 1, :], wsum[:, 0, :]))
            dve.wait_ge(pool_step, 5)
            o.then(v.tensor_tensor(rec[:, :, :, 2], wts[:, :, :], wsum[:, 1, :].unsqueeze(2).broadcast_to([P, TT, TOP]), ALU.mult))
            dve.wait_ge(pos_ready, 1)
            c = lambda n: cnt[:, n, :]
            o.then(v.tensor_copy(c(0), psb[1][:, 0:EXPERTS]))
            o.then(v.tensor_scalar(c(1), c(0), 0.0, None, ALU.is_gt))
            for n in range(1, -(-SEQ // NT)):
                o.then(v.scalar_tensor_tensor(c(1), c(0), float(n * NT), c(1), ALU.is_gt, ALU.add))
            o.then(v.memset(c(2), 1.0))
            o.then(v.tensor_tensor_scan(c(3), c(2), c(1), 0.0, ALU.mult, ALU.add))
            o.then(v.tensor_tensor(c(4), c(3), c(1), ALU.subtract))
            o.then(v.tensor_scalar(c(4), c(4), float(NT), None, ALU.mult))
            o.then(v.tensor_tensor(place[:, :, :], psb[0][:, 0:TT * EXPERTS].rearrange("p (t e) -> p t e", t=TT),
                                   c(4).unsqueeze(1).broadcast_to(shape), ALU.add))
            for k in range(TOP):
                o.then(v.tensor_tensor(picked[:, :, :], hot[:, k], place[:, :, :], ALU.mult))
                o.then(v.tensor_reduce(slot_f[:, k, :], picked[:, :, :], AX.X, ALU.add))
            o.tell(v.tensor_copy(slot_u[:, :, :], slot_f[:, :, :]), slots_done)
            o.then(v.tensor_scalar(c(5), c(3), iota_w[:, 0:1], None, ALU.is_le))
            o.then(v.tensor_reduce(item_e[:, :], c(5), AX.X, ALU.add))
            o.then(v.tensor_copy(items_sb[:, 0:1], c(3)[0:1, EXPERTS - 1:EXPERTS]))
            o.tell(v.tensor_scalar(item_i[:, :], item_e[:, :], float(EXPERTS - 1), None, ALU.min), items_done)

        @block.tensor
        def _(pe):
            mm = nc.tensor.matmul
            pe.wait_ge(b_in, 48)
            for j in range(6):
                last = nc.tensor.transpose(psb[4 + j // 2][:, (j % 2) * P:(j % 2 + 1) * P], b_nat[:, j, :], ident)
            last.then_inc(bt_ready, 1)
            pe.wait_ge(w_in_, 16)
            for m in range(2 * KC):
                b, t = m // 2, m % 2
                if m >= 4:
                    pe.wait_ge(mix_done, m - 3)
                for k in range(4):
                    last = mm(psb[m % 4][:, :], w_ab[:, k, b * P:(b + 1) * P], oT[:, k, t * HALF:(t + 1) * HALF], start=k == 0, stop=k == 3)
                last.then_inc(br_ready, 1)
            pe.wait_ge(wo_in, 16)
            pe.wait_ge(mix_done, 2 * KC)
            pe.wait_ge(par_in, 64)
            for i in range(TT + 2):
                if i < TT:
                    if i >= 2:
                        pe.wait_ge(r1_done, i - 1)
                    for b in range(2):
                        for k in range(KC):
                            last = mm(psb[2 * (i % 2) + b][:, :], mixT[:, k, i * P:(i + 1) * P], w_o[:, k, b * HALF:(b + 1) * HALF], start=k == 0, stop=k == KC - 1)
                    last.then_inc(o_ready, 1)
                if 1 <= i <= TT:
                    pe.wait_ge(h2_done, i)
                    for b in range(2):
                        if i >= 2:
                            pe.wait_ge(ht_used, 2 * (i - 2) + b + 1)
                        for k in range(4):
                            last = nc.tensor.transpose(psb[4 + b][:, k * P:(k + 1) * P], h2[:, (i - 1) % 2, (4 * b + k) * P:(4 * b + k + 1) * P], ident)
                        last.then_inc(ht_ready, 1)
                if i >= 2:
                    n = i - 2
                    pe.wait_ge(ht_used, 2 * n + 2)
                    if n >= 2:
                        pe.wait_ge(lg_done, n - 1)
                    for k in range(KC):
                        last = mm(psb[6 + n % 2][:, 0:EXPERTS], h2T[:, n % 2, k, :], w_r[:, k, :], start=k == 0, stop=k == KC - 1)
                    last.then_inc(lg_ready, 1)
            pe.wait_ge(hs_done, 1)
            for i in range(TT):
                for j in range(i + 1):
                    mm(psb[0][:, i * EXPERTS:(i + 1) * EXPERTS], (tri16 if j == i else ones16)[:, :], hsum16[:, j, :], start=j == 0, stop=j == i)
            for j in range(TT):
                last = mm(psb[1][:, 0:EXPERTS], ones16[:, :], hsum16[:, j, :], start=j == 0, stop=j == TT - 1)
            last.then_inc(pos_ready, 1)
    clear_sems(nc, sems)


CW = 256
NCW = D // CW


def experts(nc, I, S, items_sb, bias_all, psb, const):
    ctx, sems = ExitStack(), []
    with ctx:
        sb = lambda n, s, d=F32: ctx.enter_context(nc.sbuf_tensor("d_" + n, s, d))
        sem = lambda n: own_sem(nc, sems, "d_" + n)
        w_g, w_u, w_d = (sb(n, [P, NCW, KC, CW]) for n in ("w_g", "w_u", "w_d"))
        x_rows, x_rows2 = sb("x_rows", [P, D]), sb("x_rows2", [NT2, D])
        xT = sb("xT", [P, KC, NT])
        aT = sb("aT", [P, KC, NT])
        yT = sb("yT", [P, 2, NT])
        y_rows, y_rows2 = sb("y_rows", [P, D]), sb("y_rows2", [NT2, D])
        g_sb, s_sb, u_sb = sb("g_sb", [P, 2, NT]), sb("s_sb", [P, 2, NT]), sb("u_sb", [P, 2, NT])
        nxt, nxt2 = sb("nxt", [P, REC]), sb("nxt2", [NT2, REC])
        cur, cur2 = sb("cur", [P, REC]), sb("cur2", [NT2, REC])
        b_nxt, b_cur = sb("b_nxt", [P, 3, KC]), sb("b_cur", [P, 3, KC])
        e_sb = sb("e_sb", [1, 1], I32)
        ident = const["ident"]

        wg_in, wu_in, wd_in = ([sem(f"{n}{c}") for c in range(NCW)] for n in ("wg_in", "wu_in", "wd_in"))
        e_in, b_in, list_in, x_in, x2_in, y_out = (sem(n) for n in ("e_in", "b_in", "list_in", "x_in", "x2_in", "y_out"))
        dve_step = sem("dve_step")
        sp_held, pool_held = sem("sp_held"), sem("pool_held")
        cur_ready, gu_ready, g_done, gu_read, s_done, a_done = (sem(n) for n in ("cur_ready", "gu_ready", "g_done", "gu_read", "s_done", "a_done"))
        xt_ready, xt_used, yd_ready, yt_done, yr_ready, yr_done = (sem(n) for n in ("xt_ready", "xt_used", "yd_ready", "yt_done", "yr_ready", "yr_done"))
        block = ctx.enter_context(nc.Block())

        def held(eng, own):
            eng.sem_inc(own, 1)

        XR = [(0, 3), (3, 6), (6, 8)]
        most = ITEMS

        def loop(eng, body):
            n = eng.value_load(items_sb[0:1, 0:1], min_val=2, max_val=most)
            body(0, True)
            with eng.Fori(1, n) as w:
                body(w, False)

        @block.sync
        def _(sp):
            def expert_of(w):
                sp.dma_start(e_sb[:, :], S["items"].unsqueeze(0)[:, bass.ds(w, 1)]).then_inc(e_in, 16)
                sp.wait_ge(e_in, 16 * (w + 1))
                held(sp, sp_held)
                return sp.value_load(e_sb[0:1, 0:1], min_val=0, max_val=EXPERTS - 1)

            def body(w, first):
                e = expert_of(w)
                if not first:
                    sp.wait_ge(cur_ready, w)
                sp.dma_start(b_nxt[:, :, :], bias_all[:, bass.ds(e, 1), :, :].rearrange("p a j b -> p (a j) b")).then_inc(b_in, 16)
                for c in range(NCW):
                    if not first:
                        sp.wait_ge(gu_ready, 2 * KC // 2 * w - KC + 2 * c + 2)
                    for t, name, s in ((w_g, "w_gate", wg_in), (w_u, "w_up", wu_in)):
                        sp.dma_start(t[:, c], I[name][0][bass.ds(e, 1), :, c * CW:(c + 1) * CW]
                                     .rearrange("a (k p) n -> p (a k) n", p=P)).then_inc(s[c], 16)
                for c in range(NCW):
                    if not first:
                        sp.wait_ge(yd_ready, KC * w - KC + 2 * c + 2)
                    sp.dma_start(w_d[:, c], I["w_down"][0][bass.ds(e, 1), :, c * CW:(c + 1) * CW]
                                 .rearrange("a (k p) n -> p (a k) n", p=P)).then_inc(wd_in[c], 16)
            loop(sp, body)

        @block.gpsimd
        def _(pool):
            def fetch(w):
                pool.dma_start(nxt[:, :], S["list"][bass.ds(w * NT, P), :]).then_inc(list_in, 16)
                pool.dma_start(nxt2[:, :], S["list"][bass.ds(w * NT + P, NT2), :]).then_inc(list_in, 16)
                pool.wait_ge(list_in, 32 * (w + 1))
                held(pool, pool_held)
                for t, n, s in ((x_rows, nxt, x_in), (x_rows2, nxt2, x2_in)):
                    nc.gpsimd.indirect_dma_start(out=t[:, :], out_offset=None, in_=S["h2"],
                                                 in_offset=bass.IndirectOffsetOnAxis(ap=n[:, 0:1].bitcast(U32), axis=0)).then_inc(s, 16)

            def body(w, first):
                pool.wait_ge(cur_ready, w + 1)
                pool.wait_ge(xt_ready, 3 * w + 3)
                fetch(w + 1)
                pool.wait_ge(yr_done, 4 * w + 4)
                held(pool, pool_held)
                for t, n in ((y_rows, cur), (y_rows2, cur2)):
                    nc.gpsimd.indirect_dma_start(out=S["ys"], out_offset=bass.IndirectOffsetOnAxis(ap=n[:, 1:2].bitcast(U32), axis=0),
                                                 in_=t[:, :], in_offset=None, bounds_check=NO_ROW - 1, oob_is_err=False).then_inc(y_out, 16)
                pool.wait_ge(y_out, 32 * (w + 1))
            fetch(0)
            loop(pool, body)
            pool.wait_ge(list_in, 32)

        @block.scalar
        def _(act):
            def turned_rows(w):
                for r, (k0, k1) in enumerate(XR):
                    act.wait_ge(xt_ready, 3 * w + r + 1)
                    nc.scalar.copy(xT[:, k0:k1, :], psb[7][:, 0:(k1 - k0) * NT].rearrange("p (k n) -> p k n", n=NT)).then_inc(xt_used, 1)

            def body(w, first):
                for b in range(KC):
                    act.wait_ge(g_done, KC * w + b + 1)
                    if b >= 2:
                        act.wait_ge(a_done, KC * w + b - 1)
                    elif not first:
                        act.wait_ge(a_done, KC * w + b - 1)
                    nc.scalar.activation(s_sb[:, b % 2, :], g_sb[:, b % 2, :], ACT.Sigmoid, scale=1.702).then_inc(s_done, 1)
                turned_rows(w + 1)
                for b in range(KC + 1):
                    if b < KC:
                        act.wait_ge(yd_ready, KC * w + b + 1)
                        if b >= 2 and b % 2 == 0:
                            act.wait_ge(yr_ready, 4 * w + b // 2)
                        nc.scalar.activation(yT[:, b % 2, :], psb[3 + b % 2][:, 0:NT], ACT.Identity,
                                             bias=b_cur[:, 2, b:b + 1]).then_inc(yt_done, 1)
                    if b >= 2 and b % 2 == 0:
                        r = b // 2 - 1
                        act.wait_ge(yr_ready, 4 * w + r + 1)
                        src = psb[5 + r % 2]
                        cols = slice(r * 2 * P, (r + 1) * 2 * P)
                        nc.scalar.activation(y_rows[:, cols], src[:, 0:2 * P], ACT.Copy, scale=cur[:, 2:3])
                        nc.scalar.activation(y_rows2[:, cols], src[0:NT2, 2 * P:4 * P], ACT.Copy, scale=cur2[:, 2:3]).then_inc(yr_done, 1)
            turned_rows(0)
            loop(act, body)

        @block.vector
        def _(dve):
            v = nc.vector

            def body(w, first):
                dve.wait_ge(list_in, 32 * (w + 1))
                dve.wait_ge(b_in, 16 * (w + 1))
                if not first:
                    dve.wait_ge(y_out, 32 * w)
                    dve.wait_ge(yr_done, 4 * w)
                v.tensor_copy(cur[:, :].bitcast(U32), nxt[:, :].bitcast(U32))
                v.tensor_copy(cur2[:, :].bitcast(U32), nxt2[:, :].bitcast(U32))
                v.tensor_copy(b_cur[:, :, :], b_nxt[:, :, :]).then_inc(cur_ready, 1)
                dve.wait_ge(cur_ready, w + 1)
                for b in range(KC + 1):
                    if b < KC:
                        src, s = psb[b % 3], b % 2
                        dve.wait_ge(gu_ready, KC * w + b + 1)
                        if b >= 2 or not first:
                            dve.wait_ge(a_done, KC * w + b - 1)
                        v.tensor_scalar(g_sb[:, s, :], src[:, 0:NT], b_cur[:, 0, b:b + 1], SWIGLU_LIMIT, ALU.add, ALU.min).then_inc(g_done, 1)
                        v.tensor_scalar(u_sb[:, s, :], src[:, CW:CW + NT], b_cur[:, 1, b:b + 1], SWIGLU_LIMIT, ALU.add, ALU.min).then_inc(gu_read, 1)
                        dve.wait_ge(gu_read, KC * w + b + 1)
                        v.tensor_scalar(u_sb[:, s, :], u_sb[:, s, :], -SWIGLU_LIMIT, 1.0, ALU.max, ALU.add).then_inc(dve_step, 1)
                    if b >= 1:
                        s = (b - 1) % 2
                        dve.wait_ge(s_done, KC * w + b)
                        v.tensor_tensor(s_sb[:, s, :], s_sb[:, s, :], g_sb[:, s, :], ALU.mult).then_inc(dve_step, 1)
                        dve.wait_ge(dve_step, 2 * KC * w + min(b + 1, KC) + b)
                        v.tensor_tensor(aT[:, b - 1, :], s_sb[:, s, :], u_sb[:, s, :], ALU.mult).then_inc(a_done, 1)
            loop(dve, body)

        @block.tensor
        def _(pe):
            mm, tr = nc.tensor.matmul, nc.tensor.transpose

            def turn_rows(w):
                pe.wait_ge(x_in, 16 * (w + 1))
                pe.wait_ge(x2_in, 16 * (w + 1))
                for r, (k0, k1) in enumerate(XR):
                    if r or not isinstance(w, int):
                        pe.wait_ge(xt_used, 3 * w + r)
                    for k in range(k0, k1):
                        at = (k - k0) * NT
                        tr(psb[7][:, at:at + P], x_rows[:, k * P:(k + 1) * P], ident)
                        last = tr(psb[7][:, at + P:at + NT], x_rows2[:, k * P:(k + 1) * P], ident[0:NT2, 0:NT2])
                    last.then_inc(xt_ready, 1)

            def body(w, first):
                pe.wait_ge(xt_used, 3 * w + 3)
                for b in range(KC):
                    c, at = b // 2, (b % 2) * P
                    if b % 2 == 0:
                        pe.wait_ge(wg_in[c], 16 * (w + 1))
                        pe.wait_ge(wu_in[c], 16 * (w + 1))
                    if b >= 3 or not first:
                        pe.wait_ge(gu_read, KC * w + b - 2)
                    for wt, to in ((w_g, 0), (w_u, CW)):
                        for k in range(KC):
                            last = mm(psb[b % 3][:, to:to + NT], wt[:, c, k, at:at + P], xT[:, k, :], start=k == 0, stop=k == KC - 1)
                    last.then_inc(gu_ready, 1)
                turn_rows(w + 1)
                pe.wait_ge(a_done, KC * w + KC)
                for b in range(KC + 1):
                    if b < KC:
                        c, at = b // 2, (b % 2) * P
                        if b % 2 == 0:
                            pe.wait_ge(wd_in[c], 16 * (w + 1))
                        if b >= 2 or not first:
                            pe.wait_ge(yt_done, KC * w + b - 1)
                        for k in range(KC):
                            last = mm(psb[3 + b % 2][:, 0:NT], w_d[:, c, k, at:at + P], aT[:, k, :], start=k == 0, stop=k == KC - 1)
                        last.then_inc(yd_ready, 1)
                    if b >= 1:
                        d = b - 1
                        r, at = d // 2, (d % 2) * P
                        pe.wait_ge(yt_done, KC * w + b)
                        if d % 2 == 0 and (d >= 4 or not first):
                            pe.wait_ge(yr_done, 4 * w + r - 1)
                        tr(psb[5 + r % 2][:, at:at + P], yT[:, d % 2, 0:P], ident)
                        last = tr(psb[5 + r % 2][0:NT2, 2 * P + at:2 * P + at + P], yT[:, d % 2, P:NT], ident)
                        if d % 2:
                            last.then_inc(yr_ready, 1)
            turn_rows(0)
            loop(pe, body)
    clear_sems(nc, sems)


def combine(nc, I, S, out, psb, const):
    ctx, sems = ExitStack(), []
    with ctx:
        sb = lambda n, s, d=F32: ctx.enter_context(nc.sbuf_tensor("e_" + n, s, d))
        sem = lambda n: own_sem(nc, sems, "e_" + n)
        PK = PLE // P
        w_gate = sb("w_gate", [P, KC, D])
        w_proj = sb("w_proj", [P, PK, D])
        gain = sb("gain", [P, D])
        ys = sb("ys", [P, 2, TOP, D])
        r = sb("r", [P, 2, D])
        p_t = sb("p_t", [P, 2, PLE])
        part = sb("part", [P, D])
        rT = sb("rT", [P, 2, KC, P])
        pT = sb("pT", [P, 2, PK, P])
        gate = sb("gate", [P, 2, D])
        sq = sb("sq", [P, D])
        ssq = sb("ssq", [P, 3, TT])
        res = sb("res", [P, 2, D])
        ident = const["ident"]
        w_in_, gain_in = sem("w_in"), sem("gain_in")
        t_in = [sem(f"t_in{s}") for s in range(2)]
        outs = [sem(f"outs{s}") for s in range(2)]
        dve_step = sem("dve_step")
        r2_done, t_ready, t_used, g_ready, g_done, p_ready, r3_done, sq_done, res_done = (
            sem(n) for n in ("r2_done", "t_ready", "t_used", "g_ready", "g_done", "p_ready", "r3_done", "sq_done", "res_done"))
        block = ctx.enter_context(nc.Block())

        @block.sync
        def _(sp):
            for i in range(TT + 2):
                if i < TT:
                    rows = slice(i * P, (i + 1) * P)
                    if i >= 2:
                        sp.wait_ge(res_done, i - 1)
                    sp.dma_start(ys[:, i % 2], S["ys"][i * P * TOP:(i + 1) * P * TOP, :].rearrange("(p k) d -> p k d", k=TOP)).then_inc(t_in[i % 2], 16)
                    sp.dma_start(r[:, i % 2, :], S["r1"][rows, :]).then_inc(t_in[i % 2], 16)
                    sp.dma_start(p_t[:, i % 2, :], I["p"][0, 0][rows, :]).then_inc(t_in[i % 2], 16)
                if i == 1:
                    sp.dma_start(w_gate[:, :, :], I["w_ple_gate"][0].rearrange("(k p) n -> p k n", p=P)).then_inc(w_in_, 16)
                    sp.dma_start(w_proj[:, :, :], I["w_ple_proj"][0].rearrange("(k p) n -> p k n", p=P)).then_inc(w_in_, 16)
                if 1 <= i <= TT:
                    sp.wait_ge(res_done, i)
                    sp.dma_start(out[0, (i - 1) * P:i * P, :], res[:, (i - 1) % 2, :]).then_inc(outs[(i - 1) % 2], 16)
            for s in range(2):
                sp.wait_ge(outs[s], 16 * (TT // 2))

        @block.scalar
        def _(act):
            act.dma_start(gain[:, :], I["norm_final"].unsqueeze(0).broadcast_to([P, D])).then_inc(gain_in, 16)
            for i in range(TT):
                for b in range(2):
                    act.wait_ge(t_ready, 3 * i + b + 1)
                    nc.scalar.copy(rT[:, i % 2, 4 * b:4 * b + 4, :], psb[b][:, :].rearrange("p (b n) -> p b n", b=4)).then_inc(t_used, 1)
                act.wait_ge(t_ready, 3 * i + 3)
                nc.scalar.copy(pT[:, i % 2], psb[2][:, 0:PLE].rearrange("p (b n) -> p b n", b=PK)).then_inc(t_used, 1)
                for b in range(2):
                    act.wait_ge(g_ready, 2 * i + b + 1)
                    nc.scalar.activation(gate[:, i % 2, b * HALF:(b + 1) * HALF], psb[3 + b][:, :], ACT.Sigmoid).then_inc(g_done, 1)
                act.wait_ge(r3_done, i + 1)
                if i:
                    act.wait_ge(sq_done, i)
                nc.scalar.activation(sq[:, :], r[:, i % 2, :], ACT.Square, accum_out=ssq[:, 0, i:i + 1]).then_inc(sq_done, 1)

        @block.vector
        def _(dve):
            v = nc.vector
            o = Order(dve, dve_step)

            def gather_sum(i):
                s = i % 2
                dve.wait_ge(t_in[s], 48 * (i // 2 + 1))
                o.go(v.tensor_tensor(part[:, :], ys[:, s, 0, :], ys[:, s, 1, :], ALU.add))
                o.then(v.tensor_tensor(r[:, s, :], r[:, s, :], ys[:, s, 2, :], ALU.add))
                o.go(v.tensor_tensor(part[:, :], part[:, :], ys[:, s, 3, :], ALU.add))
                o.wait()
                o.tell(v.tensor_tensor(r[:, s, :], r[:, s, :], part[:, :], ALU.add), r2_done)

            gather_sum(0)
            dve.wait_ge(gain_in, 16)
            for i in range(TT):
                s = i % 2
                if i + 1 < TT:
                    gather_sum(i + 1)
                for b in range(2):
                    cols = slice(b * HALF, (b + 1) * HALF)
                    dve.wait_ge(g_done, 2 * i + b + 1)
                    dve.wait_ge(p_ready, 2 * i + b + 1)
                    o.then(v.tensor_tensor(gate[:, s, cols], gate[:, s, cols], psb[5 + b][:, :], ALU.mult))
                o.tell(v.tensor_tensor(r[:, s, :], r[:, s, :], gate[:, s, :], ALU.add), r3_done)
                dve.wait_ge(sq_done, i + 1)
                one = lambda n: ssq[:, n, i:i + 1]
                o.then(v.tensor_scalar(one(0), one(0), 1.0 / D, EPS, ALU.mult, ALU.add))
                rsqrt(v, o, one(1), one(0), one(2))
                if i >= 2:
                    dve.wait_ge(outs[s], 16 * (i // 2))
                o.tell(v.scalar_tensor_tensor(res[:, s, :], r[:, s, :], one(1), gain[:, :], ALU.mult, ALU.mult), res_done)

        @block.tensor
        def _(pe):
            mm = nc.tensor.matmul

            def turn(i):
                s = i % 2
                pe.wait_ge(r2_done, i + 1)
                for b in range(3):
                    if i:
                        pe.wait_ge(t_used, 3 * (i - 1) + b + 1)
                    n = 4 if b < 2 else PK
                    for k in range(n):
                        src = r[:, s, (4 * b + k) * P:(4 * b + k + 1) * P] if b < 2 else p_t[:, s, k * P:(k + 1) * P]
                        last = nc.tensor.transpose(psb[b][:, k * P:(k + 1) * P], src, ident)
                    last.then_inc(t_ready, 1)

            turn(0)
            for i in range(TT):
                s = i % 2
                if i + 1 < TT:
                    turn(i + 1)
                if i == 0:
                    pe.wait_ge(w_in_, 32)
                pe.wait_ge(t_used, 3 * i + 3)
                for b in range(2):
                    cols = slice(b * HALF, (b + 1) * HALF)
                    if i:
                        pe.wait_ge(r3_done, i)
                    for k in range(KC):
                        last = mm(psb[3 + b][:, :], rT[:, s, k, :], w_gate[:, k, cols], start=k == 0, stop=k == KC - 1)
                    last.then_inc(g_ready, 1)
                    for k in range(PK):
                        last = mm(psb[5 + b][:, :], pT[:, s, k, :], w_proj[:, k, cols], start=k == 0, stop=k == PK - 1)
                    last.then_inc(p_ready, 1)
    clear_sems(nc, sems)


def build(nc, I, out):
    ctx = ExitStack()
    with ctx:
        sb = lambda n, s, d=F32: ctx.enter_context(nc.sbuf_tensor(n, s, d))
        dram = lambda n, s, d=F32: nc.dram_tensor("s_" + n, s, d, kind="Internal").ap()
        S = {"u": dram("u", (SSM, STEP, CHUNKS)), "y": dram("y", (SSM, STEP, CHUNKS)), "k": dram("k", (GROUPS, GCH, P)),
             "mix_s": dram("mix_s", (KC, P, SEQ)), "gate_a": dram("gate_a", (KC, P, SEQ)),
             "r1": dram("r1", (SEQ, D)), "h2": dram("h2", (SEQ, D)), "list": dram("list", (LIST, REC)), "items": dram("items", (P,), I32),
             "ys": dram("ys", (SEQ * TOP, D))}
        psb = [ctx.enter_context(nc.psum_tensor(f"bank{i}", [P, HALF], F32)) for i in range(8)]
        ident = sb("ident", [P, P])
        const = {"ident": ident[:, :]}
        items_sb = sb("items_sb", [1, 1], I32)
        bias_all = sb("bias_all", [P, EXPERTS, 3, KC])
        mixer = ExitStack()
        with mixer:
            hT = mixer.enter_context(nc.sbuf_tensor("hT", [P, KC, SEQ], F32))
            y2T = mixer.enter_context(nc.sbuf_tensor("y2T", [P, 4, SEQ], F32))
            norm_and_ssm(nc, I, S, hT, y2T, psb, const)
            attention(nc, I, S, hT, y2T, y2T, psb, const)
            mix_and_route(nc, I, S, y2T, hT, items_sb, bias_all, psb, const)
        experts(nc, I, S, items_sb, bias_all, psb, const)
        combine(nc, I, S, out, psb, const)


_INS = ['x', 'p', 'w_in', 'b_gates', 'lam_re', 'lam_im', 'log_dt', 'b_re', 'b_im', 'c_re', 'c_im', 'd_skip', 'w_glu', 'b_glu',
        'w_ssm_br', 'w_attn_br', 'w_o', 'norm_mix', 'norm_ffn', 'w_router', 'b_router', 'w_gate', 'b_gate', 'w_up', 'b_up',
        'w_down', 'b_down', 'w_ple_gate', 'w_ple_proj', 'norm_final']


def _tables():
    def rope(width):
        inv = (np.float32(10000.0) ** (-np.arange(width // 2, dtype=np.float32) * np.float32(2.0) / np.float32(width))).astype(np.float32)
        ang = np.arange(SEQ, dtype=np.float32)[:, None] * inv[None, :]
        return np.cos(ang).astype(np.float32), np.sin(ang).astype(np.float32)
    (c1, s1), (c2, s2) = rope(HD), rope(ID)
    return {"t_ident": np.eye(P, dtype=np.float32), "t_cos": np.concatenate([c1, c2], 1), "t_sin": np.concatenate([s1, s2], 1),
            "t_tri": np.triu(np.ones((P, P), np.float32), 1)}


def kernel(**inputs):
    import numpy as _np
    import concourse.bacc as _bacc
    from concourse import mybir as _mybir
    from concourse.bass_utils import run_bass_kernel_spmd as _run

    nc = _bacc.Bacc("TRN2", target_bir_lowering=False, num_devices=1)
    arrays = {n: _np.ascontiguousarray(inputs[n]) for n in _INS} | _tables()
    ins = {n: nc.dram_tensor(n, a.shape, _mybir.dt.from_np(a.dtype), kind="ExternalInput").ap() for n, a in arrays.items()}
    out = nc.dram_tensor("out", (1, SEQ, D), _mybir.dt.float32, kind="ExternalOutput").ap()
    build(nc, ins, out)
    r = _run(nc, [arrays], core_ids=[0])
    return r.results[0]["out"]
```

```python
import math
from contextlib import ExitStack

import numpy as np

import concourse.bass as bass
from concourse import mybir

F32 = mybir.dt.float32
F32R = mybir.dt.float32r
BF16 = mybir.dt.bfloat16
U32 = mybir.dt.uint32
I32 = mybir.dt.int32
ALU = mybir.AluOpType
ACT = mybir.ActivationFunctionType
AX = mybir.AxisListType

P = 128
D = 1024
SEQ = 1024
EPS = 1e-6
KC = D // P
TT = SEQ // P
HALF = 512
GROUPS, GCH, STATE = 32, 16, 64
SSM = GROUPS * GCH
PAIRS = GROUPS // 2
STEP = P // GCH
CHUNKS = SEQ // STEP
HEADS, HD = 8, 64
AW = HEADS * HD
IH, ID = 8, 32
TOPK = 256
PLE = 256
EXPERTS, TOP = 32, 4
FF = 1024
SWIGLU_LIMIT = 7.0
C_U, C_Q, C_K, C_V = 0, SSM, SSM + AW, SSM + 2 * AW
C_QI = SSM + 3 * AW
C_KI = C_QI + IH * ID
C_WI = C_KI + ID
C_GS = C_WI + IH
C_GA = C_GS + D
NI = IH * ID + ID + IH
NEG = -1e30
LEAD = -4096
MAGIC = 12582912.0


class Banks:

    def __init__(self, t):
        self.all = t

    def __getitem__(self, i):
        return self.all[:, i * HALF:(i + 1) * HALF]


def own_sem(nc, sems, name):
    sems.append(nc.alloc_semaphore(name))
    return sems[-1]


def clear_sems(nc, sems):
    nc.clear_and_free_semaphores(sems)
    nc.all_engine_barrier()


class Order:

    def __init__(self, eng, sem):
        self.eng, self.sem, self.n, self.said = eng, sem, 0, {}

    def go(self, ins):
        self.n += 1
        return ins.then_inc(self.sem, 1)

    def wait(self):
        self.eng.wait_ge(self.sem, self.n)

    def then(self, ins):
        self.go(ins)
        self.wait()

    def tell(self, ins, sem):
        self.said[sem.name] = self.said.get(sem.name, 0) + 1
        ins.then_inc(sem, 1)
        self.eng.wait_ge(sem, self.said[sem.name])


def norm_and_ssm(nc, I, S, hT, y2T, psb, const):
    ctx, sems = ExitStack(), []
    with ctx:
        sb = lambda n, s, d=F32: ctx.enter_context(nc.sbuf_tensor("a_" + n, s, d))
        sem = lambda n: own_sem(nc, sems, "a_" + n)
        x_all = sb("x_all", [P, TT, D])
        flat = x_all[:, :, :].rearrange("p a b -> p (a b)")
        n_st = PAIRS * CHUNKS
        view = lambda at: flat[:, at * n_st:(at + 1) * n_st].rearrange("p (j c) -> p j c", j=PAIRS)
        st_re, st_im, turned_re, turned_im = (view(i) for i in range(4))
        w_u = sb("w_u", [P, KC, SSM])
        u_grp = sb("u_grp", [P, GROUPS, CHUNKS])
        toep = sb("toep", [P, GROUPS, P])
        m_both = y2T[:, :, :].rearrange("p b t -> p (b t)").rearrange("p (i j n) -> p i j n", i=2, j=PAIRS)
        m_in = [m_both[:, 0], m_both[:, 1]]
        m_out = [sb("m_out_re", [P, PAIRS, STEP + 1, GCH]), sb("m_out_im", [P, PAIRS, STEP + 1, GCH])]
        scratch = sb("scratch", [P, PAIRS * CHUNKS * 4])
        w1 = [scratch[:, i * n_st:(i + 1) * n_st].rearrange("p (j s h) -> p j s h", j=PAIRS, s=STEP) for i in range(2)]
        ph_re, ph_im = (scratch[:, (2 + i) * n_st:(3 + i) * n_st].rearrange("p (j c) -> p j c", j=PAIRS) for i in range(2))
        u_ch = toep[:, :, :].rearrange("p g n -> p (g n)").rearrange("p (b s c) -> p b s c", b=4, s=STEP)
        y_ch = scratch[:, 0:2 * n_st].rearrange("p (b s c) -> p b s c", b=4, s=STEP)
        gel = toep[:, :, :].rearrange("p g n -> p (g n)")
        tmp = sb("tmp", [P, PAIRS * (STEP + 1) * GCH])
        small = sb("small", [P, 40, PAIRS])
        powers = sb("powers", [P, 4, PAIRS, STEP + 1])
        lam = sb("lam", [P, 3, PAIRS])
        b_sb = sb("b_sb", [P, 4, PAIRS, GCH])
        c_nat = sb("c_nat", [P, 2, 4, 2, STATE])
        c_sb = sb("c_sb", [P, 2, PAIRS, GCH])
        d_sb = sb("d_sb", [GCH, GROUPS])
        k_sb = scratch[0:GCH, 0:GROUPS * P].rearrange("p (g n) -> p g n", g=GROUPS)
        gain = sb("gain", [P, KC])
        b_glu = sb("b_glu", [P, 4])
        ssq = sb("ssq", [P, 6, TT])
        ssq_done, rstd_done, h_done, h2_done = sem("ssq"), sem("rstd"), sem("h"), sem("h2")
        x_in, w_in_, par_in = [sem(f"x_in{i}") for i in range(TT)], sem("w_in"), sem("par_in")
        lam_in, b_in, c_in = sem("lam_in"), sem("b_in"), sem("c_in")
        dve_step, act_step = sem("dve_step"), sem("act_step")
        tr_ready, tr_used = sem("tr_ready"), sem("tr_used")
        c_tr, c_used = sem("c_tr"), sem("c_used")
        u_ready, u_used, u_out, u_back = sem("u_ready"), sem("u_used"), sem("u_out"), sem("u_back")
        w1_ready, m_tr, m_used = sem("w1_ready"), sem("m_tr"), sem("m_used")
        mo_ready, k_ready, k_used, k_diag, k_out, t_back = (sem(n) for n in ("mo_ready", "k_ready", "k_used", "k_diag", "k_out", "t_back"))
        toep_zero = sem("toep_zero")
        s_ready, s_turned = sem("s_ready"), sem("s_turned")
        y_ready, y_used = sem("y_ready"), sem("y_used")
        y_out, y_back = ([sem(f"{n}{b}") for b in range(4)] for n in ("y_out", "y_back"))
        sq_done, inner_done, sig_done, gel_done = sem("sq_done"), sem("inner_done"), sem("sig_done"), sem("gel_done")
        glu_w, z_ready, z_sig, y2_done = sem("glu_w"), sem("z_ready"), sem("z_sig"), sem("y2_done")
        y_grp = toep
        block = ctx.enter_context(nc.Block())
        ident = const["ident"]

        lamv = lambda a: a[0].rearrange("(j g) p -> (g p) j", g=2)

        def bank_groups(t, q):
            return t[:, :, :].rearrange("p (j g) n -> p g j n", g=2)[:, q % 2, 4 * (q // 2):4 * (q // 2) + 4, :]

        @block.sync
        def _(sp):
            with nc.allow_non_contiguous_dma(reason="parameters laid out by state, a few KB"):
                sp.dma_start(lam[:, 0, :], lamv(I["lam_re"])).then_inc(lam_in, 16)
                sp.dma_start(lam[:, 1, :], lamv(I["lam_im"])).then_inc(lam_in, 16)
                for g in range(2):
                    sp.dma_start(lam[g * STATE:(g + 1) * STATE, 2, :],
                                  I["log_dt"][0].rearrange("(j g) -> g j", g=2)[g].unsqueeze(0).broadcast_to([STATE, PAIRS])).then_inc(lam_in, 16)
            for i in range(TT):
                sp.dma_start(x_all[:, i, :], I["x"][0, i * P:(i + 1) * P, :]).then_inc(x_in[i], 16)
            sp.dma_start(w_u[:, :, :], I["w_in"][0][:, C_U:C_U + SSM].rearrange("(k p) n -> p k n", p=P)).then_inc(w_in_, 16)
            for b in range(4):
                sp.wait_ge(u_used, 2 * b + 2)
                sp.dma_start(S["u"][b * P:(b + 1) * P, :, :], u_ch[:, b]).then_inc(u_out, 16)
            sp.wait_ge(u_out, 64)
            for s in range(STEP):
                sp.dma_start(u_grp[s * GCH:(s + 1) * GCH, :, :],
                             S["u"][:, s, :].rearrange("(g h) c -> h g c", h=GCH)).then_inc(u_back, 16)
            sp.wait_ge(k_diag, 1)
            sp.dma_start(S["k"].rearrange("g h n -> h g n"), k_sb[:, :, :]).then_inc(k_out, 16)
            sp.wait_ge(k_out, 16)
            sp.wait_ge(toep_zero, 1)
            for s in range(STEP):
                sp.dma_start(toep[s * GCH:(s + 1) * GCH, :, s * GCH:],
                             S["k"].rearrange("g h n -> h g n")[:, :, 0:P - s * GCH]).then_inc(t_back, 16)
            sp.wait_ge(u_ready, 8)
            sp.dma_start(w_u[:, 0:4, :], I["w_glu"][0].rearrange("(k p) n -> p k n", p=P)).then_inc(glu_w, 16)
            for b in range(4):
                sp.wait_ge(y_used, 2 * b + 2)
                for s in range(STEP):
                    sp.dma_start(S["y"][:, s, :].rearrange("(g h) c -> h g c", h=GCH)[:, 8 * b:8 * b + 8, :],
                                 y_grp[s * GCH:(s + 1) * GCH, 8 * b:8 * b + 8, :]).then_inc(y_out[b], 16)

        @block.gpsimd
        def _(pool):
            pool.wait_ge(rstd_done, 2)
            for i in range(TT - 2, TT):
                nc.gpsimd.tensor_scalar(x_all[:, i, :], x_all[:, i, :], ssq[:, 3, i:i + 1], None, ALU.mult).then_inc(h2_done, 1)
            pool.wait_ge(u_out, 64)
            nc.gpsimd.memset(toep[:, :, :], 0.0).then_inc(toep_zero, 1)
            for b in range(5):
                if b < 4:
                    pool.wait_ge(y_out[b], 16 * STEP)
                    pool.dma_start(y_ch[:, b], S["y"][b * P:(b + 1) * P, :, :]).then_inc(y_back[b], 16)
                if b:
                    pool.wait_ge(y_back[b - 1], 16)
                    y = y_ch[:, b - 1].rearrange("p s c -> p (s c)")
                    nc.gpsimd.tensor_tensor(gel[:, (b - 1) * SEQ:b * SEQ], y, y, ALU.mult).then_inc(sq_done, 1)

        @block.scalar
        def _(act):
            o = Order(act, act_step)
            for i in range(TT):
                if i == 3:
                    with nc.allow_non_contiguous_dma(reason="parameters laid out by state, a few KB"):
                        act.dma_start(b_sb[:, 0], I["b_re"][0].rearrange("(j g) p h -> (g p) j h", g=2)).then_inc(b_in, 16)
                        act.dma_start(b_sb[:, 1], I["b_im"][0].rearrange("(j g) p h -> (g p) j h", g=2)).then_inc(b_in, 16)
                        act.dma_start(ident, I["t_ident"]).then_inc(c_in, 16)
                        for n, name in enumerate(("c_re", "c_im")):
                            for twice in range(2):
                                act.dma_start(c_nat[:, n, :, twice, :], I[name][0].rearrange("(b g) h p -> (g h) b p", b=4)).then_inc(c_in, 16)
                        act.dma_start(d_sb[:, :], I["d_skip"][0].rearrange("g h -> h g")).then_inc(par_in, 16)
                        act.dma_start(gain[:, :], I["norm_mix"][0].rearrange("(k p) -> p k", p=P)).then_inc(par_in, 16)
                        act.dma_start(b_glu[:, :], I["b_glu"][0].rearrange("(k p) -> p k", p=P)).then_inc(par_in, 16)
                act.wait_ge(x_in[i], 16)
                nc.scalar.activation(u_grp[:, 0:D // CHUNKS, :].rearrange("p g c -> p (g c)"), x_all[:, i, :], ACT.Square, accum_out=ssq[:, 0, i:i + 1]).then_inc(ssq_done, 1)
                act.wait_ge(ssq_done, i + 1)
            act.wait_ge(rstd_done, 1)
            o.then(nc.scalar.activation(ssq[:, 2, :], ssq[:, 1, :], ACT.Sqrt))
            nc.scalar.activation(ssq[:, 5, :], ssq[:, 2, :], ACT.Copy).then_inc(ssq_done, 1)
            act.wait_ge(rstd_done, 2)
            for i in range(TT - 2):
                nc.scalar.activation(x_all[:, i, :], x_all[:, i, :], ACT.Copy, scale=ssq[:, 3, i:i + 1]).then_inc(h_done, 1)
            act.wait_ge(par_in, 16 * 3)
            for n in range(2 * KC):
                k, t = n % KC, n // KC
                act.wait_ge(tr_ready, n + 1)
                nc.scalar.activation(hT[:, k, t * HALF:(t + 1) * HALF], psb[n % 8][:, :], ACT.Copy, scale=gain[:, k:k + 1]).then_inc(tr_used, 1)
            for b in range(4):
                for t in range(2):
                    n = 2 * b + t
                    act.wait_ge(u_ready, n + 1)
                    nc.scalar.copy(u_ch[:, b].rearrange("p s c -> p c s")[:, t * 64:(t + 1) * 64, :],
                                   psb[n % 8][:, :].rearrange("p (c s) -> p c s", s=STEP)).then_inc(u_used, 1)
            for n in range(8):
                act.wait_ge(m_tr, n + 1)
                nc.scalar.copy(m_in[n // 4][:, 4 * (n % 4):4 * (n % 4) + 4, :], psb[n][:, :].rearrange("p (j n) -> p j n", j=4)).then_inc(m_used, 1)
            for q in range(8):
                act.wait_ge(k_ready, q + 1)
                nc.scalar.copy(bank_groups(k_sb, q), psb[q][0:GCH, :].rearrange("p (g n) -> p g n", g=4)).then_inc(k_used, 1)
            for q in range(8):
                act.wait_ge(y_ready, q + 1)
                nc.scalar.copy(bank_groups(y_grp, q), psb[q][:, :].rearrange("p (g n) -> p g n", g=4)).then_inc(y_used, 1)
            for b in range(4):
                act.wait_ge(inner_done, b + 1)
                nc.scalar.activation(gel[:, b * SEQ:(b + 1) * SEQ], gel[:, b * SEQ:(b + 1) * SEQ], ACT.Sigmoid,
                                     scale=2.0 * math.sqrt(2.0 / math.pi)).then_inc(sig_done, 1)
            for n in range(8):
                act.wait_ge(z_ready, n + 1)
                b, t = n // 2, n % 2
                nc.scalar.activation(flat[:, 4 * SEQ + n * HALF:4 * SEQ + (n + 1) * HALF], psb[n][:, :], ACT.Sigmoid,
                                     bias=b_glu[:, b:b + 1]).then_inc(z_sig, 1)

        @block.vector
        def _(dve):
            v = nc.vector
            o = Order(dve, dve_step)
            sm = lambda i: small[:, i, :]
            mul = lambda out, a, b: o.then(v.tensor_tensor(out, a, b, ALU.mult))
            add = lambda out, a, b: o.then(v.tensor_tensor(out, a, b, ALU.add))
            sub = lambda out, a, b: o.then(v.tensor_tensor(out, a, b, ALU.subtract))

            def wide(a, like):
                for _ in range(len(like.shape) - len(a.shape)):
                    a = a.unsqueeze(len(a.shape))
                return a.broadcast_to(list(like.shape))

            def cmul(out, a, b, t1, t2):
                o.go(v.tensor_tensor(t1, a[0], b[0], ALU.mult))
                o.go(v.tensor_tensor(t2, a[1], b[1], ALU.mult))
                o.then(v.tensor_tensor(out[1], a[0], b[1], ALU.mult))
                o.then(v.tensor_tensor(out[0], t1, t2, ALU.subtract))
                o.then(v.tensor_tensor(t1, a[1], b[0], ALU.mult))
                o.then(v.tensor_tensor(out[1], out[1], t1, ALU.add))

            def round_to_int(out, a):
                o.then(v.tensor_scalar(out, a, MAGIC, None, ALU.add))
                o.then(v.tensor_scalar(out, out, -MAGIC, None, ALU.add))

            def horner(out, z, cs):
                o.then(v.tensor_scalar(out, z, cs[0], None, ALU.mult))
                for c in cs[1:]:
                    o.then(v.scalar_tensor_tensor(out, out, c, z, ALU.add, ALU.mult))

            def exp(out, a, t1, t2, t3):
                o.then(v.tensor_scalar(t1, a, -87.0, 88.0, ALU.max, ALU.min))
                o.then(v.tensor_scalar(t2, t1, 1.0 / math.log(2.0), None, ALU.mult))
                round_to_int(t2, t2)
                o.then(v.scalar_tensor_tensor(t1, t2, -0.693359375, t1, ALU.mult, ALU.add))
                o.then(v.scalar_tensor_tensor(t1, t2, 2.12194440e-4, t1, ALU.mult, ALU.add))
                horner(out, t1, [1.0 / math.factorial(n) for n in range(8, 0, -1)])
                o.then(v.tensor_scalar(out, out, 1.0, None, ALU.add))
                o.then(v.tensor_scalar(t3.bitcast(I32), t2, 127.0, 8388608.0, ALU.add, ALU.mult))
                mul(out, out, t3)

            dve.wait_ge(lam_in, 64)
            DT, ER, EI, E, T1, T2, T3, SN, CS, AR, AI, FR, FI, DEN, E8, PR, PI = range(17)
            exp(sm(DT), lam[:, 2, :], sm(T1), sm(T2), sm(T3))
            mul(sm(ER), lam[:, 0, :], sm(DT))
            mul(sm(EI), lam[:, 1, :], sm(DT))
            exp(sm(E), sm(ER), sm(T1), sm(T2), sm(T3))
            o.then(v.tensor_scalar(sm(T2), sm(EI), 1.0 / (2.0 * math.pi), None, ALU.mult))
            round_to_int(sm(T2), sm(T2))
            for part in (-6.28125, -1.9350051879882812e-3, -3.0199159819e-7):
                o.then(v.scalar_tensor_tensor(sm(EI), sm(T2), part, sm(EI), ALU.mult, ALU.add))
            o.then(v.tensor_scalar(sm(EI), sm(EI), 0.5, None, ALU.mult))
            mul(sm(T1), sm(EI), sm(EI))
            horner(sm(T2), sm(T1), [(-1.0) ** n / math.factorial(2 * n + 1) for n in range(7, 0, -1)])
            o.then(v.scalar_tensor_tensor(sm(T2), sm(T2), 1.0, sm(EI), ALU.add, ALU.mult))
            horner(sm(T3), sm(T1), [(-1.0) ** n / math.factorial(2 * n) for n in range(8, 0, -1)])
            o.then(v.tensor_scalar(sm(T3), sm(T3), 1.0, None, ALU.add))
            mul(sm(SN), sm(T2), sm(T3))
            o.then(v.tensor_scalar(sm(SN), sm(SN), 2.0, None, ALU.mult))
            mul(sm(CS), sm(T2), sm(T2))
            o.then(v.tensor_scalar(sm(CS), sm(CS), -2.0, 1.0, ALU.mult, ALU.add))
            mul(sm(AR), sm(E), sm(CS))
            mul(sm(AI), sm(E), sm(SN))
            dve.wait_ge(ssq_done, TT)
            o.then(v.tensor_scalar(ssq[:, 0, :], ssq[:, 0, :], 1.0 / D, EPS, ALU.mult, ALU.add))
            o.tell(v.reciprocal(ssq[:, 1, :], ssq[:, 0, :]), rstd_done)
            dve.wait_ge(ssq_done, TT + 1)
            mul(ssq[:, 4, :], ssq[:, 5, :], ssq[:, 5, :])
            mul(ssq[:, 4, :], ssq[:, 4, :], ssq[:, 0, :])
            o.then(v.tensor_scalar(ssq[:, 4, :], ssq[:, 4, :], -0.5, 1.5, ALU.mult, ALU.add))
            o.tell(v.tensor_tensor(ssq[:, 3, :], ssq[:, 5, :], ssq[:, 4, :], ALU.mult), rstd_done)

            dve.wait_ge(c_tr, 1)
            for n in range(8):
                i, b = n // 4, n % 4
                src = psb[6 + i][:, b * P:(b + 1) * P].rearrange("p (j g h) -> p g j h", g=2, h=GCH)
                for g in range(2):
                    v.tensor_copy(c_sb[g * STATE:(g + 1) * STATE, i, 4 * b:4 * b + 4, :], src[g * STATE:(g + 1) * STATE, g]).then_inc(c_used, 1)
            dve.wait_ge(c_used, 16)
            mul(sm(DEN), lam[:, 0, :], lam[:, 0, :])
            mul(sm(T1), lam[:, 1, :], lam[:, 1, :])
            add(sm(DEN), sm(DEN), sm(T1))
            o.then(v.reciprocal(sm(DEN), sm(DEN)))
            o.then(v.tensor_scalar(sm(T1), sm(AR), -1.0, None, ALU.add))
            mul(sm(FR), sm(T1), lam[:, 0, :])
            mul(sm(T2), sm(AI), lam[:, 1, :])
            add(sm(FR), sm(FR), sm(T2))
            mul(sm(FR), sm(FR), sm(DEN))
            mul(sm(FI), sm(AI), lam[:, 0, :])
            mul(sm(T2), sm(T1), lam[:, 1, :])
            sub(sm(FI), sm(FI), sm(T2))
            mul(sm(FI), sm(FI), sm(DEN))
            dve.wait_ge(b_in, 32)
            b_bar = (b_sb[:, 2], b_sb[:, 3])
            half = PAIRS * CHUNKS // 8
            tv = lambda n, at=0: tmp[:, at * half:at * half + n]
            tb = [tv(PAIRS * GCH, i).rearrange("p (j h) -> p j h", j=PAIRS) for i in range(2)]
            cmul(b_bar, (wide(sm(FR), b_bar[0]), wide(sm(FI), b_bar[0])), (b_sb[:, 0], b_sb[:, 1]), *tb)
            pw = [powers[:, 0], powers[:, 1]]
            rev = [powers[:, 2], powers[:, 3]]
            o.go(v.memset(pw[0][:, :, 0], 1.0))
            o.then(v.memset(pw[1][:, :, 0], 0.0))
            for n in range(STEP):
                cmul((pw[0][:, :, n + 1], pw[1][:, :, n + 1]), (pw[0][:, :, n], pw[1][:, :, n]), (sm(AR), sm(AI)), sm(T1), sm(T2))
            for n in range(STEP):
                for i in range(2):
                    o.go(v.tensor_copy(rev[i][:, :, n], pw[i][:, :, STEP - 1 - n]))
            o.wait()
            shape = [P, PAIRS, STEP, GCH]
            rw = [r[:, :, 0:STEP].unsqueeze(3).broadcast_to(shape) for r in rev]
            bw = [b.unsqueeze(2).broadcast_to(shape) for b in b_bar]
            t4 = tmp[:, 0:n_st].rearrange("p (j s h) -> p j s h", j=PAIRS, s=STEP)
            mul(w1[0], rw[0], bw[0])
            mul(t4, rw[1], bw[1])
            sub(w1[0], w1[0], t4)
            mul(w1[1], rw[0], bw[1])
            mul(t4, rw[1], bw[0])
            o.tell(v.tensor_tensor(w1[1], w1[1], t4, ALU.add), w1_ready)
            shape = [P, PAIRS, STEP + 1, GCH]
            pb = [x.unsqueeze(3).broadcast_to(shape) for x in pw]
            cb = [c_sb[:, i].unsqueeze(2).broadcast_to(shape) for i in range(2)]
            t4 = tmp[:, :].rearrange("p (j s h) -> p j s h", j=PAIRS, s=STEP + 1)
            mul(m_out[0][:, :, :, :], pb[0], cb[0])
            mul(t4, pb[1], cb[1])
            sub(m_out[0][:, :, :, :], m_out[0][:, :, :, :], t4)
            mul(m_out[1][:, :, :, :], pb[0], cb[1])
            mul(t4, pb[1], cb[0])
            o.then(v.tensor_tensor(m_out[1][:, :, :, :], m_out[1][:, :, :, :], t4, ALU.add))
            o.tell(v.tensor_scalar(m_out[1][:, :, :, :].rearrange("p a b c -> p (a b c)"),
                                   m_out[1][:, :, :, :].rearrange("p a b c -> p (a b c)"), -1.0, None, ALU.mult), mo_ready)
            cur = [(sm(CS), sm(SN)), (sm(17), sm(18)), (sm(19), sm(20)), (sm(PR), sm(PI))]
            for n in range(3):
                cmul(cur[n + 1], cur[n], cur[n], sm(T1), sm(T2))
            mul(sm(E8), sm(E), sm(E))
            mul(sm(T1), sm(E8), sm(E8))
            mul(sm(E8), sm(T1), sm(T1))
            o.go(v.memset(ph_re[:, :, 0], 1.0))
            o.then(v.memset(ph_im[:, :, 0], 0.0))
            a, b = (sm(PR), sm(PI)), (sm(21), sm(22))
            n = 1
            while n < CHUNKS:
                new = (ph_re[:, :, n:2 * n], ph_im[:, :, n:2 * n])
                old = (ph_re[:, :, 0:n], ph_im[:, :, 0:n])
                sc = [tmp[:, i * 1024:i * 1024 + PAIRS * n].rearrange("p (j c) -> p j c", j=PAIRS) for i in range(2)]
                cmul(new, (wide(a[0], new[0]), wide(a[1], new[0])), old, *sc)
                cmul(b, a, a, sm(T1), sm(T2))
                a, b = b, a
                n *= 2
            dve.wait_ge(par_in, 16 * 3)
            dve.wait_ge(k_used, 8)
            shape = [GCH, GROUPS, GCH]
            t3 = tmp[0:GCH, 0:GROUPS * GCH].rearrange("p (g h) -> p g h", g=GROUPS)
            mul(t3, d_sb[:, :].unsqueeze(2).broadcast_to(shape), ident[0:GCH, 0:GCH].unsqueeze(1).broadcast_to(shape))
            o.tell(v.tensor_tensor(k_sb[:, :, 0:GCH], k_sb[:, :, 0:GCH], t3, ALU.add), k_diag)
            for q in range(4):
                dve.wait_ge(s_ready, 2 * q + 2)
                js = slice(4 * q, 4 * q + 4)
                s_in = [psb[2 * q + i][:, :].rearrange("p (j c) -> p j c", j=4) for i in range(2)]
                tq = tmp[:, 0:HALF].rearrange("p (j c) -> p j c", j=4)
                mul(turned_re[:, js], s_in[0], ph_re[:, js])
                mul(tq, s_in[1], ph_im[:, js])
                add(turned_re[:, js], turned_re[:, js], tq)
                mul(turned_im[:, js], s_in[1], ph_re[:, js])
                mul(tq, s_in[0], ph_im[:, js])
                sub(turned_im[:, js], turned_im[:, js], tq)
                for j in range(4 * q, 4 * q + 4):
                    for t in (turned_re, turned_im):
                        o.go(v.tensor_tensor_scan(t[:, j, :], small[:, E8, j:j + 1].broadcast_to([P, CHUNKS]), t[:, j, :], 0.0, ALU.mult, ALU.add))
                o.wait()
                last = CHUNKS - 1
                t3 = tmp[:, 0:4 * last].rearrange("p (j c) -> p j c", j=4)
                cut = lambda t: t[:, js, 0:last]
                o.go(v.memset(st_re[:, js, 0], 0.0))
                o.go(v.memset(st_im[:, js, 0], 0.0))
                mul(st_re[:, js, 1:], cut(turned_re), cut(ph_re))
                mul(t3, cut(turned_im), cut(ph_im))
                sub(st_re[:, js, 1:], st_re[:, js, 1:], t3)
                mul(st_im[:, js, 1:], cut(turned_re), cut(ph_im))
                mul(t3, cut(turned_im), cut(ph_re))
                o.tell(v.tensor_tensor(st_im[:, js, 1:], st_im[:, js, 1:], t3, ALU.add), s_turned)
            for b in range(5):
                if b < 4:
                    dve.wait_ge(sq_done, b + 1)
                    f = gel[:, b * SEQ:(b + 1) * SEQ]
                    o.then(v.tensor_scalar(f, f, 0.044715, 1.0, ALU.mult, ALU.add))
                    o.tell(v.tensor_tensor(f, f, y_ch[:, b].rearrange("p s c -> p (s c)"), ALU.mult), inner_done)
                if b:
                    dve.wait_ge(sig_done, b)
                    f = gel[:, (b - 1) * SEQ:b * SEQ]
                    o.tell(v.tensor_tensor(f, f, y_ch[:, b - 1].rearrange("p s c -> p (s c)"), ALU.mult), gel_done)
            for n in range(8):
                dve.wait_ge(z_sig, n + 1)
                b, t = n // 2, n % 2
                to = y2T[:, b, :].rearrange("p (c s) -> p s c", s=STEP)[:, 4 * t:4 * t + 4, :]
                cs = lambda x: x.rearrange("p (s c) -> p s c", s=4)
                o.tell(v.tensor_tensor(to, cs(gel[:, b * SEQ + t * HALF:b * SEQ + (t + 1) * HALF]),
                                       cs(flat[:, 4 * SEQ + n * HALF:4 * SEQ + (n + 1) * HALF]), ALU.mult), y2_done)

        @block.tensor
        def _(pe):
            mm = nc.tensor.matmul
            pe.wait_ge(c_in, 16 * 5)
            for n in range(8):
                i, b = n // 4, n % 4
                last = nc.tensor.transpose(psb[6 + i][:, b * P:(b + 1) * P], c_nat[:, i, b].rearrange("p a b -> p (a b)"), ident)
            last.then_inc(c_tr, 1)
            for n in range(2 * KC):
                k, t = n % KC, n // KC
                if k == 0:
                    pe.wait_ge(h_done, 4 if t == 0 else TT - 2)
                    if t:
                        pe.wait_ge(h2_done, 2)
                if n == 6:
                    pe.wait_ge(c_used, 16)
                if n >= 8:
                    pe.wait_ge(tr_used, n - 7)
                for i in range(4):
                    last = nc.tensor.transpose(psb[n % 8][:, i * P:(i + 1) * P], x_all[:, 4 * t + i, k * P:(k + 1) * P], ident)
                last.then_inc(tr_ready, 1)
            pe.wait_ge(w_in_, 16)
            pe.wait_ge(tr_used, 2 * KC)
            for b in range(4):
                for t in range(2):
                    for k in range(KC):
                        last = mm(psb[2 * b + t][:, :], w_u[:, k, b * P:(b + 1) * P], hT[:, k, t * HALF:(t + 1) * HALF], start=k == 0, stop=k == KC - 1)
                    last.then_inc(u_ready, 1)
            pe.wait_ge(u_used, 8)
            pe.wait_ge(mo_ready, 1)
            for n in range(8):
                for q in range(4):
                    last = nc.tensor.transpose(psb[n][:, q * P:(q + 1) * P], w1[n // 4][:, 4 * (n % 4) + q].rearrange("p s h -> p (s h)"), ident)
                last.then_inc(m_tr, 1)
            for q in range(8):
                pe.wait_ge(m_used, q + 1)
                for gg in range(4):
                    j, at = 4 * (q // 2) + gg, (q % 2) * STATE
                    g = 2 * j + q % 2
                    for i in range(2):
                        last = mm(psb[q][0:GCH, gg * P:(gg + 1) * P], b_sb[at:at + STATE, 2 + i, j, :],
                                  m_out[i][at:at + STATE, j, 0:STEP, :].rearrange("p s h -> p (s h)"), start=i == 0, stop=i == 1)
                last.then_inc(k_ready, 1)
            pe.wait_ge(u_back, 16 * STEP)
            for q in range(4):
                for i in range(2):
                    pe.wait_ge(k_used, 2 * q + i + 1)
                    for jj in range(4):
                        j = 4 * q + jj
                        for g in range(2):
                            last = mm(psb[2 * q + i][g * STATE:(g + 1) * STATE, jj * P:(jj + 1) * P],
                                      m_in[i][:, j, g * STATE:(g + 1) * STATE], u_grp[:, 2 * j + g, :], start=True, stop=True)
                    last.then_inc(s_ready, 1)
            pe.wait_ge(t_back, 16 * STEP)
            for q in range(8):
                pe.wait_ge(s_turned, q // 2 + 1)
                for gg in range(4):
                    j, at = 4 * (q // 2) + gg, (q % 2) * STATE
                    g = 2 * j + q % 2
                    out = psb[q][:, gg * P:(gg + 1) * P]
                    mm(out, toep[:, g, :], u_grp[:, g, :], start=True, stop=False)
                    for i, st in enumerate((st_re, st_im)):
                        last = mm(out, m_out[i][at:at + STATE, j, 1:STEP + 1, :].rearrange("p s h -> p (s h)"),
                                  st[at:at + STATE, j, :], start=False, stop=i == 1)
                last.then_inc(y_ready, 1)
            pe.wait_ge(glu_w, 16)
            for k in range(4):
                pe.wait_ge(gel_done, k + 1)
                for n in range(8):
                    b, t = n // 2, n % 2
                    if k == 0:
                        pe.wait_ge(y_used, n + 1)
                    last = mm(psb[n][:, :], w_u[:, k, b * P:(b + 1) * P], gel[:, k * SEQ + t * HALF:k * SEQ + (t + 1) * HALF], start=k == 0, stop=k == 3)
                    if k == 3:
                        last.then_inc(z_ready, 1)
    clear_sems(nc, sems)


def attention(nc, I, S, hT, y2T, oT, w_br, psb, const):
    ctx, sems = ExitStack(), []
    with ctx:
        sb = lambda n, s, d=F32: ctx.enter_context(nc.sbuf_tensor("b_" + n, s, d))
        sem = lambda n: own_sem(nc, sems, "b_" + n)
        wring = sb("wring", [P, 2, KC * HALF])
        wv = lambda s: wring[:, s, :].rearrange("p (k n) -> p k n", k=KC)
        att = wring[:, :, :].rearrange("p a b -> p (a b)")
        with nc.sbuf_tensor("b_qiT", [P, IH, SEQ], F32R) as qiT:
            pass
        qT, kT = sb("qT", [P, 4, SEQ]), sb("kT", [P, 4, SEQ])
        VP = 3 * HD
        v_sb = sb("v", [P, TT, HEADS // 2, VP])
        kiT = sb("kiT", [P, SEQ], F32R)
        wi = sb("wi", [P, TT, IH])
        off = [P * i * (i + 1) // 2 for i in range(TT + 1)]
        score = sb("score", [P, off[TT]])
        buf = sb("buf", [P, 4, HALF])
        nat = sb("nat", [P, 2, (IH + 1) * P])
        raw = sb("raw", [P, 2, AW])
        turn = sb("turn", [P, 2, AW // 2])
        top8 = sb("top8", [P, 8])
        stats = sb("stats", [P, 8, 2])
        b_gates = sb("b_gates", [P, 16])
        cos, sin = (sb(n, [P, TT, (HD + ID) // 2]) for n in ("cos", "sin"))
        ident = const["ident"]

        w_in_ = [sem(f"w_in{s}") for s in range(3)]
        bias_in, rope_in = sem("bias_in"), sem("rope_in")
        dve_step, pool_done = sem("dve_step"), sem("pool_done")
        i_ready, i_rope, it_ready, it_used = (sem(n) for n in ("i_ready", "i_rope", "it_ready", "it_used"))
        proj_ready, raw_done, rope_step, rope_done, tr_ready, tr_used, v_ready, v_used, ones_done = (
            sem(n) for n in ("proj_ready", "raw_done", "rope_step", "rope_done", "tr_ready", "tr_used", "v_ready", "v_used", "ones_done"))
        dots_ready, relu_done, relu_used = sem("dots_ready"), sem("relu_done"), sem("relu_used")
        gate_ready, gate_used, br_used = sem("gate_ready"), sem("gate_used"), sem("br_used")
        gate_out = [sem(f"gate_out{s}") for s in range(2)]
        block = ctx.enter_context(nc.Block())

        N_QK = 2 * TT
        blocks = [(C_QI, NI), (C_V, AW), (C_Q, AW), (C_K, AW), (C_GS, HALF), (C_GS + HALF, HALF), (C_GA, HALF), (C_GA + HALF, HALF)]
        order = list(range(TT - 1, -1, -1))
        dots = [(i, kb, h) for i in order if (i + 1) * P > TOPK for kb in range((i + 4) // 4) for h in range(IH)]
        passes = [Pass(nc, sems, psb, att, [i for i in order if i >= 4], 2), Pass(nc, sems, psb, att, [i for i in order if i < 4], 4)]

        @block.sync
        def _(sp):
            w3 = I["w_in"][0].rearrange("(k p) n -> p k n", p=P)
            for n, (c, width) in enumerate(blocks):
                if n == 2:
                    sp.wait_ge(i_ready, TT)
                if n == 3:
                    sp.wait_ge(v_ready, TT)
                if 4 <= n <= 5:
                    sp.wait_ge(proj_ready, TT * (n - 3))
                if n >= 6:
                    sp.wait_ge(gate_ready, 8 * (n - 5))
                sp.dma_start(wv(n % 2)[:, :, 0:width], w3[:, :, c:c + width]).then_inc(w_in_[n % 2], 16)
                if n == 1:
                    sp.dma_start(w_br[:, :, :], I["w_ssm_br"][0].rearrange("(k p) n -> p k n", p=P)).then_inc(w_in_[2], 16)
                    with nc.allow_non_contiguous_dma(reason="8 KB of biases"):
                        sp.dma_start(b_gates[:, :], I["b_gates"][0].rearrange("(b p) -> p b", p=P)).then_inc(bias_in, 16)
                if n >= 5:
                    for m in range(8 * (n - 5), 8 * (n - 4)) if n < 7 else range(8 * (n - 5), 32):
                        to = S["mix_s"] if m < 16 else S["gate_a"]
                        b, t = (m % 16) // 2, m % 2
                        if m < 16:
                            sp.wait_ge(pool_done, m + 1)
                        else:
                            sp.wait_ge(gate_used, m + 1)
                        sp.dma_start(to[b, :, t * HALF:(t + 1) * HALF], buf[:, m % 2, :]).then_inc(gate_out[m % 2], 16)
            sp.dma_start(w_br[:, :, :], I["w_attn_br"][0].rearrange("(k p) n -> p k n", p=P)).then_inc(w_in_[2], 16)
            for s in range(2):
                sp.wait_ge(gate_out[s], 16 * 16)
            sp.wait_ge(w_in_[2], 32)

        @block.gpsimd
        def _(pool):
            g = nc.gpsimd
            g.memset(v_sb[:, :, :, HD:2 * HD], 1.0).then_inc(ones_done, 1)
            pool.wait_ge(rope_in, 32)
            for n in range(N_QK):
                t = n % TT
                z = raw[:, n % 2, :].rearrange("p (h two c) -> p h two c", h=HEADS, two=2)
                out = nat[:, n % 2, 0:AW].rearrange("p (h two c) -> p h two c", h=HEADS, two=2)
                cs, sn = (c[:, t, 0:HD // 2].unsqueeze(1).broadcast_to([P, HEADS, HD // 2]) for c in (cos, sin))
                tm = [turn[:, s, :].rearrange("p (h c) -> p h c", h=HEADS) for s in range(2)]
                pool.wait_ge(raw_done, n + 1)
                if n >= 2:
                    pool.wait_ge(tr_ready, n - 1)
                else:
                    pool.wait_ge(it_ready, TT)
                if n:
                    pool.wait_ge(rope_done, 2 * n)
                g.tensor_tensor(out[:, :, 0], z[:, :, 0], cs, ALU.mult).then_inc(rope_step, 1)
                g.tensor_tensor(tm[0], z[:, :, 1], sn, ALU.mult).then_inc(rope_step, 1)
                g.tensor_tensor(out[:, :, 1], z[:, :, 1], cs, ALU.mult).then_inc(rope_step, 1)
                g.tensor_tensor(tm[1], z[:, :, 0], sn, ALU.mult).then_inc(rope_step, 1)
                pool.wait_ge(rope_step, 4 * (n + 1))
                g.tensor_tensor(out[:, :, 0], out[:, :, 0], tm[0], ALU.subtract).then_inc(rope_done, 1)
                g.tensor_tensor(out[:, :, 1], out[:, :, 1], tm[1], ALU.add).then_inc(rope_done, 1)
            for m in range(16):
                pool.wait_ge(br_used, m + 1)
                g.tensor_tensor(buf[:, m % 2, :], buf[:, m % 2, :], buf[:, 2 + m % 2, :], ALU.mult).then_inc(pool_done, 1)

        @block.scalar
        def _(act):
            for t, name in ((cos, "t_cos"), (sin, "t_sin")):
                act.dma_start(t[:, :, :], I[name].rearrange("(t p) n -> p t n", p=P)).then_inc(rope_in, 16)
            for t in range(TT):
                cols = slice(t * P, (t + 1) * P)
                at = 2 + 3 * (t % 2)
                act.wait_ge(it_ready, t + 1)
                for g in range(2):
                    nc.scalar.copy(qiT[:, 4 * g:4 * g + 4, cols], psb[at + g][:, :].rearrange("p (b n) -> p b n", b=4))
                nc.scalar.copy(kiT[:, cols], psb[at + 2][:, 0:P]).then_inc(it_used, 1)
            act.wait_ge(i_rope, TT)
            for m, (i, kb, h) in enumerate(dots):
                w = min(HALF, (i + 1) * P - kb * HALF)
                act.wait_ge(dots_ready, m + 1)
                if m >= 4:
                    act.wait_ge(relu_used, m - 3)
                nc.scalar.activation(buf[:, m % 4, 0:w], psb[m % 4][:, 0:w], ACT.Relu).then_inc(relu_done, 1)
                t = (m - KC - 2) // KC
                if (m - KC - 2) % KC == 0 and 0 <= t < TT:
                    act.wait_ge(v_ready, t + 1)
                    src = psb[4 + t % 4][:, :].rearrange("p (j two d) -> p j two d", two=2, d=HD)
                    nc.scalar.copy(v_sb[:, t, :, 0:HD], src[:, :, 0])
                    nc.scalar.copy(v_sb[:, t, :, 2 * HD:VP], src[:, :, 1]).then_inc(v_used, 1)
            for n in range(N_QK + 2):
                if n < N_QK:
                    act.wait_ge(proj_ready, n + 1)
                    if n >= 2:
                        act.wait_ge(rope_done, 2 * (n - 1))
                    nc.scalar.copy(raw[:, n % 2, :], psb[n % 4][:, :]).then_inc(raw_done, 1)
                if n >= 2:
                    u = n - 2
                    t = u % TT
                    act.wait_ge(tr_ready, u + 1)
                    nc.scalar.copy((qT if u < TT else kT)[:, :, t * P:(t + 1) * P],
                                   psb[4 + u % 4][:, :].rearrange("p (b n) -> p b n", b=4)).then_inc(tr_used, 1)
            act.wait_ge(relu_used, len(dots))
            act.wait_ge(bias_in, 16)
            for m in range(32):
                b, t = (m % 16) // 2, m % 2
                act.wait_ge(gate_ready, m + 1)
                if m >= 2:
                    act.wait_ge(gate_out[m % 2], 16 * (m // 2))
                nc.scalar.activation(buf[:, m % 2, :], psb[2 + m % 2][:, :], ACT.Sigmoid,
                                     bias=b_gates[:, m // 2:m // 2 + 1]).then_inc(gate_used, 1)
                if m < 16:
                    act.wait_ge(gate_used, m + 1)
                    nc.scalar.copy(buf[:, 2 + m % 2, :], psb[4 + m % 2][:, :]).then_inc(br_used, 1)
            for a in passes:
                for n in range(a.n + a.depth):
                    if n < a.n:
                        nk = (a.heads[n][0] + 1) * P
                        act.wait_ge(a.m_done, n + 1)
                        if n >= a.depth:
                            act.wait_ge(a.pt_ready, n - a.depth + 1)
                        nc.scalar.activation(a.probs(n)[:, 0:nk], a.masked(n)[:, 0:nk], ACT.Exp, bias=stats[:, n % 8, 1:2],
                                             scale=HD ** -0.5).then_inc(a.e_done, 1)
                    if n >= a.depth:
                        m = n - a.depth
                        w = min(HALF, (a.heads[m][0] + 1) * P)
                        act.wait_ge(a.pt_ready, m + 1)
                        if m >= 2:
                            act.wait_ge(a.pv_ready, m - 1)
                        nc.scalar.copy(a.probsT(m)[:, 0:w], a.turned(m)[0][:, 0:w]).then_inc(a.pt_act, 1)

        @block.vector
        def _(dve):
            v = nc.vector
            o = Order(dve, dve_step)
            dve.wait_ge(rope_in, 32)
            nh, half = IH + 1, ID // 2
            for t in range(TT):
                dve.wait_ge(i_ready, t + 1)
                if t >= 2:
                    dve.wait_ge(it_ready, t - 1)
                z = psb[t % 2][:, 0:nh * ID].rearrange("p (h two c) -> p h two c", h=nh, two=2)
                rot = raw[:, t % 2, 0:nh * ID]
                out = rot.rearrange("p (h two c) -> p h two c", h=nh, two=2)
                cs, sn = (c[:, t, HD // 2:HD // 2 + half].unsqueeze(1).broadcast_to([P, nh, half]) for c in (cos, sin))
                tm = [buf[:, s, 0:nh * half].rearrange("p (h c) -> p h c", h=nh) for s in range(4)]
                for s, (a, b) in enumerate(((0, cs), (1, sn), (1, cs), (0, sn))):
                    o.go(v.tensor_tensor(tm[s], z[:, :, a], b, ALU.mult))
                o.then(v.tensor_scalar(wi[:, t, :], psb[t % 2][:, NI - IH:NI], float(IH * ID) ** -0.5, None, ALU.mult))
                o.go(v.tensor_tensor(out[:, :, 0], tm[0], tm[1], ALU.subtract))
                o.then(v.tensor_tensor(out[:, :, 1], tm[2], tm[3], ALU.add))
                parts = nat[:, t % 2, :].rearrange("p (h a b c) -> p h a b c", h=nh, a=2, b=2)
                wide = lambda h0, h1: rot[:, h0 * ID:h1 * ID].rearrange("p (h c) -> p h c", c=ID).unsqueeze(2).broadcast_to([P, h1 - h0, 2, ID])
                split = ((0, IH, parts[:, 0:IH, 0], parts[:, 0:IH, 1]), (IH, nh, parts[:, IH:nh, :, 0], parts[:, IH:nh, :, 1]))
                for h0, h1, lead, _ in split:
                    o.go(v.tensor_scalar(lead.bitcast(I32), wide(h0, h1).bitcast(I32), LEAD, None, ALU.bitwise_and))
                o.wait()
                for h0, h1, lead, rest in split:
                    last = v.tensor_tensor(rest, wide(h0, h1), lead, ALU.subtract)
                    if h0 == 0:
                        o.go(last)
                    else:
                        o.tell(last, i_rope)
                o.wait()
            for m, (i, kb, h) in enumerate(dots):
                w = min(HALF, (i + 1) * P - kb * HALF)
                sc = score[:, off[i] + kb * HALF:off[i] + kb * HALF + w]
                dve.wait_ge(relu_done, m + 1)
                if h == 0:
                    o.tell(v.tensor_scalar(sc, buf[:, m % 4, 0:w], wi[:, i, h:h + 1], None, ALU.mult), relu_used)
                else:
                    o.tell(v.scalar_tensor_tensor(sc, buf[:, m % 4, 0:w], wi[:, i, h:h + 1], sc, ALU.mult, ALU.add), relu_used)
            for i in order:
                row = score[:, off[i]:off[i + 1]]
                corner = row[0:P // 2, (i + 1) * P - P // 2:(i + 1) * P]
                if (i + 1) * P > TOPK:
                    o.then(v.memset(corner, NEG))
                    for _ in range(TOPK // 8):
                        o.then(v.max(top8[:, :], row))
                        o.then(v.match_replace(row, top8[:, :], row, 10.0 * NEG))
                    o.then(v.tensor_scalar(row, row, 10.0 * NEG, NEG, ALU.not_equal, ALU.mult))
                else:
                    o.then(v.memset(row, 0.0))
                    o.then(v.memset(corner, NEG))
            dve.wait_ge(gate_ready, 32)
            for a in passes:
                for n in range(a.n + a.depth + 1):
                    if n < a.n:
                        i, h = a.heads[n]
                        nk = (i + 1) * P
                        dve.wait_ge(a.s_ready, n + 1)
                        if n >= a.depth:
                            dve.wait_ge(a.e_done, n - a.depth + 1)
                        st = stats[:, n % 8]
                        o.then(v.tensor_tensor_reduce(out=a.masked(n)[:, 0:nk], in0=a.scores(n)[:, 0:nk], in1=score[:, off[i]:off[i + 1]],
                                                      scale=1.0, scalar=10.0 * NEG, op0=ALU.add, op1=ALU.max, accum_out=st[:, 0:1]))
                        o.tell(v.tensor_scalar(st[:, 1:2], st[:, 0:1], -(HD ** -0.5), None, ALU.mult), a.m_done)
                    m = n - a.depth
                    if 0 <= m < a.n and a.depth == 2:
                        w = (a.heads[m][0] + 1) * P - HALF
                        dve.wait_ge(a.pt_ready, m + 1)
                        if m >= 2:
                            dve.wait_ge(a.pv_ready, m - 1)
                        o.tell(v.tensor_copy(a.probsT(m)[:, HALF:HALF + w], a.turned(m)[1][:, 0:w]), a.pt_dve)
                    m -= 1
                    if m >= 0:
                        i, h = a.heads[m]
                        own, sums = (slice(h % 2 * HD, (h % 2 + 1) * HD), slice((1 - h % 2) * HD, (2 - h % 2) * HD))
                        dve.wait_ge(a.pv_ready, m + 1)
                        o.then(v.reciprocal(a.rsum[own, :], psb[m % 2][sums, 0:P]))
                        o.tell(v.tensor_tensor(oT[own, h // 2, i * P:(i + 1) * P], psb[m % 2][own, 0:P], a.rsum[own, :], ALU.mult), a.o_done)

        @block.tensor
        def _(pe):
            mm = nc.tensor.matmul
            pe.wait_ge(w_in_[0], 16)
            for n in range(TT + 1):
                if n < TT:
                    if n >= 2:
                        pe.wait_ge(i_rope, n - 1)
                    for k in range(KC):
                        last = mm(psb[n % 2][:, 0:NI], hT[:, k, n * P:(n + 1) * P], wv(0)[:, k, 0:NI], start=k == 0, stop=k == KC - 1)
                    last.then_inc(i_ready, 1)
                if n >= 1:
                    u = n - 1
                    pe.wait_ge(i_rope, u + 1)
                    if u >= 2:
                        pe.wait_ge(it_used, u - 1)
                    for b in range(IH + 1):
                        last = nc.tensor.transpose(psb[2 + 3 * (u % 2) + b // 4][:, b % 4 * P:(b % 4 + 1) * P], nat[:, u % 2, b * P:(b + 1) * P], ident)
                    last.then_inc(it_ready, 1)
            pe.wait_ge(it_used, TT)
            pe.wait_ge(w_in_[1], 16)
            for m, (i, kb, h) in enumerate(dots):
                w = min(HALF, (i + 1) * P - kb * HALF)
                if m >= 4:
                    pe.wait_ge(relu_done, m - 3)
                mm(psb[m % 4][:, 0:w], qiT[:, h, i * P:(i + 1) * P], kiT[:, kb * HALF:kb * HALF + w],
                   start=True, stop=True).then_inc(dots_ready, 1)
                t, k = m // KC, m % KC
                if t < TT:
                    if k == 0 and t >= 4:
                        pe.wait_ge(v_used, t - 3)
                    last = mm(psb[4 + t % 4][:, :], hT[:, k, t * P:(t + 1) * P], wv(1)[:, k, :], start=k == 0, stop=k == KC - 1)
                    if k == KC - 1:
                        last.then_inc(v_ready, 1)
            pe.wait_ge(relu_done, len(dots))
            pe.wait_ge(v_used, TT)
            for n in range(N_QK + 2):
                kind, t = 2 + n // TT, n % TT
                if n < N_QK:
                    if t == 0:
                        pe.wait_ge(w_in_[kind % 2], 16 * (kind // 2 + 1))
                    if n >= 4:
                        pe.wait_ge(raw_done, n - 3)
                    for k in range(KC):
                        last = mm(psb[n % 4][:, :], hT[:, k, t * P:(t + 1) * P], wv(kind % 2)[:, k, :], start=k == 0, stop=k == KC - 1)
                    last.then_inc(proj_ready, 1)
                if n >= 2:
                    u = n - 2
                    pe.wait_ge(rope_done, 2 * (u + 1))
                    if u >= 4:
                        pe.wait_ge(tr_used, u - 3)
                    for b in range(4):
                        last = nc.tensor.transpose(psb[4 + u % 4][:, b * P:(b + 1) * P], nat[:, u % 2, b * P:(b + 1) * P], ident)
                    last.then_inc(tr_ready, 1)
            pe.wait_ge(tr_used, N_QK)
            pe.wait_ge(w_in_[2], 16)
            for m in range(32):
                b, t = (m % 16) // 2, m % 2
                wb = m // 8
                if m % 8 == 0:
                    pe.wait_ge(w_in_[wb % 2], 16 * (wb // 2 + 3))
                if m >= 2:
                    pe.wait_ge(gate_used, m - 1)
                if 2 <= m < 16:
                    pe.wait_ge(br_used, m - 1)
                last = None
                if m < 16:
                    for k in range(4):
                        mm(psb[4 + m % 2][:, :], w_br[:, k, b * P:(b + 1) * P], y2T[:, k, t * HALF:(t + 1) * HALF], start=k == 0, stop=k == 3)
                for k in range(KC):
                    last = mm(psb[2 + m % 2][:, :], wv(wb % 2)[:, k, (b % 4) * P:(b % 4 + 1) * P], hT[:, k, t * HALF:(t + 1) * HALF],
                              start=k == 0, stop=k == KC - 1)
                last.then_inc(gate_ready, 1)
            pe.wait_ge(gate_used, 32)
            pe.wait_ge(br_used, 16)
            pe.wait_ge(ones_done, 1)
            for p, a in enumerate(passes):
                if p:
                    pe.wait_ge(passes[p - 1].m_done, passes[p - 1].n)
                    pe.wait_ge(passes[p - 1].o_done, passes[p - 1].n)
                for n in range(-a.depth, a.n + 1):
                    if n + a.depth < a.n:
                        i, h = a.heads[n + a.depth]
                        r = HD * (h % 2)
                        if n >= 0:
                            pe.wait_ge(a.m_done, n + 1)
                        for kb in range((i + 4) // 4):
                            w = min(HALF, (i + 1) * P - kb * HALF)
                            last = mm(a.scores(n + a.depth)[:, kb * HALF:kb * HALF + w], qT[r:r + HD, h // 2, i * P:(i + 1) * P],
                                      kT[r:r + HD, h // 2, kb * HALF:kb * HALF + w], start=True, stop=True)
                        last.then_inc(a.s_ready, 1)
                    if 0 <= n < a.n:
                        i, h = a.heads[n]
                        pe.wait_ge(a.e_done, n + 1)
                        if a.depth == 2 and n >= 1:
                            pe.wait_ge(a.pt_act, n)
                            pe.wait_ge(a.pt_dve, n)
                        elif a.depth > 2 and n >= 2:
                            pe.wait_ge(a.pt_act, n - 1)
                        for b in range(i + 1):
                            last = nc.tensor.transpose(a.turned(n)[b // 4][:, (b % 4) * P:(b % 4 + 1) * P], a.probs(n)[:, b * P:(b + 1) * P], ident)
                        last.then_inc(a.pt_ready, 1)
                    if n >= 1:
                        m = n - 1
                        i, h = a.heads[m]
                        pe.wait_ge(a.pt_act, m + 1)
                        if a.depth == 2:
                            pe.wait_ge(a.pt_dve, m + 1)
                        if m >= 2:
                            pe.wait_ge(a.o_done, m - 1)
                        for b in range(i + 1):
                            last = mm(psb[m % 2][:, 0:P], v_sb[:, b, h // 2, h % 2 * HD:h % 2 * HD + P],
                                      a.probsT(m)[:, b * P:(b + 1) * P], start=b == 0, stop=b == i)
                        last.then_inc(a.pv_ready, 1)

    clear_sems(nc, sems)


class Pass:

    def __init__(self, nc, sems, psb, att, tiles, depth):
        self.heads = [(i, h) for i in tiles for h in range(HEADS)]
        self.n, self.depth, self.psb, self.att = len(self.heads), depth, psb, att
        self.width = 2 * SEQ // depth
        sem = lambda n: own_sem(nc, sems, f"b{depth}_{n}")
        self.s_ready, self.m_done, self.e_done, self.pt_ready = sem("s_ready"), sem("m_done"), sem("e_done"), sem("pt_ready")
        self.pt_act, self.pt_dve, self.pv_ready, self.o_done = sem("pt_act"), sem("pt_dve"), sem("pv_ready"), sem("o_done")
        self.rsum = att[:, 6 * SEQ:6 * SEQ + P]

    def scores(self, n):
        at = (4 + n % self.depth * (4 // self.depth)) * HALF
        return self.psb.all[:, at:at + self.width]

    def slot(self, at, n):
        return self.att[:, at * SEQ + n % self.depth * self.width:at * SEQ + (n % self.depth + 1) * self.width]

    def masked(self, n):
        return self.slot(0, n)

    def probs(self, n):
        return self.slot(2, n)

    def probsT(self, n):
        return self.att[:, 4 * SEQ + n % 2 * self.width:4 * SEQ + (n % 2 + 1) * self.width]

    def turned(self, n):
        return (self.psb[2], self.psb[3]) if self.depth == 2 else (self.psb[2 + n % 2],)


NT = 208
WIDTHS = (128, 136, 144, 160, NT)
NT2 = NT - P
ITEMS = (SEQ * TOP + EXPERTS * (NT - 1)) // NT
LIST = -(-((ITEMS + 1) * NT) // P) * P
REC = 4
NO_ROW = SEQ * TOP


def rsqrt(v, o, out, a, t):
    o.then(v.tensor_scalar(t.bitcast(I32), a.bitcast(I32), 1, None, ALU.logical_shift_right))
    o.then(v.tensor_scalar(out.bitcast(I32), t.bitcast(I32), -1.0, float(0x5F3759DF), ALU.mult, ALU.add))
    for _ in range(4):
        o.then(v.scalar_tensor_tensor(t, out, 1.0, out, ALU.mult, ALU.mult))
        o.then(v.tensor_tensor(t, t, a, ALU.mult))
        o.then(v.tensor_scalar(t, t, -0.5, 1.5, ALU.mult, ALU.add))
        o.then(v.tensor_tensor(out, out, t, ALU.mult))


class Routes:
    pass


def route_buffers(space):
    flat = space.rearrange("p b t -> p (b t)")
    used = 0

    def sb(n, shape, dtype=F32):
        nonlocal used
        size = math.prod(shape[1:])
        words = size // 2 if dtype == BF16 else size
        part = flat[:, used:used + words]
        used += words
        if dtype != F32:
            part = part.bitcast(dtype)
        names = "abcd"[:len(shape) - 1]
        return part.rearrange(f"p ({' '.join(names)}) -> p {' '.join(names)}", **dict(zip(names, shape[1:])))

    R = Routes()
    R.logits = sb("logits", [P, TT, EXPERTS])
    R.tri16, R.ones16 = sb("tri16", [P, P], BF16), sb("ones16", [P, P], BF16)
    R.iota_e, R.iota_w = sb("iota_e", [P, EXPERTS]), sb("iota_w", [P, 1])
    R.rec = sb("rec", [P, TT, TOP, REC])
    R.v8, R.i8 = sb("v8", [P, TT, 8]), sb("i8", [P, TT, 8], U32)
    R.i4f = sb("i4f", [P, TT, TOP])
    R.wts, R.wsum = sb("wts", [P, TT, TOP]), sb("wsum", [P, 2, TT])
    R.hot = sb("hot", [P, TOP, TT, EXPERTS])
    R.hsum, R.hsum16 = sb("hsum", [P, TT, EXPERTS]), sb("hsum16", [P, TT, EXPERTS], BF16)
    R.place, R.picked = sb("place", [P, TT, EXPERTS]), sb("picked", [P, TT, EXPERTS])
    R.cnt = sb("cnt", [P, 9, EXPERTS])
    R.slot_f, R.slot_u = sb("slot_f", [P, TOP, TT]), sb("slot_u", [P, TOP, TT], U32)
    R.item_e, R.cls, R.item_i = sb("item_e", [P, 1]), sb("cls", [P, 1]), sb("item_i", [P, 2], I32)
    return R


def mix_and_route(nc, I, S, oT, mix_lead, w_ab, w_rest_hi, R, bias_all, psb, const):
    ctx, sems = ExitStack(), []
    with ctx:
        sb = lambda n, s, d=F32: ctx.enter_context(nc.sbuf_tensor("c_" + n, s, d))
        sem = lambda n: own_sem(nc, sems, "c_" + n)
        mix_rest = sb("mix_rest", [P, KC, SEQ], F32R)
        w_lead = sb("w_lead", [P, KC, D], F32R)
        w_rest_lo = sb("w_rest", [P, KC // 2, D], F32R)
        w_rest = [(w_rest_lo if k < KC // 2 else w_rest_hi)[:, k % (KC // 2), :] for k in range(KC)]
        gate = sb("gate", [P, 2, HALF])
        mix_s = sb("mix_s", [P, 2, HALF])
        x_t = sb("x_t", [P, 2, D])
        r1 = sb("r1", [P, 2, D])
        h2 = sb("h2", [P, 2, D])
        h2T = sb("h2T", [P, 2, KC, P])
        gain = sb("gain", [P, D])
        w_r = sb("w_r", [P, KC, EXPERTS])
        b_r = sb("b_r", [P, EXPERTS])
        sq = sb("sq", [P, D])
        ssq = sb("ssq", [P, 4, TT])
        w_raw = [r1[:, 0, :], r1[:, 1, :], h2[:, 1, :], sq[:, :]]
        mix = h2[:, 0, :].rearrange("p (s n) -> p s n", s=2)
        tri = sb("tri", [P, P])
        empty = sb("empty", [P, LIST // P, REC])
        b_nat = sb("b_nat", [P, 6, P])
        logits, tri16, ones16, rec = R.logits, R.tri16, R.ones16, R.rec
        ident = const["ident"]

        dve_step, act_step = sem("dve_step"), sem("act_step")
        wo_in, par_in = [sem(f"wo_in{s}") for s in range(4)], sem("par_in")
        sum_done, lead_done, wl_done, wr_done = sem("sum_done"), sem("lead_done"), sem("wl_done"), sem("wr_done")
        gm_in = [sem(f"gm_in{s}") for s in range(2)]
        x_in = [sem(f"x_in{s}") for s in range(2)]
        br_ready, mix_done = sem("br_ready"), sem("mix_done")
        o_ready, r1_done, sq_done, h2_done = sem("o_ready"), sem("r1_done"), sem("sq_done"), sem("h2_done")
        r1_out = [sem(f"r1_out{s}") for s in range(2)]
        ht_ready, ht_used, lg_ready, lg_done = sem("ht_ready"), sem("ht_used"), sem("lg_ready"), sem("lg_done")
        list_clear, pool_step = sem("list_clear"), sem("pool_step")
        b_in, bt_ready = sem("b_in"), sem("bt_ready")
        block = ctx.enter_context(nc.Block())

        @block.sync
        def _(sp):
            for m in range(2 * KC):
                b, t = m // 2, m % 2
                if m >= 2:
                    sp.wait_ge(sum_done, m - 1)
                cols = slice(t * HALF, (t + 1) * HALF)
                sp.dma_start(gate[:, m % 2, :], S["gate_a"][b, :, cols]).then_inc(gm_in[m % 2], 16)
                sp.dma_start(mix_s[:, m % 2, :], S["mix_s"][b, :, cols]).then_inc(gm_in[m % 2], 16)
                if m % 2:
                    k = m // 2
                    if k >= 4:
                        sp.wait_ge(wr_done, k - 3)
                    sp.dma_start(w_raw[k % 4], I["w_o"][0][k * P:(k + 1) * P, :]).then_inc(wo_in[k % 4], 16)
            for i in range(TT + 1):
                if i < TT:
                    if i >= 2:
                        sp.wait_ge(r1_done, i - 1)
                    sp.dma_start(x_t[:, i % 2, :], I["x"][0, i * P:(i + 1) * P, :]).then_inc(x_in[i % 2], 16)
                if i >= 1:
                    rows = slice((i - 1) * P, i * P)
                    sp.wait_ge(h2_done, i)
                    sp.dma_start(S["r1"][rows, :], r1[:, (i - 1) % 2, :]).then_inc(r1_out[(i - 1) % 2], 16)
                    sp.dma_start(S["h2"][rows, :], h2[:, (i - 1) % 2, :]).then_inc(r1_out[(i - 1) % 2], 16)
            for s in range(2):
                sp.wait_ge(r1_out[s], 16 * TT)

        @block.gpsimd
        def _(pool):
            g = nc.gpsimd
            for m in range(2 * KC):
                cols = slice(m % 2 * HALF, (m % 2 + 1) * HALF)
                pool.wait_ge(lead_done, m + 1)
                g.tensor_tensor(mix_rest[:, m // 2, cols], mix[:, m % 2, :], mix_lead[:, m // 2, cols].bitcast(F32), ALU.subtract).then_inc(mix_done, 1)
            pool.wait_ge(br_ready, 2 * KC)
            g.iota(R.iota_e[:, :], pattern=[[1, EXPERTS]], base=0, channel_multiplier=0, allow_small_or_imprecise_dtypes=True).then_inc(pool_step, 1)
            g.iota(R.iota_w[:, :], pattern=[[1, 1]], base=0, channel_multiplier=1, allow_small_or_imprecise_dtypes=True).then_inc(pool_step, 1)
            g.memset(empty[:, :, :], 0.0).then_inc(pool_step, 1)
            pool.wait_ge(pool_step, 3)
            g.iota(empty[:, :, 0:2].bitcast(U32), pattern=[[0, LIST // P], [0, 2]], base=NO_ROW, channel_multiplier=0).then_inc(pool_step, 1)
            g.memset(rec[:, :, :, :], 0.0).then_inc(pool_step, 1)
            pool.wait_ge(pool_step, 5)
            pool.dma_start(S["list"].rearrange("(p n) r -> p n r", p=P), empty[:, :, :]).then_inc(list_clear, 16)
            g.iota(rec[:, :, :, 0].bitcast(U32), pattern=[[P, TT], [0, TOP]], base=0, channel_multiplier=1).then_inc(pool_step, 1)
            g.iota(rec[:, :, :, 1].bitcast(U32), pattern=[[P * TOP, TT], [1, TOP]], base=0, channel_multiplier=TOP).then_inc(pool_step, 1)
            pool.wait_ge(list_clear, 16)

        @block.scalar
        def _(act):
            o = Order(act, act_step)
            with nc.allow_non_contiguous_dma(reason="small rows, repeated over partitions"):
                act.dma_start(gain[:, :], I["norm_ffn"][0].unsqueeze(0).broadcast_to([P, D])).then_inc(par_in, 16)
                act.dma_start(b_r[:, :], I["b_router"][0].unsqueeze(0).broadcast_to([P, EXPERTS])).then_inc(par_in, 16)
                act.dma_start(w_r[:, :, :], I["w_router"][0].rearrange("(k p) e -> p k e", p=P)).then_inc(par_in, 16)
                act.dma_start(tri[:, :], I["t_tri"]).then_inc(par_in, 16)
            for j, name in enumerate(("b_gate", "b_up", "b_down")):
                act.dma_start(b_nat[:, 2 * j:2 * j + 2, :], I[name][0].rearrange("(a e) (b p) -> (e b) a p", a=2, p=P)).then_inc(b_in, 16)
            for m in range(2 * KC):
                cols = slice(m % 2 * HALF, (m % 2 + 1) * HALF)
                act.wait_ge(sum_done, m + 1)
                nc.scalar.copy(mix_lead[:, m // 2, cols], mix[:, m % 2, :]).then_inc(lead_done, 1)
                if m % 2:
                    k = m // 2
                    act.wait_ge(wo_in[k % 4], 16 * (k // 4 + 1))
                    nc.scalar.copy(w_lead[:, k, :], w_raw[k % 4]).then_inc(wl_done, 1)
            act.wait_ge(bt_ready, 1)
            for j in range(3):
                o.go(nc.scalar.copy(bias_all[:, :, j, :].rearrange("p (a e) b -> p a e b", a=2),
                                    psb[4 + j][:, 0:2 * P].rearrange("p (a e b) -> p a e b", a=2, b=KC)))
            for i in range(TT):
                act.wait_ge(r1_done, i + 1)
                if i:
                    act.wait_ge(sq_done, i)
                nc.scalar.activation(sq[:, :], r1[:, i % 2, :], ACT.Square, accum_out=ssq[:, 0, i:i + 1]).then_inc(sq_done, 1)
                for b in range(2):
                    act.wait_ge(ht_ready, 2 * i + b + 1)
                    nc.scalar.copy(h2T[:, i % 2, 4 * b:4 * b + 4, :], psb[4 + b][:, :].rearrange("p (b n) -> p b n", b=4)).then_inc(ht_used, 1)

        @block.vector
        def _(dve):
            v = nc.vector
            o = Order(dve, dve_step)
            dve.wait_ge(par_in, 64)
            for m in range(2 * KC):
                b, t = m // 2, m % 2
                dve.wait_ge(br_ready, m + 1)
                dve.wait_ge(gm_in[m % 2], 32 * (m // 2 + 1))
                if m >= 2:
                    dve.wait_ge(mix_done, m - 1)
                o.then(v.tensor_tensor(mix[:, m % 2, :], psb[m % 4][:, :], gate[:, m % 2, :], ALU.mult))
                o.tell(v.tensor_tensor(mix[:, m % 2, :], mix[:, m % 2, :], mix_s[:, m % 2, :], ALU.add), sum_done)
                k = m // 2 - 1
                if m % 2 and 0 <= k < KC // 2:
                    dve.wait_ge(wl_done, k + 1)
                    o.tell(v.tensor_tensor(w_rest[k], w_raw[k % 4], w_lead[:, k, :].bitcast(F32), ALU.subtract), wr_done)
            dve.wait_ge(br_ready, 2 * KC)
            for k in range(KC // 2, KC):
                dve.wait_ge(wl_done, k + 1)
                o.tell(v.tensor_tensor(w_rest[k], w_raw[k % 4], w_lead[:, k, :].bitcast(F32), ALU.subtract), wr_done)
            o.go(v.tensor_copy(tri16[:, :], tri[:, :]))
            o.go(v.memset(ones16[:, :], 1.0))
            dve.wait_ge(pool_step, 7)
            for i in range(TT + 1):
                if i < TT:
                    dve.wait_ge(x_in[i % 2], 16 * (i // 2 + 1))
                    dve.wait_ge(o_ready, i + 1)
                    if i >= 2:
                        dve.wait_ge(r1_out[i % 2], 32 * (i // 2))
                    half = lambda b: (r1[:, i % 2, b * HALF:(b + 1) * HALF], psb[2 * (i % 2) + b][:, :], x_t[:, i % 2, b * HALF:(b + 1) * HALF])
                    o.then(v.tensor_tensor(*half(0), ALU.add))
                    o.tell(v.tensor_tensor(*half(1), ALU.add), r1_done)
                    dve.wait_ge(sq_done, i + 1)
                    one = lambda r: ssq[:, r, i:i + 1]
                    o.then(v.tensor_scalar(one(0), one(0), 1.0 / D, EPS, ALU.mult, ALU.add))
                    rsqrt(v, o, one(1), one(0), one(2))
                    o.tell(v.scalar_tensor_tensor(h2[:, i % 2, :], r1[:, i % 2, :], one(1), gain[:, :], ALU.mult, ALU.mult), h2_done)
                if i >= 1:
                    dve.wait_ge(lg_ready, i)
                    n = i - 1
                    o.tell(v.tensor_tensor(logits[:, n, :], psb[6 + n % 2][:, 0:EXPERTS], b_r[:, :], ALU.add), lg_done)
                    o.then(v.max(R.v8[:, n, :], logits[:, n, :]))
                    o.go(v.max_index(R.i8[:, n, :], R.v8[:, n, :], logits[:, n, :]))
                    o.then(v.tensor_tensor(R.wts[:, n, :], R.v8[:, n, 0:TOP], R.v8[:, n, 0:1].broadcast_to([P, TOP]), ALU.subtract))
                    o.then(v.tensor_copy(R.i4f[:, n, :], R.i8[:, n, 0:TOP]))
                    for k in range(TOP):
                        o.go(v.tensor_scalar(R.hot[:, k, n, :], R.iota_e[:, :], R.i4f[:, n, k:k + 1], None, ALU.is_equal))
                    o.wait()
                    o.go(v.tensor_tensor(R.hsum[:, n, :], R.hot[:, 0, n, :], R.hot[:, 1, n, :], ALU.add))
                    o.then(v.tensor_tensor(R.picked[:, n, :], R.hot[:, 2, n, :], R.hot[:, 3, n, :], ALU.add))
                    o.then(v.tensor_tensor(R.hsum16[:, n, :], R.hsum[:, n, :], R.picked[:, n, :], ALU.add))

        @block.tensor
        def _(pe):
            mm = nc.tensor.matmul
            for m in range(2 * KC):
                b, t = m // 2, m % 2
                if m >= 4:
                    pe.wait_ge(sum_done, m - 3)
                for k in range(4):
                    last = mm(psb[m % 4][:, :], w_ab[:, k, b * P:(b + 1) * P], oT[:, k, t * HALF:(t + 1) * HALF], start=k == 0, stop=k == 3)
                last.then_inc(br_ready, 1)
            pe.wait_ge(b_in, 48)
            for j in range(6):
                last = nc.tensor.transpose(psb[4 + j // 2][:, (j % 2) * P:(j % 2 + 1) * P], b_nat[:, j, :], ident)
            last.then_inc(bt_ready, 1)
            pe.wait_ge(wl_done, KC)
            pe.wait_ge(mix_done, 2 * KC)
            pe.wait_ge(par_in, 64)
            for i in range(TT + 2):
                if i < TT:
                    if i >= 2:
                        pe.wait_ge(r1_done, i - 1)
                    for b in range(2):
                        rows, cols = slice(i * P, (i + 1) * P), slice(b * HALF, (b + 1) * HALF)
                        for n, (x, w) in enumerate(((mix_lead, "lead"), (mix_rest, "lead"), (mix_lead, "rest"))):
                            if i == 0 and b == 0 and n == 2:
                                pe.wait_ge(wr_done, KC)
                            for k in range(KC):
                                w_k = w_lead[:, k, :] if w == "lead" else w_rest[k]
                                last = mm(psb[2 * (i % 2) + b][:, :], x[:, k, rows], w_k[:, cols], start=n == 0 and k == 0, stop=n == 2 and k == KC - 1)
                    last.then_inc(o_ready, 1)
                if 1 <= i <= TT:
                    pe.wait_ge(h2_done, i)
                    for b in range(2):
                        if i >= 2:
                            pe.wait_ge(ht_used, 2 * (i - 2) + b + 1)
                        for k in range(4):
                            last = nc.tensor.transpose(psb[4 + b][:, k * P:(k + 1) * P], h2[:, (i - 1) % 2, (4 * b + k) * P:(4 * b + k + 1) * P], ident)
                        last.then_inc(ht_ready, 1)
                if i >= 2:
                    n = i - 2
                    pe.wait_ge(ht_used, 2 * n + 2)
                    if n >= 2:
                        pe.wait_ge(lg_done, n - 1)
                    for k in range(KC):
                        last = mm(psb[6 + n % 2][:, 0:EXPERTS], h2T[:, n % 2, k, :], w_r[:, k, :], start=k == 0, stop=k == KC - 1)
                    last.then_inc(lg_ready, 1)
    clear_sems(nc, sems)


NB = 4


CW = 256
NCW = D // CW


def experts(nc, I, S, R, w_next, ple, r, pp, items_sb, class_sb, bias_all, psb, const):
    ctx, sems = ExitStack(), []
    with ctx:
        sb = lambda n, s, d=F32: ctx.enter_context(nc.sbuf_tensor("d_" + n, s, d))
        sem = lambda n: own_sem(nc, sems, "d_" + n)
        w_g, w_u, w_d = (sb(n, [P, NCW, KC, CW]) for n in ("w_g", "w_u", "w_d"))
        x_rows, x_rows2 = sb("x_rows", [P, D]), sb("x_rows2", [NT2, D])
        xT = sb("xT", [P, KC, NT])
        aT = sb("aT", [P, KC, NT])
        yT = sb("yT", [P, 2, NT])
        y_rows, y_rows2 = sb("y_rows", [P, D]), sb("y_rows2", [NT2, D])
        g_sb, s_sb, u_sb = sb("g_sb", [P, 2, NT]), sb("s_sb", [P, 2, NT]), sb("u_sb", [P, 2, NT])
        nxt, nxt2 = sb("nxt", [P, REC]), sb("nxt2", [NT2, REC])
        cur, cur2 = sb("cur", [P, REC]), sb("cur2", [NT2, REC])
        b_nxt, b_cur = sb("b_nxt", [P, 3, KC]), sb("b_cur", [P, 3, KC])
        e_sb = sb("e_sb", [1, 1], I32)
        PK = PLE // P
        w_proj = ple[:, 0:PK, :]
        p_all = ple[:, PK:2 * PK, :].rearrange("p a (t n) -> p (a t) n", n=PLE)
        pT = sb("pT", [P, 2, PK, P])
        ident = const["ident"]

        e_done, routed = sem("e_done"), sem("routed")
        pos_ready, slots_done, items_done = sem("pos_ready"), sem("slots_done"), sem("items_done")
        list_out = [sem(f"list_out{k}") for k in range(TOP)]
        item_out, item_back = sem("item_out"), sem("item_back")
        next_in = sem("next_in")
        ple_in, p_ready, pt_done, pp_ready, pp_done = (sem(n) for n in ("ple_in", "p_ready", "pt_done", "pp_ready", "pp_done"))
        pp_out = [sem(f"pp_out{s}") for s in range(2)]

        wg_in, wu_in, wd_in = ([sem(f"{n}{c}") for c in range(NCW)] for n in ("wg_in", "wu_in", "wd_in"))
        e_in, b_in, list_in, x_in, x2_in, y_out = (sem(n) for n in ("e_in", "b_in", "list_in", "x_in", "x2_in", "y_out"))
        dve_step = sem("dve_step")
        rows_clear = sem("rows_clear")
        sp_held, pool_held = sem("sp_held"), sem("pool_held")
        cur_ready, gu_ready, g_done, gu_read, s_done, a_done = (sem(n) for n in ("cur_ready", "gu_ready", "g_done", "gu_read", "s_done", "a_done"))
        xt_ready, xt_used, yd_ready, yt_done, yr_ready, yr_done = (sem(n) for n in ("xt_ready", "xt_used", "yd_ready", "yt_done", "yr_ready", "yr_done"))
        block = ctx.enter_context(nc.Block())

        def held(eng, own):
            eng.sem_inc(own, 1)

        XB = (7, 5, 6, 4)
        XR = [(k, k + 2) for k in range(0, KC, 2)]
        most = ITEMS

        def loop(eng, body):
            n = eng.value_load(items_sb[0:1, 0:1], min_val=2, max_val=most)
            body(0, True)
            with eng.Fori(1, n) as w:
                body(w, False)
            return n

        @block.sync
        def _(sp):
            def expert_of(w):
                sp.dma_start(e_sb[:, :], S["items"][0:1, bass.ds(w, 1)]).then_inc(e_in, 16)
                sp.wait_ge(e_in, 16 * (w + 1))
                held(sp, sp_held)
                return sp.value_load(e_sb[0:1, 0:1], min_val=0, max_val=EXPERTS - 1)

            def body(w, first):
                e = expert_of(w)
                if not first:
                    sp.wait_ge(cur_ready, w)
                sp.dma_start(b_nxt[:, :, :], bias_all[:, bass.ds(e, 1), :, :].rearrange("p a j b -> p (a j) b")).then_inc(b_in, 16)
                for c in range(NCW):
                    if not first:
                        sp.wait_ge(gu_ready, 2 * KC // 2 * w - KC + 2 * c + 2)
                    elif c < NCW - 1:
                        if c:
                            sp.wait_ge(list_out[c - 1], 16 * TT)
                    else:
                        sp.wait_ge(x_in, 16)
                        sp.wait_ge(x2_in, 16)
                    for t, name, s in ((w_g, "w_gate", wg_in), (w_u, "w_up", wu_in)):
                        sp.dma_start(t[:, c], I[name][0][bass.ds(e, 1), :, c * CW:(c + 1) * CW]
                                     .rearrange("a (k p) n -> p (a k) n", p=P)).then_inc(s[c], 16)
                for c in range(NCW):
                    if not first:
                        sp.wait_ge(yd_ready, KC * w - KC + 2 * c + 2)
                    sp.dma_start(w_d[:, c], I["w_down"][0][bass.ds(e, 1), :, c * CW:(c + 1) * CW]
                                 .rearrange("a (k p) n -> p (a k) n", p=P)).then_inc(wd_in[c], 16)
            sp.dma_start(p_all[:, :, :], I["p"][0, 0].rearrange("(t p) n -> p t n", p=P)).then_inc(ple_in, 16)
            sp.dma_start(w_proj[:, :, :], I["w_ple_proj"][0].rearrange("(k p) n -> p k n", p=P)).then_inc(ple_in, 16)
            sp.wait_ge(items_done, 1)
            with nc.allow_non_contiguous_dma(reason="512 bytes"):
                sp.dma_start(S["items"].rearrange("c n -> n c"), R.item_i[:, :]).then_inc(item_out, 16)
            sp.wait_ge(item_out, 16)
            sp.dma_start(class_sb[:, :], S["items"][1:2, :]).then_inc(item_back, 16)
            sp.wait_ge(item_back, 16)
            held(sp, sp_held)
            n = loop(sp, body)
            for s in range(2):
                sp.wait_ge(pp_out[s], 16 * (TT // 2))
            sp.wait_ge(x_in, 16 * (n + 1))
            sp.wait_ge(x2_in, 16 * (n + 1))
            for half, to in enumerate((w_next, ple)):
                sp.dma_start(to, I["w_ple_gate"][0][half * 4 * P:(half + 1) * 4 * P, :].rearrange("(k p) n -> p k n", p=P)).then_inc(next_in, 16)
            for name, to in (("r1", r), ("pp", pp)):
                sp.dma_start(to, S[name][0:NB * P, :].rearrange("(i p) d -> p i d", p=P)).then_inc(next_in, 16)
            sp.wait_ge(next_in, 64)

        @block.gpsimd
        def _(pool):
            def fetch(w):
                pool.dma_start(nxt[:, :], S["list"][bass.ds(w * NT, P), :]).then_inc(list_in, 16)
                pool.dma_start(nxt2[:, :], S["list"][bass.ds(w * NT + P, NT2), :]).then_inc(list_in, 16)
                pool.wait_ge(list_in, 32 * (w + 1))
                held(pool, pool_held)
                for t, n, s in ((x_rows, nxt, x_in), (x_rows2, nxt2, x2_in)):
                    nc.gpsimd.indirect_dma_start(out=t[:, :], out_offset=None, in_=S["h2"],
                                                 in_offset=bass.IndirectOffsetOnAxis(ap=n[:, 0:1].bitcast(U32), axis=0),
                                                 bounds_check=SEQ - 1, oob_is_err=False).then_inc(s, 16)

            def body(w, first):
                pool.wait_ge(cur_ready, w + 1)
                pool.wait_ge(xt_ready, len(XR) * (w + 1))
                fetch(w + 1)
                pool.wait_ge(yr_done, 4 * w + 4)
                held(pool, pool_held)
                for t, n in ((y_rows, cur), (y_rows2, cur2)):
                    nc.gpsimd.indirect_dma_start(out=S["ys"], out_offset=bass.IndirectOffsetOnAxis(ap=n[:, 1:2].bitcast(U32), axis=0),
                                                 in_=t[:, :], in_offset=None, bounds_check=NO_ROW - 1, oob_is_err=False).then_inc(y_out, 16)
                pool.wait_ge(y_out, 32 * (w + 1))
            nc.gpsimd.memset(x_rows[:, :], 0.0).then_inc(rows_clear, 1)
            nc.gpsimd.memset(x_rows2[:, :], 0.0).then_inc(rows_clear, 1)
            pool.wait_ge(rows_clear, 2)
            pool.wait_ge(slots_done, 1)
            for k in range(TOP):
                for i in range(TT):
                    nc.gpsimd.indirect_dma_start(out=S["list"], out_offset=bass.IndirectOffsetOnAxis(ap=R.slot_u[:, k, i:i + 1], axis=0),
                                         in_=R.rec[:, i, k, :], in_offset=None).then_inc(list_out[k], 16)
            for k in range(TOP):
                pool.wait_ge(list_out[k], 16 * TT)
            pool.wait_ge(items_done, 1)
            fetch(0)
            loop(pool, body)
            pool.wait_ge(list_in, 32)

        @block.scalar
        def _(act):
            def turned_rows(w):
                for r, (k0, k1) in enumerate(XR):
                    act.wait_ge(xt_ready, len(XR) * w + r + 1)
                    nc.scalar.copy(xT[:, k0:k1, :], psb[XB[r]][:, 0:(k1 - k0) * NT].rearrange("p (k n) -> p k n", n=NT)).then_inc(xt_used, 1)

            def body(w, first):
                for b in range(KC):
                    act.wait_ge(g_done, KC * w + b + 1)
                    if b >= 2:
                        act.wait_ge(a_done, KC * w + b - 1)
                    elif not first:
                        act.wait_ge(a_done, KC * w + b - 1)
                    nc.scalar.activation(s_sb[:, b % 2, :], g_sb[:, b % 2, :], ACT.Sigmoid, scale=1.702).then_inc(s_done, 1)
                turned_rows(w + 1)
                for b in range(KC + 1):
                    if b < KC:
                        act.wait_ge(yd_ready, KC * w + b + 1)
                        if b >= 2 and b % 2 == 0:
                            act.wait_ge(yr_ready, 4 * w + b // 2)
                        nc.scalar.activation(yT[:, b % 2, :], psb[3 + b % 2][:, 0:NT], ACT.Identity,
                                             bias=b_cur[:, 2, b:b + 1]).then_inc(yt_done, 1)
                    if b >= 2 and b % 2 == 0:
                        r = b // 2 - 1
                        act.wait_ge(yr_ready, 4 * w + r + 1)
                        src = psb[5 + r % 2]
                        cols = slice(r * 2 * P, (r + 1) * 2 * P)
                        nc.scalar.activation(y_rows[:, cols], src[:, 0:2 * P], ACT.Copy, scale=cur[:, 2:3])
                        nc.scalar.activation(y_rows2[:, cols], src[0:NT2, 2 * P:4 * P], ACT.Copy, scale=cur2[:, 2:3]).then_inc(yr_done, 1)
            nc.scalar.activation(R.wts[:, :, :], R.wts[:, :, :], ACT.Exp).then_inc(e_done, 1)
            for i in range(TT):
                act.wait_ge(p_ready, i + 1)
                nc.scalar.copy(pT[:, i % 2], psb[2 + i % 2][:, 0:PLE].rearrange("p (b n) -> p b n", b=PK)).then_inc(pt_done, 1)
                if i >= 2:
                    act.wait_ge(pp_out[i % 2], 16 * (i // 2))
                for b in range(2):
                    act.wait_ge(pp_ready, 2 * i + b + 1)
                    nc.scalar.copy(pp[:, i % 2, b * HALF:(b + 1) * HALF], psb[4 + b][:, :]).then_inc(pp_done, 1)
                act.wait_ge(pp_done, 2 * i + 2)
                act.dma_start(S["pp"][i * P:(i + 1) * P, :], pp[:, i % 2, :]).then_inc(pp_out[i % 2], 16)
            act.wait_ge(items_done, 1)
            turned_rows(0)
            loop(act, body)

        @block.vector
        def _(dve):
            v = nc.vector

            def body(w, first):
                dve.wait_ge(list_in, 32 * (w + 1))
                dve.wait_ge(b_in, 16 * (w + 1))
                if not first:
                    dve.wait_ge(y_out, 32 * w)
                    dve.wait_ge(yr_done, 4 * w)
                v.tensor_copy(cur[:, :].bitcast(U32), nxt[:, :].bitcast(U32))
                v.tensor_copy(cur2[:, :].bitcast(U32), nxt2[:, :].bitcast(U32))
                v.tensor_copy(b_cur[:, :, :], b_nxt[:, :, :]).then_inc(cur_ready, 1)
                dve.wait_ge(cur_ready, w + 1)
                for b in range(KC + 1):
                    if b < KC:
                        src, s = psb[b % 3], b % 2
                        dve.wait_ge(gu_ready, KC * w + b + 1)
                        if b >= 2 or not first:
                            dve.wait_ge(a_done, KC * w + b - 1)
                        v.tensor_scalar(g_sb[:, s, :], src[:, 0:NT], b_cur[:, 0, b:b + 1], SWIGLU_LIMIT, ALU.add, ALU.min).then_inc(g_done, 1)
                        v.tensor_scalar(u_sb[:, s, :], src[:, CW:CW + NT], b_cur[:, 1, b:b + 1], SWIGLU_LIMIT, ALU.add, ALU.min).then_inc(gu_read, 1)
                        dve.wait_ge(gu_read, KC * w + b + 1)
                        v.tensor_scalar(u_sb[:, s, :], u_sb[:, s, :], -SWIGLU_LIMIT, 1.0, ALU.max, ALU.add).then_inc(dve_step, 1)
                    if b >= 1:
                        s = (b - 1) % 2
                        dve.wait_ge(s_done, KC * w + b)
                        v.tensor_tensor(s_sb[:, s, :], s_sb[:, s, :], g_sb[:, s, :], ALU.mult).then_inc(dve_step, 1)
                        dve.wait_ge(dve_step, 2 * KC * w + min(b + 1, KC) + b)
                        v.tensor_tensor(aT[:, b - 1, :], s_sb[:, s, :], u_sb[:, s, :], ALU.mult).then_inc(a_done, 1)
            o = Order(dve, routed)
            shape = [P, TT, EXPERTS]
            dve.wait_ge(e_done, 1)
            o.then(v.tensor_reduce(R.wsum[:, 0, :], R.wts[:, :, :], AX.X, ALU.add))
            o.then(v.reciprocal(R.wsum[:, 1, :], R.wsum[:, 0, :]))
            o.then(v.tensor_tensor(R.rec[:, :, :, 2], R.wts[:, :, :], R.wsum[:, 1, :].unsqueeze(2).broadcast_to([P, TT, TOP]), ALU.mult))
            dve.wait_ge(pos_ready, 1)
            COUNT, ITEMS_OF, ONE, END, FIRST, CLASS, SHARE, REST, EDGE = range(9)
            c = lambda n: R.cnt[:, n, :]
            wide = lambda n: c(n).unsqueeze(1).broadcast_to(shape)
            o.then(v.tensor_copy(c(COUNT), psb[1][:, 0:EXPERTS]))
            o.then(v.tensor_scalar(c(ITEMS_OF), c(COUNT), 0.0, None, ALU.is_gt))
            for n in range(1, -(-SEQ // NT)):
                o.then(v.scalar_tensor_tensor(c(ITEMS_OF), c(COUNT), float(n * NT), c(ITEMS_OF), ALU.is_gt, ALU.add))
            o.then(v.memset(c(ONE), 1.0))
            o.then(v.tensor_tensor_scan(c(END), c(ONE), c(ITEMS_OF), 0.0, ALU.mult, ALU.add))
            o.then(v.tensor_tensor(c(FIRST), c(END), c(ITEMS_OF), ALU.subtract))
            o.then(v.tensor_scalar(c(FIRST), c(FIRST), float(NT), None, ALU.mult))
            o.go(v.memset(c(CLASS), 0.0))
            o.then(v.memset(c(SHARE), float(WIDTHS[0])))
            for n in range(len(WIDTHS) - 1):
                o.then(v.scalar_tensor_tensor(c(EDGE), c(ITEMS_OF), float(WIDTHS[n]), c(COUNT), ALU.mult, ALU.is_lt))
                o.go(v.tensor_tensor(c(CLASS), c(CLASS), c(EDGE), ALU.add))
                o.then(v.scalar_tensor_tensor(c(SHARE), c(EDGE), float(WIDTHS[n + 1] - WIDTHS[n]), c(SHARE), ALU.mult, ALU.add))
            o.then(v.tensor_scalar(c(REST), c(SHARE), -1.0, float(NT), ALU.mult, ALU.add))
            number = psb[0][:, 0:TT * EXPERTS].rearrange("p (t e) -> p t e", t=TT)
            o.then(v.tensor_tensor(R.place[:, :, :], number, wide(FIRST), ALU.add))
            for n in range(1, -(-SEQ // NT)):
                o.then(v.tensor_scalar(c(EDGE), c(SHARE), float(n), None, ALU.mult))
                o.then(v.tensor_tensor(R.picked[:, :, :], number, wide(EDGE), ALU.is_ge))
                o.then(v.tensor_tensor(R.picked[:, :, :], R.picked[:, :, :], wide(REST), ALU.mult))
                o.then(v.tensor_tensor(R.place[:, :, :], R.place[:, :, :], R.picked[:, :, :], ALU.add))
            for k in range(TOP):
                o.then(v.tensor_tensor(R.picked[:, :, :], R.hot[:, k], R.place[:, :, :], ALU.mult))
                o.then(v.tensor_reduce(R.slot_f[:, k, :], R.picked[:, :, :], AX.X, ALU.add))
            o.tell(v.tensor_copy(R.slot_u[:, :, :], R.slot_f[:, :, :]), slots_done)
            o.then(v.tensor_scalar(c(EDGE), c(END), R.iota_w[:, 0:1], None, ALU.is_le))
            o.then(v.tensor_reduce(R.item_e[:, :], c(EDGE), AX.X, ALU.add))
            o.then(v.tensor_scalar(R.item_e[:, :], R.item_e[:, :], float(EXPERTS - 1), None, ALU.min))
            o.then(v.tensor_scalar(c(EDGE), R.iota_e[:, :], R.item_e[:, 0:1], None, ALU.is_equal))
            o.then(v.tensor_tensor(c(EDGE), c(EDGE), c(CLASS), ALU.mult))
            o.then(v.tensor_reduce(R.cls[:, :], c(EDGE), AX.X, ALU.add))
            o.then(v.tensor_copy(items_sb[:, 0:1], c(END)[0:1, EXPERTS - 1:EXPERTS]))
            o.then(v.tensor_copy(R.item_i[:, 1:2], R.cls[:, :]))
            o.tell(v.tensor_copy(R.item_i[:, 0:1], R.item_e[:, :]), items_done)
            loop(dve, body)

        @block.tensor
        def _(pe):
            mm, tr = nc.tensor.matmul, nc.tensor.transpose

            def turn_rows(w):
                pe.wait_ge(x_in, 16 * (w + 1))
                pe.wait_ge(x2_in, 16 * (w + 1))
                if not isinstance(w, int):
                    pe.wait_ge(yr_done, 4 * (w - 1))
                for x, size, start in ((x_rows, P, 0), (x_rows2, NT2, P)):
                    for r, (k0, k1) in enumerate(XR):
                        for k in range(k0, k1):
                            at = (k - k0) * NT + start
                            last = tr(psb[XB[r]][:, at:at + size], x[:, k * P:(k + 1) * P], ident[0:size, 0:size])
                        if start:
                            last.then_inc(xt_ready, 1)

            def item(w, first, wd):
                pe.wait_ge(xt_used, len(XR) * (w + 1))
                for b in range(KC):
                    c, at = b // 2, (b % 2) * P
                    if b % 2 == 0:
                        pe.wait_ge(wg_in[c], 16 * (w + 1))
                        pe.wait_ge(wu_in[c], 16 * (w + 1))
                    if b >= 3 or not first:
                        pe.wait_ge(gu_read, KC * w + b - 2)
                    for wt, to in ((w_g, 0), (w_u, CW)):
                        for k in range(KC):
                            last = mm(psb[b % 3][:, to:to + wd], wt[:, c, k, at:at + P], xT[:, k, 0:wd], start=k == 0, stop=k == KC - 1)
                    last.then_inc(gu_ready, 1)
                turn_rows(w + 1)
                pe.reg_load(width_reg, class_sb[0:1, 1:2] if first else class_sb[0:1, bass.ds(w + 1, 1)])
                for b in range(KC + 1):
                    if b < KC:
                        c, at = b // 2, (b % 2) * P
                        if b % 2 == 0:
                            pe.wait_ge(wd_in[c], 16 * (w + 1))
                        if b == 1:
                            pe.wait_ge(xt_used, len(XR) * (w + 2))
                        if b >= 2 or not first:
                            pe.wait_ge(yt_done, KC * w + b - 1)
                        for k in range(KC):
                            if b == 0 and (k == 0 or k == KC - 1):
                                pe.wait_ge(a_done, KC * w + KC - (k == 0))
                            last = mm(psb[3 + b % 2][:, 0:wd], w_d[:, c, k, at:at + P], aT[:, k, 0:wd], start=k == 0, stop=k == KC - 1)
                        last.then_inc(yd_ready, 1)
                    if b >= 1:
                        d = b - 1
                        r, at = d // 2, (d % 2) * P
                        pe.wait_ge(yt_done, KC * w + b)
                        if d % 2 == 0 and (d >= 4 or not first):
                            pe.wait_ge(yr_done, 4 * w + r - 1)
                        last = tr(psb[5 + r % 2][:, at:at + P], yT[:, d % 2, 0:P], ident)
                        if wd > P:
                            last = tr(psb[5 + r % 2][0:wd - P, 2 * P + at:2 * P + at + P], yT[:, d % 2, P:wd], ident)
                        if d % 2:
                            last.then_inc(yr_ready, 1)

            def body(w, first):
                width = pe.snap(width_reg, min_val=0, max_val=len(WIDTHS) - 1)

                def pick(lo, hi):
                    if hi - lo == 1:
                        item(w, first, WIDTHS[lo])
                        return
                    mid = (lo + hi) // 2
                    with pe.If(width < mid):
                        pick(lo, mid)
                    with pe.Else():
                        pick(mid, hi)
                pick(0, len(WIDTHS))
            width_reg = pe.alloc_register("item_width")
            for i in range(TT):
                for j in range(i + 1):
                    mm(psb[0][:, i * EXPERTS:(i + 1) * EXPERTS], (R.tri16 if j == i else R.ones16)[:, :], R.hsum16[:, j, :], start=j == 0, stop=j == i)
            for j in range(TT):
                last = mm(psb[1][:, 0:EXPERTS], R.ones16[:, :], R.hsum16[:, j, :], start=j == 0, stop=j == TT - 1)
            last.then_inc(pos_ready, 1)
            pe.wait_ge(ple_in, 32)
            for i in range(TT + 1):
                if i < TT:
                    if i >= 2:
                        pe.wait_ge(pt_done, i - 1)
                    for k in range(PK):
                        last = tr(psb[2 + i % 2][:, k * P:(k + 1) * P], p_all[:, i, k * P:(k + 1) * P], ident)
                    last.then_inc(p_ready, 1)
                if i >= 1:
                    n = i - 1
                    pe.wait_ge(pt_done, n + 1)
                    for b in range(2):
                        if n >= 1:
                            pe.wait_ge(pp_done, 2 * n + b - 1)
                        for k in range(PK):
                            last = mm(psb[4 + b][:, :], pT[:, n % 2, k, :], w_proj[:, k, b * HALF:(b + 1) * HALF], start=k == 0, stop=k == PK - 1)
                        last.then_inc(pp_ready, 1)
            pe.wait_ge(pp_done, 2 * TT)
            pe.wait_ge(slots_done, 1)
            pe.wait_ge(item_back, 16)
            turn_rows(0)
            pe.reg_load(width_reg, class_sb[0:1, 0:1])
            loop(pe, body)
    clear_sems(nc, sems)


def combine(nc, I, S, out, w_gate, w_rest, r, pp, psb, const):
    ctx, sems = ExitStack(), []
    with ctx:
        sb = lambda n, s, d=F32: ctx.enter_context(nc.sbuf_tensor("e_" + n, s, d))
        sem = lambda n: own_sem(nc, sems, "e_" + n)
        gain = sb("gain", [P, D])
        ys = sb("ys", [P, NB, TOP, D])
        part = sb("part", [P, D])
        w_gate, w_rest = ([w[k // 4][:, k % 4, :] for k in range(KC)] for w in (w_gate, w_rest))
        w_lead = sb("w_lead", [P, KC, D], F32R)
        r_lead, r_rest = sb("r_lead", [P, 2, KC, P], F32R), sb("r_rest", [P, 2, KC, P], F32R)
        gate = sb("gate", [P, 2, D])
        ssq = sb("ssq", [P, 3, TT])
        res = sb("res", [P, 2, D])
        ident = const["ident"]
        gain_in = sem("gain_in")
        wl_done, wr_dve, wr_pool, pair_done, rl_done = (sem(n) for n in ("wl_done", "wr_dve", "wr_pool", "pair_done", "rl_done"))
        N_DVE = 6
        t_in = [sem(f"t_in{s}") for s in range(NB)]
        outs = [sem(f"outs{s}") for s in range(2)]
        dve_step = sem("dve_step")
        r2_done, t_ready, t_used, g_ready, g_done, r3_done, sq_done, res_done = (
            sem(n) for n in ("r2_done", "t_ready", "t_used", "g_ready", "g_done", "r3_done", "sq_done", "res_done"))
        block = ctx.enter_context(nc.Block())

        @block.sync
        def _(sp):
            def load(i):
                rows, s = slice(i * P, (i + 1) * P), i % NB
                sp.dma_start(ys[:, s], S["ys"][i * P * TOP:(i + 1) * P * TOP, :].rearrange("(p k) d -> p k d", k=TOP)).then_inc(t_in[s], 16)
                if i < NB:
                    return
                sp.dma_start(r[:, s, :], S["r1"][rows, :]).then_inc(t_in[s], 16)
                sp.dma_start(pp[:, s, :], S["pp"][rows, :]).then_inc(t_in[s], 16)

            load(0)
            for i in range(1, NB):
                load(i)
            for i in range(TT):
                sp.wait_ge(res_done, i + 1)
                if i + NB < TT:
                    load(i + NB)
                sp.dma_start(out[0, i * P:(i + 1) * P, :], res[:, i % 2, :]).then_inc(outs[i % 2], 16)
            for s in range(2):
                sp.wait_ge(outs[s], 16 * (TT // 2))

        @block.gpsimd
        def _(pool):
            def pair(i):
                s = i % NB
                pool.wait_ge(t_in[s], 16 + 48 * (i // NB))
                nc.gpsimd.tensor_tensor(ys[:, s, 2, :], ys[:, s, 2, :], ys[:, s, 3, :], ALU.add).then_inc(pair_done, 1)

            pair(0)
            for k in range(N_DVE, KC):
                pool.wait_ge(wl_done, k + 1)
                nc.gpsimd.tensor_tensor(w_rest[k], w_gate[k], w_lead[:, k, :].bitcast(F32), ALU.subtract).then_inc(wr_pool, 1)
            for i in range(1, TT):
                pair(i)

        @block.scalar
        def _(act):
            act.dma_start(gain[:, :], I["norm_final"].unsqueeze(0).broadcast_to([P, D])).then_inc(gain_in, 16)
            for k in range(KC):
                nc.scalar.copy(w_lead[:, k, :], w_gate[k]).then_inc(wl_done, 1)

            def turned(i):
                for b in range(2):
                    act.wait_ge(t_ready, 2 * i + b + 1)
                    nc.scalar.copy(r_lead[:, i % 2, 4 * b:4 * b + 4, :], psb[b][:, :].rearrange("p (b n) -> p b n", b=4)).then_inc(rl_done, 1)

            turned(0)
            for i in range(TT):
                for b in range(2):
                    if b and i + 1 < TT:
                        turned(i + 1)
                    act.wait_ge(g_ready, 2 * i + b + 1)
                    nc.scalar.activation(gate[:, i % 2, b * HALF:(b + 1) * HALF], psb[2 + 2 * (i % 2) + b][:, :], ACT.Sigmoid).then_inc(g_done, 1)
                act.wait_ge(r3_done, i + 1)
                if i:
                    act.wait_ge(sq_done, i)
                nc.scalar.activation(gate[:, i % 2, :], r[:, i % NB, :], ACT.Square, accum_out=ssq[:, 0, i:i + 1]).then_inc(sq_done, 1)

        @block.vector
        def _(dve):
            v = nc.vector
            o = Order(dve, dve_step)

            def gather_sum(i):
                s = i % NB
                dve.wait_ge(t_in[s], 16 + 48 * (i // NB))
                o.then(v.tensor_tensor(part[:, :], ys[:, s, 0, :], ys[:, s, 1, :], ALU.add))
                o.then(v.tensor_tensor(r[:, s, :], r[:, s, :], part[:, :], ALU.add))
                dve.wait_ge(pair_done, i + 1)
                o.tell(v.tensor_tensor(r[:, s, :], r[:, s, :], ys[:, s, 2, :], ALU.add), r2_done)

            def rests(i):
                for b in range(2):
                    dve.wait_ge(rl_done, 2 * i + b + 1)
                    part4 = slice(4 * b, 4 * b + 4)
                    v.tensor_tensor(r_rest[:, i % 2, part4, :], psb[b][:, :].rearrange("p (b n) -> p b n", b=4),
                                    r_lead[:, i % 2, part4, :].bitcast(F32), ALU.subtract).then_inc(t_used, 1)

            for k in range(N_DVE):
                dve.wait_ge(wl_done, k + 1)
                v.tensor_tensor(w_rest[k], w_gate[k], w_lead[:, k, :].bitcast(F32), ALU.subtract).then_inc(wr_dve, 1)
            gather_sum(0)
            gather_sum(1)
            rests(0)
            dve.wait_ge(gain_in, 16)
            for i in range(TT):
                s = i % 2
                if i + 2 < TT:
                    gather_sum(i + 2)
                if i + 1 < TT:
                    rests(i + 1)
                for b in range(2):
                    cols = slice(b * HALF, (b + 1) * HALF)
                    dve.wait_ge(g_done, 2 * i + b + 1)
                    o.then(v.tensor_tensor(gate[:, s, cols], gate[:, s, cols], pp[:, i % NB, cols], ALU.mult))
                o.tell(v.tensor_tensor(r[:, i % NB, :], r[:, i % NB, :], gate[:, s, :], ALU.add), r3_done)
                dve.wait_ge(sq_done, i + 1)
                one = lambda n: ssq[:, n, i:i + 1]
                o.then(v.tensor_scalar(one(0), one(0), 1.0 / D, EPS, ALU.mult, ALU.add))
                rsqrt(v, o, one(1), one(0), one(2))
                if i >= 2:
                    dve.wait_ge(outs[s], 16 * (i // 2))
                o.tell(v.scalar_tensor_tensor(res[:, s, :], r[:, i % NB, :], one(1), gain[:, :], ALU.mult, ALU.mult), res_done)

        @block.tensor
        def _(pe):
            mm = nc.tensor.matmul

            def turn(i):
                s = i % NB
                pe.wait_ge(r2_done, i + 1)
                for b in range(2):
                    if i:
                        pe.wait_ge(t_used, 2 * (i - 1) + b + 1)
                    for k in range(4 * b, 4 * b + 4):
                        last = nc.tensor.transpose(psb[b][:, k % 4 * P:(k % 4 + 1) * P], r[:, s, k * P:(k + 1) * P], ident)
                    last.then_inc(t_ready, 1)

            turn(0)
            for i in range(TT):
                s = i % 2
                pe.wait_ge(rl_done, 2 * i + 2)
                for b in range(2):
                    cols = slice(b * HALF, (b + 1) * HALF)
                    if i >= 2:
                        pe.wait_ge(g_done, 2 * (i - 2) + b + 1)
                    if b and i + 1 < TT:
                        turn(i + 1)
                    for n, x in enumerate((r_lead, r_lead, r_rest)):
                        if i == 0 and b == 0 and n == 1:
                            pe.wait_ge(wr_dve, N_DVE)
                            pe.wait_ge(wr_pool, KC - N_DVE)
                        if b == 0 and n == 2:
                            pe.wait_ge(t_used, 2 * i + 2)
                        for k in range(KC):
                            w_k = w_rest[k] if n == 1 else w_lead[:, k, :]
                            last = mm(psb[2 + 2 * (i % 2) + b][:, :], x[:, s, k, :], w_k[:, cols], start=n == 0 and k == 0, stop=n == 2 and k == KC - 1)
                    last.then_inc(g_ready, 1)
    clear_sems(nc, sems)


def build(nc, I, out):
    ctx = ExitStack()
    with ctx:
        sb = lambda n, s, d=F32: ctx.enter_context(nc.sbuf_tensor(n, s, d))
        dram = lambda n, s, d=F32: nc.dram_tensor("s_" + n, s, d, kind="Internal").ap()
        S = {"u": dram("u", (SSM, STEP, CHUNKS)), "y": dram("y", (SSM, STEP, CHUNKS)), "k": dram("k", (GROUPS, GCH, P)),
             "mix_s": dram("mix_s", (KC, P, SEQ)), "gate_a": dram("gate_a", (KC, P, SEQ)),
             "r1": dram("r1", (SEQ, D)), "h2": dram("h2", (SEQ, D)), "list": dram("list", (LIST, REC)), "items": dram("items", (2, P), I32),
             "pp": dram("pp", (SEQ, D)), "ys": dram("ys", (SEQ * TOP, D))}
        psb = Banks(ctx.enter_context(nc.psum_tensor("banks", [P, 8 * HALF], F32)))
        ident = sb("ident", [P, P])
        const = {"ident": ident[:, :]}
        items_sb, class_sb = sb("items_sb", [1, 1], I32), sb("class_sb", [1, P], I32)
        bias_all = sb("bias_all", [P, EXPERTS, 3, KC])
        with nc.sbuf_tensor("w_gate_rest_lo", [P, 4, D], F32R) as w_gate_rest_lo:
            pass
        y2T = sb("y2T", [P, 4, SEQ])
        mixer = ExitStack()
        with mixer:
            with nc.sbuf_tensor("mix_lead", [P, KC, SEQ], F32R) as mix_lead:
                pass
            hT = mixer.enter_context(nc.sbuf_tensor("hT", [P, KC, SEQ], F32))
            norm_and_ssm(nc, I, S, hT, y2T, psb, const)
            with nc.sbuf_tensor("w_rest_hi", [P, KC // 2, D], F32R) as w_rest_hi:
                pass
            w_br = mixer.enter_context(nc.sbuf_tensor("w_br", [P, 4, D], F32))
            attention(nc, I, S, hT, y2T, y2T, w_br, psb, const)
            R = route_buffers(y2T[:, :, :])
            mix_and_route(nc, I, S, y2T, mix_lead, w_br, w_rest_hi, R, bias_all, psb, const)
        with nc.sbuf_tensor("w_gate_rest_hi", [P, 4, D], F32R) as w_gate_rest_hi:
            pass
        ple = sb("ple", [P, 4, D])
        w_next = y2T[:, :, :]
        r, pp = sb("r", [P, NB, D]), sb("pp", [P, NB, D])
        experts(nc, I, S, R, w_next, ple[:, :, :], r[:, :, :], pp[:, :, :], items_sb, class_sb, bias_all, psb, const)
        combine(nc, I, S, out, (w_next, ple), (w_gate_rest_lo, w_gate_rest_hi), r, pp, psb, const)


_INS = ['x', 'p', 'w_in', 'b_gates', 'lam_re', 'lam_im', 'log_dt', 'b_re', 'b_im', 'c_re', 'c_im', 'd_skip', 'w_glu', 'b_glu',
        'w_ssm_br', 'w_attn_br', 'w_o', 'norm_mix', 'norm_ffn', 'w_router', 'b_router', 'w_gate', 'b_gate', 'w_up', 'b_up',
        'w_down', 'b_down', 'w_ple_gate', 'w_ple_proj', 'norm_final']


def _tables():
    def rope(width):
        inv = (np.float32(10000.0) ** (-np.arange(width // 2, dtype=np.float32) * np.float32(2.0) / np.float32(width))).astype(np.float32)
        ang = np.arange(SEQ, dtype=np.float32)[:, None] * inv[None, :]
        return np.cos(ang).astype(np.float32), np.sin(ang).astype(np.float32)
    (c1, s1), (c2, s2) = rope(HD), rope(ID)
    return {"t_ident": np.eye(P, dtype=np.float32), "t_cos": np.concatenate([c1, c2], 1), "t_sin": np.concatenate([s1, s2], 1),
            "t_tri": np.triu(np.ones((P, P), np.float32), 1)}


def kernel(**inputs):
    import numpy as _np
    import concourse.bacc as _bacc
    from concourse import mybir as _mybir
    from concourse.bass_utils import run_bass_kernel_spmd as _run

    nc = _bacc.Bacc("TRN2", target_bir_lowering=False, num_devices=1)
    arrays = {n: _np.ascontiguousarray(inputs[n]) for n in _INS} | _tables()
    ins = {n: nc.dram_tensor(n, a.shape, _mybir.dt.from_np(a.dtype), kind="ExternalInput").ap() for n, a in arrays.items()}
    out = nc.dram_tensor("out", (1, SEQ, D), _mybir.dt.float32, kind="ExternalOutput").ap()
    build(nc, ins, out)
    r = _run(nc, [arrays], core_ids=[0])
    return r.results[0]["out"]
```
